# Optimizing a Trainium2 kernel written in Bass

```python
import math
import jax, jax.numpy as jnp
from jax import lax
import numpy as np
import jax
import jax.numpy as jnp

D_MODEL = 1024
BATCH = 1
SEQ = 256
DEPTH = 2

GROUP_WIDTH = D_MODEL // 4
HEAD_DIM = 64
N_HEADS_GROUP = GROUP_WIDTH // HEAD_DIM
D_MIX = 4 * GROUP_WIDTH

MOBA_BLOCK = 256
MOBA_TOPK = 3
MOBA_Q_CHUNK = 32
MLA_Q_RANK = 192
MLA_KV_RANK = 128
MLA_NOPE = 64
MLA_ROPE = 32
MLA_V = HEAD_DIM
MLA_QK = MLA_NOPE + MLA_ROPE
SB_Q_BLOCK = 128
SSM_HEADDIM = 64
SSM_HEADS = GROUP_WIDTH // SSM_HEADDIM
SSM_GROUPS = 2
SSM_STATE = 64
SSM_CONV = 4
SSM_CHUNK = 128
SSM_XBC = GROUP_WIDTH + 2 * SSM_GROUPS * SSM_STATE
D_FF = 2816
FFN_CONV = 3
ROPE_THETA = 10000.0
ATTN_Q_BLOCK = 128
EPS = 1e-6

MOBA_COLS = 3 * GROUP_WIDTH
MLA_COLS = MLA_Q_RANK + MLA_KV_RANK + MLA_ROPE
SB_COLS = 3 * GROUP_WIDTH
SSM_COLS = GROUP_WIDTH + SSM_XBC + SSM_HEADS
IN_COLS = MOBA_COLS + MLA_COLS + SB_COLS + SSM_COLS


def _split(x, sizes):
    outs, o = [], 0
    for s in sizes:
        outs.append(x[..., o:o + s])
        o += s
    return outs

def rms_norm(x, g):
    xf = x.astype(jnp.float32)
    y = xf * lax.rsqrt(jnp.mean(xf * xf, axis=-1, keepdims=True) + EPS)
    return (y * g.astype(jnp.float32)).astype(x.dtype)

def rope_tables(positions, dim):
    inv = 1.0 / (ROPE_THETA ** (jnp.arange(0, dim, 2, dtype=jnp.float32) / dim))
    ang = positions.astype(jnp.float32)[..., None] * inv
    return jnp.cos(ang), jnp.sin(ang)

def apply_rope(x, cos, sin):
    x1, x2 = jnp.split(x, 2, axis=-1)
    c = cos[:, :, None, :].astype(x.dtype)
    s = sin[:, :, None, :].astype(x.dtype)
    return jnp.concatenate([x1 * c - x2 * s, x1 * s + x2 * c], axis=-1)

def causal_dwconv(x, w):
    width, ch = w.shape
    return lax.conv_general_dilated(
        x, w[:, None, :], window_strides=(1,), padding=[(width - 1, 0)],
        dimension_numbers=("NWC", "WIO", "NWC"), feature_group_count=ch)

def moba_attention(q, k, v):
    bsz, seq, nh, hd = q.shape
    scale = hd ** -0.5
    nblk = -(-seq // MOBA_BLOCK)
    pad = nblk * MOBA_BLOCK - seq
    kp = jnp.pad(k, ((0, 0), (0, pad), (0, 0), (0, 0)))
    vp = jnp.pad(v, ((0, 0), (0, pad), (0, 0), (0, 0)))
    kbt = kp.reshape(bsz, nblk, MOBA_BLOCK, nh, hd).transpose(0, 3, 1, 2, 4)
    vbt = vp.reshape(bsz, nblk, MOBA_BLOCK, nh, hd).transpose(0, 3, 1, 2, 4)
    kmean = jnp.mean(kbt.astype(jnp.float32), axis=3).astype(k.dtype)
    k_eff = min(MOBA_TOPK, nblk)
    nq = seq // MOBA_Q_CHUNK
    qc = q.reshape(bsz, nq, MOBA_Q_CHUNK, nh, hd).transpose(1, 0, 2, 3, 4)
    blk_ids = jnp.arange(nblk)
    bi = jnp.arange(bsz)[:, None, None, None]
    hi = jnp.arange(nh)[None, :, None, None]

    def one_chunk(args):
        c, qi = args
        cur = (c * MOBA_Q_CHUNK) // MOBA_BLOCK
        gate = jnp.einsum("bqhd,bhnd->bhqn", qi, kmean).astype(jnp.float32)
        gate = jnp.where(blk_ids < cur, gate, -jnp.inf)
        _, idx = lax.top_k(gate, k_eff)
        valid = jnp.arange(k_eff) < cur
        k_sel = kbt[bi, hi, idx]
        v_sel = vbt[bi, hi, idx]
        s_sel = jnp.einsum("bqhd,bhqnjd->bhqnj", qi, k_sel).astype(jnp.float32) * scale
        s_sel = jnp.where(valid[None, None, None, :, None], s_sel, -jnp.inf)
        s_sel = s_sel.reshape(bsz, nh, MOBA_Q_CHUNK, k_eff * MOBA_BLOCK)
        k_own = lax.dynamic_index_in_dim(kbt, cur, axis=2, keepdims=False)
        v_own = lax.dynamic_index_in_dim(vbt, cur, axis=2, keepdims=False)
        s_own = jnp.einsum("bqhd,bhjd->bhqj", qi, k_own).astype(jnp.float32) * scale
        q_local = c * MOBA_Q_CHUNK + jnp.arange(MOBA_Q_CHUNK) - cur * MOBA_BLOCK
        causal = jnp.arange(MOBA_BLOCK)[None, :] <= q_local[:, None]
        s_own = jnp.where(causal, s_own, -jnp.inf)
        p = jax.nn.softmax(jnp.concatenate([s_sel, s_own], axis=-1), axis=-1).astype(v.dtype)
        p_sel = p[..., :k_eff * MOBA_BLOCK].reshape(bsz, nh, MOBA_Q_CHUNK, k_eff, MOBA_BLOCK)
        p_own = p[..., k_eff * MOBA_BLOCK:]
        return (jnp.einsum("bhqnj,bhqnjd->bqhd", p_sel, v_sel)
                + jnp.einsum("bhqj,bhjd->bqhd", p_own, v_own))

    out = lax.map(one_chunk, (jnp.arange(nq), qc))
    return out.transpose(1, 0, 2, 3, 4).reshape(bsz, seq, nh, hd)

def moba_mixer(p, cos, sin, qk_g):
    bsz, seq, _ = p.shape
    q, k, v = [t.reshape(bsz, seq, N_HEADS_GROUP, HEAD_DIM) for t in _split(p, (GROUP_WIDTH,) * 3)]
    q = apply_rope(rms_norm(q, qk_g[0]), cos, sin)
    k = apply_rope(rms_norm(k, qk_g[1]), cos, sin)
    return moba_attention(q, k, v)

def causal_softmax_attention(q, k, v, scale):
    bsz, seq, nh, dk = q.shape
    nb = seq // ATTN_Q_BLOCK
    qb = q.reshape(bsz, nb, ATTN_Q_BLOCK, nh, dk).transpose(1, 0, 2, 3, 4)
    kpos = jnp.arange(seq)

    def one_block(args):
        i, qi = args
        s = jnp.einsum("bqhd,bkhd->bhqk", qi, k).astype(jnp.float32) * scale
        qpos = i * ATTN_Q_BLOCK + jnp.arange(ATTN_Q_BLOCK)
        s = jnp.where(kpos[None, :] <= qpos[:, None], s, -jnp.inf)
        pr = jax.nn.softmax(s, axis=-1).astype(v.dtype)
        return jnp.einsum("bhqk,bkhd->bqhd", pr, v)

    out = lax.map(one_block, (jnp.arange(nb), qb))
    return out.transpose(1, 0, 2, 3, 4).reshape(bsz, seq, nh, v.shape[-1])

def mla_mixer(p, cos, sin, q_norm_g, kv_norm_g, w_uq, w_ukv, qk_g):
    bsz, seq, _ = p.shape
    c_q, c_kv, k_rope = _split(p, (MLA_Q_RANK, MLA_KV_RANK, MLA_ROPE))
    q = jnp.einsum("bsr,rc->bsc", rms_norm(c_q, q_norm_g), w_uq).reshape(bsz, seq, N_HEADS_GROUP, MLA_QK)
    kv = jnp.einsum("bsr,rc->bsc", rms_norm(c_kv, kv_norm_g), w_ukv).reshape(bsz, seq, N_HEADS_GROUP, MLA_NOPE + MLA_V)
    k_nope, v = kv[..., :MLA_NOPE], kv[..., MLA_NOPE:]
    k_pe = jnp.broadcast_to(k_rope[:, :, None, :], (bsz, seq, N_HEADS_GROUP, MLA_ROPE))
    k = jnp.concatenate([k_nope, k_pe], axis=-1)
    q = rms_norm(q, qk_g[0])
    k = rms_norm(k, qk_g[1])
    q = jnp.concatenate([q[..., :MLA_NOPE], apply_rope(q[..., MLA_NOPE:], cos, sin)], axis=-1)
    k = jnp.concatenate([k[..., :MLA_NOPE], apply_rope(k[..., MLA_NOPE:], cos, sin)], axis=-1)
    return causal_softmax_attention(q, k, v, MLA_QK ** -0.5)

def stick_breaking_mixer(p):
    bsz, seq, _ = p.shape
    q, k, v = [t.reshape(bsz, seq, N_HEADS_GROUP, HEAD_DIM) for t in _split(p, (GROUP_WIDTH,) * 3)]
    scale = HEAD_DIM ** -0.5
    nb = seq // SB_Q_BLOCK
    qb = q.reshape(bsz, nb, SB_Q_BLOCK, N_HEADS_GROUP, HEAD_DIM).transpose(1, 0, 2, 3, 4)
    kpos = jnp.arange(seq)

    def one_block(args):
        i, qi = args
        z = jnp.einsum("bqhd,bkhd->bhqk", qi, k).astype(jnp.float32) * scale
        qpos = i * SB_Q_BLOCK + jnp.arange(SB_Q_BLOCK)
        strict = kpos[None, :] < qpos[:, None]
        log_beta = jax.nn.log_sigmoid(z)
        log_1mb = jnp.where(strict, jax.nn.log_sigmoid(-z), 0.0)
        tail = lax.cumsum(log_1mb, axis=3, reverse=True) - log_1mb
        a = jnp.where(strict, jnp.exp(log_beta + tail), 0.0).astype(v.dtype)
        return jnp.einsum("bhqk,bkhd->bqhd", a, v)

    out = lax.map(one_block, (jnp.arange(nb), qb))
    return out.transpose(1, 0, 2, 3, 4).reshape(bsz, seq, N_HEADS_GROUP, HEAD_DIM)

def ssd_chunked(xh, dt, a_head, bm, cm):
    bsz, seq, nh, hp = xh.shape
    ns = bm.shape[-1]
    nc, cl = seq // SSM_CHUNK, SSM_CHUNK
    x = (xh * dt[..., None]).reshape(bsz, nc, cl, nh, hp)
    a = (dt * a_head).reshape(bsz, nc, cl, nh).transpose(0, 3, 1, 2)
    bc = bm.reshape(bsz, nc, cl, nh, ns)
    cc = cm.reshape(bsz, nc, cl, nh, ns)
    a_cum = jnp.cumsum(a, axis=-1)
    tri = jnp.tril(jnp.ones((cl, cl), dtype=bool))
    seg = a_cum[..., :, None] - a_cum[..., None, :]
    lmat = jnp.where(tri, jnp.exp(jnp.where(tri, seg, 0.0)), 0.0)
    y_diag = jnp.einsum("bclhn,bcshn,bhcls,bcshp->bclhp", cc, bc, lmat, x)
    decay_states = jnp.exp(a_cum[..., -1:] - a_cum)
    states = jnp.einsum("bclhn,bhcl,bclhp->bchpn", bc, decay_states, x)
    chunk_decay = jnp.exp(a_cum[..., -1])

    def step(h, inp):
        s_c, d_c = inp
        return d_c[..., None, None] * h + s_c, h

    h0 = jnp.zeros((bsz, nh, hp, ns), jnp.float32)
    _, prev = lax.scan(step, h0, (states.transpose(1, 0, 2, 3, 4), chunk_decay.transpose(2, 0, 1)))
    prev = prev.transpose(1, 0, 2, 3, 4)
    y_off = jnp.einsum("bclhn,bchpn,bhcl->bclhp", cc, prev, jnp.exp(a_cum))
    return (y_diag + y_off).reshape(bsz, seq, nh, hp)

def mamba2_mixer(p, conv_w, conv_b, dt_bias, a_log, d_skip, norm_g):
    bsz, seq, _ = p.shape
    z, xbc, dt_raw = _split(p, (GROUP_WIDTH, SSM_XBC, SSM_HEADS))
    xbc = jax.nn.silu(causal_dwconv(xbc, conv_w) + conv_b)
    xs, bm, cm = _split(xbc, (GROUP_WIDTH, SSM_GROUPS * SSM_STATE, SSM_GROUPS * SSM_STATE))
    rep = SSM_HEADS // SSM_GROUPS
    xh = xs.reshape(bsz, seq, SSM_HEADS, SSM_HEADDIM).astype(jnp.float32)
    bm = jnp.repeat(bm.reshape(bsz, seq, SSM_GROUPS, SSM_STATE), rep, axis=2).astype(jnp.float32)
    cm = jnp.repeat(cm.reshape(bsz, seq, SSM_GROUPS, SSM_STATE), rep, axis=2).astype(jnp.float32)
    dt = jax.nn.softplus(dt_raw.astype(jnp.float32) + dt_bias.astype(jnp.float32))
    a_head = -jnp.exp(a_log.astype(jnp.float32))
    y = ssd_chunked(xh, dt, a_head, bm, cm) + d_skip.astype(jnp.float32)[:, None] * xh
    y = y.reshape(bsz, seq, GROUP_WIDTH).astype(p.dtype)
    return rms_norm(y * jax.nn.silu(z), norm_g)

def first_inputs(seed: int = 0) -> dict:
    key = jax.random.key(seed)
    ks = jax.random.split(key, 24)
    f32 = jnp.float32
    L = DEPTH

    def normal(k, shape, scale):
        return jax.random.normal(k, shape, f32) * scale

    def gain(k, shape):
        return 1.0 + 0.1 * jax.random.normal(k, shape, f32)

    x = normal(ks[0], (BATCH, SEQ, D_MODEL), 1.0)
    positions = (jax.random.randint(ks[1], (BATCH, 1), 0, 4096, dtype=jnp.int32)
                 + jnp.arange(SEQ, dtype=jnp.int32)[None, :])
    dt0 = jnp.exp(jax.random.uniform(ks[13], (L, SSM_HEADS), f32, math.log(1e-3), math.log(1e-1)))
    return {
        "x": x,
        "positions": positions,
        "mix_norm_g": gain(ks[2], (L, D_MODEL)),
        "w_in": normal(ks[3], (L, D_MODEL, IN_COLS), D_MODEL ** -0.5),
        "moba_qk_g": gain(ks[4], (L, 2, HEAD_DIM)),
        "mla_q_norm_g": gain(ks[5], (L, MLA_Q_RANK)),
        "mla_kv_norm_g": gain(ks[6], (L, MLA_KV_RANK)),
        "mla_w_uq": normal(ks[7], (L, MLA_Q_RANK, N_HEADS_GROUP * MLA_QK), MLA_Q_RANK ** -0.5),
        "mla_w_ukv": normal(ks[8], (L, MLA_KV_RANK, N_HEADS_GROUP * (MLA_NOPE + MLA_V)), MLA_KV_RANK ** -0.5),
        "mla_qk_g": gain(ks[9], (L, 2, MLA_QK)),
        "ssm_conv_w": normal(ks[10], (L, SSM_CONV, SSM_XBC), SSM_CONV ** -0.5),
        "ssm_conv_b": normal(ks[11], (L, SSM_XBC), 0.02),
        "ssm_dt_bias": dt0 + jnp.log(-jnp.expm1(-dt0)),
        "ssm_a_log": jnp.log(jax.random.uniform(ks[12], (L, SSM_HEADS), f32, 1.0, 16.0)),
        "ssm_d": gain(ks[14], (L, SSM_HEADS)),
        "ssm_norm_g": gain(ks[15], (L, GROUP_WIDTH)),
        "head_out_g": gain(ks[16], (L, 3, N_HEADS_GROUP, HEAD_DIM)),
        "w_out": normal(ks[17], (L, D_MIX, D_MODEL), D_MIX ** -0.5),
        "ffn_norm_g": gain(ks[18], (L, D_MODEL)),
        "ffn_w_in": normal(ks[19], (L, D_MODEL, 2 * D_FF), D_MODEL ** -0.5),
        "ffn_conv_w": normal(ks[20], (L, FFN_CONV, 2 * D_FF), FFN_CONV ** -0.5),
        "ffn_conv_b": normal(ks[21], (L, 2 * D_FF), 0.02),
        "ffn_w_out": normal(ks[22], (L, D_FF, D_MODEL), D_FF ** -0.5),
    }

def first_block(x, positions, mix_norm_g, w_in, moba_qk_g, mla_q_norm_g, mla_kv_norm_g,
              mla_w_uq, mla_w_ukv, mla_qk_g, ssm_conv_w, ssm_conv_b, ssm_dt_bias, ssm_a_log,
              ssm_d, ssm_norm_g, head_out_g, w_out, ffn_norm_g, ffn_w_in, ffn_conv_w,
              ffn_conv_b, ffn_w_out):
    bsz, seq, _ = x.shape
    cos_a, sin_a = rope_tables(positions, HEAD_DIM)
    cos_m, sin_m = rope_tables(positions, MLA_ROPE)
    for l in range(DEPTH):
        h = rms_norm(x, mix_norm_g[l])
        proj = jnp.einsum("bsd,dc->bsc", h, w_in[l])
        moba_p, mla_p, sb_p, ssm_p = _split(proj, (MOBA_COLS, MLA_COLS, SB_COLS, SSM_COLS))
        o_moba = moba_mixer(moba_p, cos_a, sin_a, moba_qk_g[l])
        o_mla = mla_mixer(mla_p, cos_m, sin_m, mla_q_norm_g[l], mla_kv_norm_g[l],
                          mla_w_uq[l], mla_w_ukv[l], mla_qk_g[l])
        o_sb = stick_breaking_mixer(sb_p)
        o_ssm = mamba2_mixer(ssm_p, ssm_conv_w[l], ssm_conv_b[l], ssm_dt_bias[l],
                             ssm_a_log[l], ssm_d[l], ssm_norm_g[l])
        heads = rms_norm(jnp.stack([o_moba, o_mla, o_sb], axis=2), head_out_g[l])
        mixed = jnp.concatenate([heads.reshape(bsz, seq, 3 * GROUP_WIDTH), o_ssm], axis=-1)
        x = x + jnp.einsum("bsc,cd->bsd", mixed, w_out[l])
        h = rms_norm(x, ffn_norm_g[l])
        u = causal_dwconv(jnp.einsum("bsd,df->bsf", h, ffn_w_in[l]), ffn_conv_w[l]) + ffn_conv_b[l]
        gate, up = _split(u, (D_FF, D_FF))
        x = x + jnp.einsum("bsf,fd->bsd", jax.nn.silu(gate) * up, ffn_w_out[l])
    return x


DEPTH_2 = 4

CHUNK = 64
N_MIXERS = 3
N_A = (DEPTH_2 + 2) // 3
N_B = (DEPTH_2 + 1) // 3
N_C = DEPTH_2 // 3
NEG_INF = -1e30
HEADS_A = 16
HEAD_DIM_A = D_MODEL // HEADS_A
LEFT_CHUNKS = 8
BAND = (LEFT_CHUNKS + 1) * CHUNK
REL_CLIP = 128
GMLP_CHUNK = 128
D_GATE = D_MODEL
GMLP_GROUPS = 8
GMLP_GROUP_DIM = D_GATE // GMLP_GROUPS
HEADS_C = 8
HEAD_DIM_C = D_MODEL // (2 * HEADS_C)
Q_BLOCK = 128


def rms_norm_2(x, g):
    xf = x.astype(jnp.float32)
    y = xf * lax.rsqrt(jnp.mean(xf * xf, axis=-1, keepdims=True) + EPS)
    return (y * g.astype(jnp.float32)).astype(x.dtype)

def swiglu(h, w_in, w_out):
    gate, up = jnp.split(h @ w_in, 2, axis=-1)
    return (jax.nn.silu(gate) * up) @ w_out

def mixer_a(h, w_qkv, rel_bias, w_o):
    B, S, D = h.shape
    nc = S // CHUNK
    pad = LEFT_CHUNKS * CHUNK
    q, k, v = jnp.split(h @ w_qkv, 3, axis=-1)
    q = q.reshape(B, nc, CHUNK, HEADS_A, HEAD_DIM_A).transpose(1, 0, 2, 3, 4)
    k = jnp.pad(k.reshape(B, S, HEADS_A, HEAD_DIM_A), ((0, 0), (pad, 0), (0, 0), (0, 0)))
    v = jnp.pad(v.reshape(B, S, HEADS_A, HEAD_DIM_A), ((0, 0), (pad, 0), (0, 0), (0, 0)))
    rel = jnp.clip(pad + jnp.arange(CHUNK)[:, None] - jnp.arange(BAND)[None, :], -REL_CLIP, REL_CLIP) + REL_CLIP
    bias = rel_bias.astype(jnp.float32)[:, rel]
    scale = HEAD_DIM_A ** -0.5

    def one_chunk(args):
        c, qc = args
        start = c * CHUNK
        kb = lax.dynamic_slice_in_dim(k, start, BAND, axis=1)
        vb = lax.dynamic_slice_in_dim(v, start, BAND, axis=1)
        s = jnp.einsum('bqhd,bkhd->bhqk', qc, kb).astype(jnp.float32) * scale + bias
        valid = (start - pad + jnp.arange(BAND)) >= 0
        s = jnp.where(valid, s, NEG_INF)
        p = jax.nn.softmax(s, axis=-1).astype(vb.dtype)
        return jnp.einsum('bhqk,bkhd->bqhd', p, vb)

    o = lax.map(one_chunk, (jnp.arange(nc), q))
    o = o.transpose(1, 0, 2, 3, 4).reshape(B, S, D)
    return o @ w_o

def mixer_b(h, w_in, ln_g, ln_b, w_s, b_s, w_o):
    B, S, _ = h.shape
    n = S // GMLP_CHUNK
    u, v = jnp.split(jax.nn.gelu(h @ w_in, approximate=False), 2, axis=-1)
    vf = v.astype(jnp.float32)
    mu = jnp.mean(vf, axis=-1, keepdims=True)
    var = jnp.mean(jnp.square(vf - mu), axis=-1, keepdims=True)
    v = ((vf - mu) * lax.rsqrt(var + EPS) * ln_g.astype(jnp.float32) + ln_b.astype(jnp.float32)).astype(h.dtype)
    v = v.reshape(B, n, GMLP_CHUNK, GMLP_GROUPS, GMLP_GROUP_DIM)
    causal = jnp.tril(jnp.ones((GMLP_CHUNK, GMLP_CHUNK), dtype=bool))
    w = jnp.where(causal[None], w_s, 0.0)
    sv = jnp.einsum('gts,bnsgc->bntgc', w, v) + b_s.T[None, None, :, :, None]
    y = u * sv.reshape(B, S, D_GATE)
    return y @ w_o

def mixer_c(h, w_qkv, lam, subln_g, w_o, lambda_init):
    B, S, D = h.shape
    nb = S // Q_BLOCK
    q, k, v = jnp.split(h @ w_qkv, 3, axis=-1)
    q = q.reshape(B, nb, Q_BLOCK, HEADS_C, 2, HEAD_DIM_C).transpose(1, 0, 2, 3, 4, 5)
    k = k.reshape(B, S, HEADS_C, 2, HEAD_DIM_C)
    v = v.reshape(B, S, HEADS_C, 2 * HEAD_DIM_C)
    lamf = lam.astype(jnp.float32)
    lam_full = jnp.exp(jnp.sum(lamf[0] * lamf[1])) - jnp.exp(jnp.sum(lamf[2] * lamf[3])) + lambda_init
    slopes = 2.0 ** (-8.0 * (jnp.arange(HEADS_C, dtype=jnp.float32) + 1.0) / HEADS_C)
    kpos = jnp.arange(S)
    scale = HEAD_DIM_C ** -0.5

    def one_block(args):
        blk, qblk = args
        qpos = blk * Q_BLOCK + jnp.arange(Q_BLOCK)
        dist = jnp.abs(qpos[:, None] - kpos[None, :]).astype(jnp.float32)
        alibi = -slopes[:, None, None] * dist
        allowed = kpos[None, :] < (qpos[:, None] // CHUNK + 1) * CHUNK
        s = jnp.einsum('bqhmd,bkhmd->bmhqk', qblk, k).astype(jnp.float32) * scale + alibi
        s = jnp.where(allowed, s, NEG_INF)
        p = jax.nn.softmax(s, axis=-1)
        a = p[:, 0] - lam_full * p[:, 1]
        return jnp.einsum('bhqk,bkhe->bqhe', a.astype(v.dtype), v)

    o = lax.map(one_block, (jnp.arange(nb), q))
    o = o.transpose(1, 0, 2, 3, 4).reshape(B, S, HEADS_C, 2 * HEAD_DIM_C)
    o = rms_norm_2(o, subln_g) * (1.0 - lambda_init)
    return o.reshape(B, S, D) @ w_o

def second_inputs(seed: int = 0) -> dict:
    key = jax.random.key(seed)
    ks = jax.random.split(key, 20)

    def nrm(k, shape, scale):
        return jax.random.normal(k, shape, jnp.float32) * scale

    D = D_MODEL
    return {
        'x': nrm(ks[0], (BATCH, SEQ, D), 1.0),
        'norm_g': 1.0 + nrm(ks[1], (DEPTH_2, 6, D), 0.05),
        'ff1_w_in': nrm(ks[2], (DEPTH_2, D, 2 * D_FF), D ** -0.5),
        'ff1_w_out': nrm(ks[3], (DEPTH_2, D_FF, D), D_FF ** -0.5),
        'ff2_w_in': nrm(ks[4], (DEPTH_2, D, 2 * D_FF), D ** -0.5),
        'ff2_w_out': nrm(ks[5], (DEPTH_2, D_FF, D), D_FF ** -0.5),
        'a_w_qkv': nrm(ks[6], (N_A, D, 3 * D), D ** -0.5),
        'a_rel_bias': nrm(ks[7], (N_A, HEADS_A, 2 * REL_CLIP + 1), 0.5),
        'a_w_o': nrm(ks[8], (N_A, D, D), D ** -0.5),
        'b_w_in': nrm(ks[9], (N_B, D, 2 * D_GATE), D ** -0.5),
        'b_ln_g': 1.0 + nrm(ks[10], (N_B, D_GATE), 0.05),
        'b_ln_b': nrm(ks[11], (N_B, D_GATE), 0.05),
        'b_w_s': nrm(ks[12], (N_B, GMLP_GROUPS, GMLP_CHUNK, GMLP_CHUNK), GMLP_CHUNK ** -0.5),
        'b_b_s': 1.0 + nrm(ks[13], (N_B, GMLP_GROUPS, GMLP_CHUNK), 0.1),
        'b_w_o': nrm(ks[14], (N_B, D_GATE, D), D_GATE ** -0.5),
        'c_w_qkv': nrm(ks[15], (N_C, D, 3 * D), D ** -0.5),
        'c_lambda': nrm(ks[16], (N_C, 4, HEAD_DIM_C), 0.1),
        'c_subln_g': 1.0 + nrm(ks[17], (N_C, 2 * HEAD_DIM_C), 0.05),
        'c_w_o': nrm(ks[18], (N_C, D, D), D ** -0.5),
    }

def second_block(x, norm_g, ff1_w_in, ff1_w_out, ff2_w_in, ff2_w_out, a_w_qkv, a_rel_bias, a_w_o, b_w_in, b_ln_g, b_ln_b, b_w_s, b_b_s, b_w_o, c_w_qkv, c_lambda, c_subln_g, c_w_o):
    for i in range(DEPTH_2):
        g = norm_g[i]
        x = x + 0.5 * rms_norm_2(swiglu(rms_norm_2(x, g[0]), ff1_w_in[i], ff1_w_out[i]), g[1])
        h = rms_norm_2(x, g[2])
        kind, j = i % N_MIXERS, i // N_MIXERS
        if kind == 0:
            m = mixer_a(h, a_w_qkv[j], a_rel_bias[j], a_w_o[j])
        elif kind == 1:
            m = mixer_b(h, b_w_in[j], b_ln_g[j], b_ln_b[j], b_w_s[j], b_b_s[j], b_w_o[j])
        else:
            lambda_init = 0.8 - 0.6 * math.exp(-0.3 * i)
            m = mixer_c(h, c_w_qkv[j], c_lambda[j], c_subln_g[j], c_w_o[j], lambda_init)
        x = x + rms_norm_2(m, g[3])
        x = x + 0.5 * rms_norm_2(swiglu(rms_norm_2(x, g[4]), ff2_w_in[i], ff2_w_out[i]), g[5])
    return x


def setup_inputs(seed=0):
    out = dict(first_inputs(seed))
    for name, value in second_inputs(seed + 1).items():
        if name != "x":
            out[name + "_2"] = value
    return out


def reference(
    x, positions, mix_norm_g, w_in, moba_qk_g, mla_q_norm_g, mla_kv_norm_g, mla_w_uq, mla_w_ukv,
    mla_qk_g, ssm_conv_w, ssm_conv_b, ssm_dt_bias, ssm_a_log, ssm_d, ssm_norm_g, head_out_g,
    w_out, ffn_norm_g, ffn_w_in, ffn_conv_w, ffn_conv_b, ffn_w_out, norm_g_2, ff1_w_in_2,
    ff1_w_out_2, ff2_w_in_2, ff2_w_out_2, a_w_qkv_2, a_rel_bias_2, a_w_o_2, b_w_in_2, b_ln_g_2,
    b_ln_b_2, b_w_s_2, b_b_s_2, b_w_o_2, c_w_qkv_2, c_lambda_2, c_subln_g_2, c_w_o_2,
):
    x = first_block(
        x, positions, mix_norm_g, w_in, moba_qk_g, mla_q_norm_g, mla_kv_norm_g, mla_w_uq,
        mla_w_ukv, mla_qk_g, ssm_conv_w, ssm_conv_b, ssm_dt_bias, ssm_a_log, ssm_d, ssm_norm_g,
        head_out_g, w_out, ffn_norm_g, ffn_w_in, ffn_conv_w, ffn_conv_b, ffn_w_out,
    )
    return second_block(
        x, norm_g_2, ff1_w_in_2, ff1_w_out_2, ff2_w_in_2, ff2_w_out_2, a_w_qkv_2, a_rel_bias_2,
        a_w_o_2, b_w_in_2, b_ln_g_2, b_ln_b_2, b_w_s_2, b_b_s_2, b_w_o_2, c_w_qkv_2, c_lambda_2,
        c_subln_g_2, c_w_o_2,
    )


_drawn_inputs = setup_inputs


def setup_inputs(seed=0):
    import zlib

    import numpy as np

    out = dict(_drawn_inputs(seed))
    spreads = {}
    factors = {'ssm_conv_b': 3.72, 'b_ln_g_2': 5.226, 'b_ln_b_2': 4.431, 'c_lambda_2': 4.453}
    for name, (base, spread) in spreads.items():
        noise = np.random.default_rng([zlib.crc32(name.encode()), seed]).standard_normal(out[name].shape)
        drawn = base * np.exp(spread * noise) if base else spread * noise
        out[name] = jnp.asarray(drawn.astype(out[name].dtype))
    for name, factor in factors.items():
        out[name] = (out[name] * factor).astype(out[name].dtype)
    return out
```

```python
from contextlib import ExitStack

import numpy as np

import concourse.bass as bass
import concourse.mybir as mybir
from concourse.alu_op_type import AluOpType as ALU

F32 = mybir.dt.float32
F32R = mybir.dt.float32r
I32 = mybir.dt.int32
ACT = mybir.ActivationFunctionType
AX = mybir.AxisListType.X

P = 128
SEQ, D, FF = 256, 1024, 2816
TT = SEQ // P
KT = D // P
FT = FF // P
GROUP, HD = 256, 64
QR, KVR, ROPE, NOPE = 192, 128, 32, 64
QK = NOPE + ROPE
XBC = 512
IN = 3 * GROUP + QR + KVR + ROPE + 3 * GROUP + GROUP + XBC + 4
C_MOBA = 0
C_CQ = 3 * GROUP
C_CKV = C_CQ + QR
C_KR = C_CKV + KVR
C_SB = C_KR + ROPE
C_Z = C_SB + 3 * GROUP
C_XBC = C_Z + GROUP
C_DT = C_XBC + XBC
EPS = 1e-6
BIG = -1e30
CHUNK = 64
REL = 128
THETA = 10000.0

RING = 3
AHEAD = RING - 1
CW = 2048

PLAN = ([(s, l) for l in range(2) for s in ("mix1", "ffn1")]
        + [s for i in range(4) for s in (("swiglu", i, 0), ("mix2", i), ("swiglu", i, 1))])

CONST = {}


def constants():
    parts, at = [], 0

    def add(name, a):
        nonlocal at
        a = np.asarray(a, np.float32)
        parts.append(a)
        CONST[name] = (at, at + a.shape[1])
        at += a.shape[1]

    r, c = np.arange(P)[:, None], np.arange(P)[None, :]
    add("ident", r == c)
    add("upto", r <= c)
    add("after", r > c)
    add("ones", np.ones((P, P)))
    causal = np.where(c <= r, 0, BIG)
    add("causal", np.concatenate([causal, np.zeros((P, P)), causal], 1))
    add("upto_add", np.where(r <= c, 0, BIG))
    strict = (r < c).astype(np.float32)
    add("strict", np.concatenate([strict, np.ones((P, P)), strict], 1))
    add("dist", -np.abs(np.arange(P)[:, None] + np.arange(SEQ)[None, :] - 127))
    add("minus_half", np.full((P, 64), -0.5))
    for name, dim in (("inv64", HD), ("inv32", ROPE)):
        inv = np.float32(1) / (np.float32(THETA) ** (np.arange(0, dim, 2, dtype=np.float32) / np.float32(dim)))
        add(name, np.broadcast_to(inv.astype(np.float32), (P, dim // 2)))
    return np.concatenate(parts, 1)


CONSTS = constants()

ROWS = {}
_rows = [("mix_norm_g", 2 * KT), ("ffn_norm_g", 2 * KT), ("norm_g", 24 * KT), ("ssm_conv_w", 2 * 4 * 4),
         ("ssm_conv_b", 2 * 4), ("ffn_conv_w", 2 * 3 * 2 * FT), ("ffn_conv_b", 2 * 2 * FT), ("b_b_s", 8)]
_at = 0
for _n, _k in _rows:
    ROWS[_n] = _at
    _at += _k
N_ROWS = _at
ROW_TILES = -(-N_ROWS // P)

WIDE = {}
_wide = [("moba_g", 128), ("q_norm", QR), ("kv_norm", KVR), ("qk_g", 2 * QK), ("dt_bias", 4), ("a_log", 4), ("ssm_d", 4),
         ("ssm_norm", GROUP), ("head_g", 3 * GROUP)]
_at = 0
for _n, _k in _wide:
    WIDE[_n] = (_at, _at + _k)
    _at += _k
N_WIDE = _at

class Semaphores:

    def __init__(self, new):
        self.params_in = new("params_in")
        self.rows_in = new("rows_in")
        self.rows_turned = new("rows_turned")
        self.rows_kept = new("rows_kept")
        self.pos_in = new("pos_in")
        self.wide_in = new("wide_in")
        self.ext_out = new("ext_out")
        self.ext_in = new("ext_in")
        self.w_in_small = new("w_in_small")
        self.x_in = new("x_in")
        self.angles = new("angles")
        self.sines = new("sines")
        self.out_stored = new("out_stored")
        self.split_hi = new("split_hi")
        self.split_lo = new("split_lo")
        self.chunk_done = new("chunk_done")
        self.bank_free = new("bank_free")
        self.squares = new("squares")
        self.ln_centred = new("ln_centred")
        self.ln_squares = new("ln_squares")
        self.conv_half = new("conv_half")
        self.meansq = new("meansq")
        self.rstd = new("rstd")
        self.normed = new("normed")
        self.turned = new("turned")
        self.hi_turned = new("hi_turned")
        self.features = new("features")
        self.silu = new("silu")
        self.seeded = new("seeded")
        self.gated = new("gated")
        self.hid_hi = new("hid_hi")
        self.hid_ready = new("hid_ready")
        self.m_squares = new("m_squares")
        self.m_meansq = new("m_meansq")
        self.m_rstd = new("m_rstd")
        self.residual = new("residual")
        self.scores = new("scores")
        self.masked = new("masked")
        self.maxed = new("maxed")
        self.exps = new("exps")
        self.mixed = new("mixed")
        self.probs_turned = new("probs_turned")
        self.turned_copied = new("turned_copied")
        self.pair_out = new("pair_out")
        self.out_kept = new("out_kept")
        self.bias_ready = new("bias_ready")
        self.attended = new("attended")
        self.lam_in = new("lam_in")
        self.lam_dots = new("lam_dots")
        self.lam_exps = new("lam_exps")
        self.sub_sq = new("sub_sq")
        self.sub_ms = new("sub_ms")
        self.sub_rstd = new("sub_rstd")
        self.b_rows_in = new("b_rows_in")
        self.bw_in = new("bw_in")
        self.bw_turned = new("bw_turned")
        self.bw_kept = new("bw_kept")
        self.ln_ms = new("ln_ms")
        self.ln_rstd = new("ln_rstd")
        self.v_normed = new("v_normed")
        self.gated_sums = new("gated_sums")
        self.b_y = new("b_y")
        self.moba_sq = new("moba_sq")
        self.c_sq = new("c_sq")
        self.c_ms = new("c_ms")
        self.c_rstd = new("c_rstd")
        self.moba_ready = new("moba_ready")
        self.c_ready = new("c_ready")
        self.sb_turned = new("sb_turned")
        self.sb_kept = new("sb_kept")
        self.xbc_turned = new("xbc_turned")
        self.xbc_kept = new("xbc_kept")
        self.moba_turned = new("moba_turned")
        self.moba_kept = new("moba_kept")
        self.c_turned = new("c_turned")
        self.c_kept = new("c_kept")
        self.up_done = new("up_done")
        self.up_used = new("up_used")
        self.mla_sq = new("mla_sq")
        self.mla_ms = new("mla_ms")
        self.mla_rstd = new("mla_rstd")
        self.mla_ready = new("mla_ready")
        self.mla_turned = new("mla_turned")
        self.mla_kept = new("mla_kept")
        self.z_done = new("z_done")
        self.z_ln = new("z_ln")
        self.z_l = new("z_l")
        self.tail_done = new("tail_done")
        self.z_arg = new("z_arg")
        self.z_exp = new("z_exp")
        self.sb_a = new("sb_a")
        self.sb_o = new("sb_o")
        self.sb_o_kept = new("sb_o_kept")
        self.convd = new("convd")
        self.xc_done = new("xc_done")
        self.xh_turned = new("xh_turned")
        self.xh_kept = new("xh_kept")
        self.dt_raw = new("dt_raw")
        self.dt_abs = new("dt_abs")
        self.dt_e = new("dt_e")
        self.dt_u = new("dt_u")
        self.dt_ln = new("dt_ln")
        self.a_exp = new("a_exp")
        self.a_ready = new("a_ready")
        self.cum_done = new("cum_done")
        self.expo = new("expo")
        self.expo_done = new("expo_done")
        self.gram_done = new("gram_done")
        self.w_ready = new("w_ready")
        self.ssm_y = new("ssm_y")
        self.z_silu = new("z_silu")
        self.ssm_sq = new("ssm_sq")
        self.ssm_ms = new("ssm_ms")
        self.ssm_rstd = new("ssm_rstd")
        self.y_sum = new("y_sum")
        self.head_sq = new("head_sq")
        self.head_ms = new("head_ms")
        self.head_rstd = new("head_rstd")
        self.heads_ready = new("heads_ready")
        self.ext_stored = new("ext_stored")
        self.bias_in = new("bias_in")
        self.recips = new("recips")
        self.weighed = new("weighed")
        self.act_step = new("act_step")
        self.dve_step = new("dve_step")
        self.pool_step = new("pool_step")
        self.landed = [new(f"landed{i}") for i in range(RING)]
        self.gain_in = [new(f"gain_in{i}") for i in range(2)]


class Memory:
    pass


def view(t, **k):
    return t.rearrange("p (a b) -> p a b", **k)


class Program:
    def __init__(self, nc, eng, m, s, d):
        self.nc, self.e, self.m, self.s, self.d = nc, eng, m, s, d
        self.c0 = 0
        self.b0 = 0
        self.f0 = 0
        self.v0 = 0
        self.p0 = 0
        self.rounds = {}
        self.steps_made = 0

    def bank(self, b):
        return (self.b0 + b) % RING

    def round(self, name):
        self.rounds[name] = self.rounds.get(name, 0) + 1
        return self.rounds[name]

    def at(self, sem, value, i=0, per_turn=0):
        if isinstance(i, int):
            value += i * per_turn
            if value > 0:
                self.e.wait_ge(sem, value)
        else:
            assert value > 0
            self.e.wait_ge(sem, i * per_turn + value)

    def steps(self, n, body, unroll=RING, peel=1, last=0):
        if self.c0 == 0:
            peel = n
        peel = min(peel, n)
        for b in range(peel):
            body(b, 0)
        turns = (n - peel - last) // unroll
        b = peel
        if turns >= 2:
            with self.e.Fori(0, turns) as i:
                for u in range(unroll):
                    body(peel + u, i)
            b += turns * unroll
        for b in range(b, n):
            body(b, 0)

    def gated(self, kind, b, i):
        if kind == "ffn1":
            self.at(self.s.gated, self.v0 + b + 1, i, RING)
        else:
            self.at(self.s.bank_free, self.b0 + b + 1, i, RING)

    def after_hidden(self, kind):
        self.advance(FT)
        self.f0 += FT
        if kind == "ffn1":
            self.v0 += FT

    def start(self): pass
    def finish(self): pass
    def norm(self, gain): pass
    def turn(self, src, gain, ready): pass
    def post_norm(self, source, weight, plain=False): pass
    def load_gain(self, layer, which): pass

    def advance(self, n, banks=True):
        self.c0 += n
        if banks:
            self.b0 += n


def walk(e):
    e.start()
    for stage in PLAN:
        if stage[0] == "mix1":
            l = stage[1]
            e.norm(ROWS["mix_norm_g"] + l * KT)
            e.product_tokens("in1", l, -(-IN // 256), lambda m, j: None)
            e.mixers(l)
            e.turn("mixed", None, "heads_ready")
            e.product_tokens("out1", l, 4, None)
            e.post_norm("sb", None, plain=True)
        elif stage[0] == "ffn1":
            l = stage[1]
            e.norm(ROWS["ffn_norm_g"] + l * KT)
            e.hidden("ffn1", l)
            e.down("ffn1", l)
            e.post_norm("psum", None, plain=True)
        elif stage[0] == "swiglu":
            _, i, w = stage
            e.load_gain(i, 4 * w + 1)
            e.norm(ROWS["norm_g"] + (i * 6 + 4 * w) * KT)
            e.hidden("swiglu", (i, w))
            e.down("swiglu", (i, w))
            e.post_norm("psum", 0.5)
        else:
            i = stage[1]
            e.load_gain(i, 3)
            e.norm(ROWS["norm_g"] + (i * 6 + 2) * KT)
            if i % 3 == 1:
                e.product_tokens("b_in", i // 3, 8, None)
                e.gmlp(i // 3)
                e.turn("xn", None, "b_y")
                e.product_tokens("b_o", i // 3, 4, None)
            else:
                kind = "a" if i % 3 == 0 else "c"
                e.bias_tables(kind, i // 3)
                e.product_features(kind + "_qkv", i // 3, 8)
                e.product_tokens(kind + "_v", i // 3, 4, None)
                e.attention(kind, 8)
                if kind == "c":
                    e.sub_norm(i)
                e.turn("xn", None, "attended" if kind == "c" else "out_kept")
                e.product_tokens(kind + "_o", i // 3, 4, None)
            e.post_norm("sb", 1.0)
    e.finish()


class Sync(Program):

    def start(self):
        e, m, s, d = self.e, self.m, self.s, self.d
        e.dma_start(m.x[:, :, :], d.x.rearrange("o (t p) c -> p (o t) c", p=P)).then_inc(s.x_in, 16)

    def chunk(self, b, i, dst_src):
        c = self.c0 + b
        self.at(self.s.split_lo, c + 1 - RING, i, RING)
        dst, src = dst_src(self.m.raw[:, c % RING, :], b if isinstance(i, int) else i * RING + b)
        self.e.dma_start(dst, src).then_inc(self.s.landed[c % RING], 16)

    def columns(self, w, col, n):
        wv = w.rearrange("(k p) c -> p k c", p=P)

        def pick(raw, j):
            return (raw[:, :].rearrange("p (k c) -> p k c", k=KT), wv[:, :, bass.ds(j * 256 + col, 256)])
        return lambda b, i: self.chunk(b, i, pick)

    def product_tokens(self, what, l, n, _):
        d = self.d
        if what == "in1":
            full = self.columns(d.w_in[l], 0, n)
            for b in range(n - 1):
                full(b, 0)
            rest = IN - 256 * (n - 1)
            wv = d.w_in[l].rearrange("(k p) c -> p k c", p=P)
            self.chunk(n - 1, 0, lambda raw, j: (raw[:, 0:KT * 256].rearrange("p (k c) -> p k c", k=KT)[:, :, 0:rest],
                                                 wv[:, :, 256 * (n - 1):IN]))
        else:
            w, col = {"out1": (d.w_out, 0), "b_in": (d.b_w_in, 0), "b_o": (d.b_w_o, 0), "a_v": (d.a_w_qkv, 2 * D),
                      "a_o": (d.a_w_o, 0), "c_v": (d.c_w_qkv, 2 * D), "c_o": (d.c_w_o, 0)}[what]
            self.steps(n, self.columns(w[l], col, n), peel=0)
        self.advance(n)

    def product_features(self, what, l, n):
        w = self.d.a_w_qkv if what == "a_qkv" else self.d.c_w_qkv
        self.steps(n, self.columns(w[l], 0, n), peel=0)
        self.advance(n)

    def weights_of(self, kind, l):
        d = self.d
        if kind == "ffn1":
            return d.ffn_w_in[l], d.ffn_w_out[l]
        i, w = l
        return (d.ff2_w_in[i], d.ff2_w_out[i]) if w else (d.ff1_w_in[i], d.ff1_w_out[i])

    def hidden(self, kind, l):
        w = self.weights_of(kind, l)[0].rearrange("(k p) (h n c) -> p h k n c", p=P, h=2, c=P)

        def pick(raw, j):
            return (raw[:, :].rearrange("p (h k n c) -> p h k n c", h=2, k=KT, n=1), w[:, :, :, bass.ds(j, 1), :])
        self.steps(FT, lambda b, i: self.chunk(b, i, pick), peel=0)
        self.advance(FT)

    def down(self, kind, l):
        w = self.weights_of(kind, l)[1].rearrange("(n k p) c -> p n k c", p=P, k=2)

        def pick(raw, j):
            return (raw[:, :].rearrange("p (n k c) -> p n k c", n=1, k=2), w[:, bass.ds(j, 1), :, :])
        self.steps(FT // 2, lambda b, i: self.chunk(b, i, pick), peel=0)
        self.advance(FT // 2, banks=False)

    def mixers(self, l): pass
    def gmlp(self, l): pass
    def bias_tables(self, kind, l): pass
    def attention(self, kind, n): pass
    def sub_norm(self, i): pass

    def finish(self):
        e, m, s = self.e, self.m, self.s
        e.wait_ge(s.residual, TT * len(PLAN))
        e.dma_start(self.d.out.rearrange("o (t p) c -> p (o t) c", p=P), m.x[:, :, :]).then_inc(s.out_stored, 16)
        e.wait_ge(s.out_stored, 16)


class Tensor(Program):
    def start(self):
        e, m, s = self.e, self.m, self.s
        e.wait_ge(s.params_in, 16)
        e.wait_ge(s.rows_in, 16 * m.row_loads)
        for r in range(ROW_TILES):
            ins = e.transpose(m.ps[:, r, 0:P], m.rows[:, r, :], m.ident)
        ins.then_inc(s.rows_turned, 1)

    def turn(self, src, gain, ready):
        e, m, s = self.e, self.m, self.s
        a = {"xn": m.xn, "mixed": m.xn}[src]
        if ready == "out_kept":
            e.wait_ge(s.out_kept, self.p0)
        else:
            done = {"normed": s.normed, "heads_ready": s.heads_ready, "b_y": s.b_y, "attended": s.attended}[ready]
            e.wait_ge(done, self.round(ready))
        for b in range(4):
            for k in range(2):
                for t in range(TT):
                    ins = e.transpose(m.ps[:, b, k * 256 + t * P:k * 256 + (t + 1) * P],
                                      a[:, t, (2 * b + k) * P:(2 * b + k + 1) * P], m.ident)
            ins.then_inc(s.turned, 1)

    def norm(self, gain):
        self.turn("xn", gain, "normed")

    def begin_product(self):
        self.e.wait_ge(self.s.features, 4 * self.round("features"))

    def chunk_start(self, b, i):
        self.at(self.s.split_lo, self.c0 + b + 1, i, RING)
        self.at(self.s.bank_free, self.b0 + b + 1 - RING, i, RING)

    def product_tokens(self, what, l, n, _):
        e, m, s = self.e, self.m, self.s
        self.begin_product()

        def body(b, i):
            self.chunk_start(b, i)
            c, w = self.c0 + b, 256
            if what == "in1" and b == n - 1:
                w = IN - 256 * (n - 1)
            whi = m.whi[:, c % RING, :].rearrange("p (k c) -> p k c", k=KT)
            wlo = m.wlo[:, c % RING, :].rearrange("p (k c) -> p k c", k=KT)
            for t in range(TT):
                out = m.ps[:, self.bank(b), t * 256:t * 256 + w]
                for k in range(KT):
                    hi, lo = m.h_hi[:, k, t * P:(t + 1) * P], m.h_lo[:, k, t * P:(t + 1) * P]
                    e.matmul(out, hi, whi[:, k, 0:w], start=(k == 0), stop=False)
                    e.matmul(out, hi, wlo[:, k, 0:w], start=False, stop=False)
                    ins = e.matmul(out, lo, whi[:, k, 0:w], start=False, stop=(k == KT - 1))
            ins.then_inc(s.chunk_done, 1)
        self.steps(n, body, peel=n if what == "in1" else 0)
        self.advance(n)

    def features_chunk(self, b, i, w_of):
        e, m, s = self.e, self.m, self.s
        self.chunk_start(b, i)
        c = self.c0 + b
        for f in range(2):
            out = m.ps[:, self.bank(b), f * 256:(f + 1) * 256]
            for k in range(KT):
                hi, lo = w_of(m.whi[:, c % RING, :], f, k), w_of(m.wlo[:, c % RING, :], f, k)
                e.matmul(out, hi, m.h_hi[:, k, :], start=(k == 0), stop=False)
                e.matmul(out, hi, m.h_lo[:, k, :], start=False, stop=False)
                ins = e.matmul(out, lo, m.h_hi[:, k, :], start=False, stop=(k == KT - 1))
        ins.then_inc(s.chunk_done, 1)

    def product_features(self, what, l, n):
        self.begin_product()

        def w_of(w, f, k):
            return w[:, k * 256 + f * P:k * 256 + (f + 1) * P]
        self.steps(n, lambda b, i: self.features_chunk(b, i, w_of), peel=0)
        self.advance(n)
        self.rounds["features"] -= 1

    def hidden(self, kind, l):
        self.begin_product()

        def w_of(w, f, k):
            return w[:, (f * KT + k) * P:(f * KT + k + 1) * P]
        self.steps(FT, lambda b, i: self.features_chunk(b, i, w_of), peel=1)
        self.after_hidden(kind)

    def down(self, kind, l):
        e, m, s = self.e, self.m, self.s
        for b in range(FT // 2):
            c = self.c0 + b
            self.at(s.split_lo, c + 1)
            self.at(s.hid_ready, self.f0 - FT + 2 * b + 2)
            whi = m.whi[:, c % RING, :].rearrange("p (k c) -> p k c", k=2)
            wlo = m.wlo[:, c % RING, :].rearrange("p (k c) -> p k c", k=2)
            for t in range(TT):
                for k in range(2):
                    f = 2 * b + k
                    hi, lo = m.hid_hi[:, f, t * P:(t + 1) * P], m.hid_lo[:, f, t * P:(t + 1) * P]
                    for x, w in ((hi, whi), (hi, wlo), (lo, whi)):
                        for h in range(2):
                            ins = e.matmul(m.ps[:, 4 + 2 * t + h, :], x, w[:, k, h * 512:(h + 1) * 512],
                                           start=(f == 0 and x is hi and w is whi),
                                           stop=(f == FT - 1 and x is lo))
            ins.then_inc(s.chunk_done, 1)
        self.advance(FT // 2, banks=False)

    def attention(self, kind, n):
        e, m, s = self.e, self.m, self.s
        q, k, v = m.heads[kind]
        if kind in ("a", "c"):
            e.wait_ge(s.bank_free, self.b0)

        def ix(b, i):
            return b if isinstance(i, int) else i * 2 + b

        def scores(b, i):
            self.at(s.masked, self.p0 + b, i, 2)
            for h in range(2):
                e.matmul(m.ps[:, h, 0:P], q(ix(b, i), h, 0), k(ix(b, i), h, 1), start=True, stop=True)
                ins = e.matmul(m.ps[:, h, P:P + SEQ], q(ix(b, i), h, 1), k(ix(b, i), h, 2), start=True, stop=True)
            ins.then_inc(s.scores, 1)

        def rest(b, i):
            par, parts = b % 2, 1 if kind == "c" else 2
            if kind == "c":
                self.at(s.mixed, self.m0 + b + 1)
            else:
                self.at(s.exps, self.p0 + b + 1)
            self.at(s.turned_copied, self.p0 + b, i, 2)
            for h in range(parts):
                for j in range(3):
                    ins = e.transpose(m.ps[:, 2 + h, j * P:(j + 1) * P], m.prob[:, par, h, j * P:(j + 1) * P], m.ident)
            ins.then_inc(s.probs_turned, 1)
            self.at(s.turned_copied, self.p0 + b + 1, i, 2)
            self.at(s.out_kept, self.p0 + b, i, 2)
            w = P // parts
            for h in range(parts):
                pt = m.prob_t[:, par, h, :]
                e.matmul(m.ps[:, 4, h * w:(h + 1) * w], pt[:, 0:P], v(ix(b, i), h, 0), start=True, stop=True)
                e.matmul(m.ps[:, 4, P + h * w:P + (h + 1) * w], pt[:, P:2 * P], v(ix(b, i), h, 0), start=True, stop=False)
                ins = e.matmul(m.ps[:, 4, P + h * w:P + (h + 1) * w], pt[:, 2 * P:3 * P], v(ix(b, i), h, 1),
                               start=False, stop=True)
            ins.then_inc(s.pair_out, 1)

        def body(b, i):
            if not (isinstance(i, int) and b == n - 1):
                scores(b + 1, i)
            rest(b, i)
        scores(0, 0)
        self.steps(n, body, unroll=2, peel=n)
        self.p0 += n
        self.m0 += n if kind == "c" else 0

    m0 = 0

    def bias_tables(self, kind, l): pass
    def sub_norm(self, i): pass

    def gmlp(self, l):
        e, m, s = self.e, self.m, self.s
        r = self.round("gmlp")
        e.wait_ge(s.bw_in, 16 * r)
        e.wait_ge(s.bank_free, self.b0)
        for g in range(8):
            ins = e.transpose(m.ps[:, 4 + g // 4, (g % 4) * P:(g % 4 + 1) * P], m.b_w[:, g, :], m.ident)
        ins.then_inc(s.bw_turned, 1)
        e.wait_ge(s.bw_kept, 2 * r)
        e.wait_ge(s.v_normed, r)
        for t in range(TT):
            for g in range(8):
                ins = e.matmul(m.ps[:, 2 * t + g // 4, (g % 4) * P:(g % 4 + 1) * P], m.b_wt[:, g, :],
                               m.b_v[:, t, g * P:(g + 1) * P], start=True, stop=True)
        ins.then_inc(s.gated_sums, 1)

    def mixers(self, l):
        e, m, s = self.e, self.m, self.s
        r = self.round("mixers")
        ps, proj, ident = m.ps, m.proj, m.ident
        e.wait_ge(s.bank_free, self.b0)
        for x in range(2):
            for j in range(2):
                for t in range(TT):
                    col = C_SB + x * GROUP + j * P
                    ins = e.transpose(ps[:, 2 + x, j * 256 + t * P:j * 256 + (t + 1) * P], proj[:, t, col:col + P], ident)
        ins.then_inc(s.sb_turned, 1)
        for j in range(4):
            for t in range(TT):
                col = C_XBC + j * P
                ins = e.transpose(ps[:, 4 + j // 2, (j % 2) * 256 + t * P:(j % 2) * 256 + (t + 1) * P],
                                  proj[:, t, col:col + P], ident)
        ins.then_inc(s.xbc_turned, 1)
        e.wait_ge(s.c_ready, r)
        for t in range(TT):
            e.transpose(ps[:, 6, t * P:(t + 1) * P], m.cn[:, t, 0:P], ident)
            e.transpose(ps[0:64, 6, 256 + t * P:256 + (t + 1) * P], m.cn[:, t, P:QR], ident)
            ins = e.transpose(ps[:, 7, t * P:(t + 1) * P], m.cn[:, t, QR:QR + KVR], ident)
        ins.then_inc(s.c_turned, 1)
        e.wait_ge(s.w_in_small, 48 * r)
        e.wait_ge(s.c_kept, r)
        e.wait_ge(s.xbc_kept, r)
        for t in range(TT):
            tok = slice(t * P, (t + 1) * P)
            e.matmul(ps[:, t, 0:4 * QK], m.c_t[:, 0, tok], m.w_uq[:, 0, :], start=True, stop=False)
            e.matmul(ps[:, t, 0:4 * QK], m.c_t[0:64, 1, tok], m.w_uq[0:64, 1, :], start=False, stop=True)
            ins = e.matmul(ps[:, 4 + t, :], m.c_t[:, 2, tok], m.w_ukv[:, :], start=True, stop=True)
        ins.then_inc(s.up_done, 1)
        e.wait_ge(s.moba_ready, r)
        e.wait_ge(s.c_kept, r)
        for x in range(2):
            for j in range(2):
                for t in range(TT):
                    col = x * GROUP + j * P
                    ins = e.transpose(ps[:, 6 + x, j * 256 + t * P:j * 256 + (t + 1) * P], m.qk_rot[:, t, col:col + P], ident)
        ins.then_inc(s.moba_turned, 1)
        e.wait_ge(s.up_used, r)
        e.wait_ge(s.sb_kept, r)
        for h in range(4):
            part = slice(64 * (h % 2), 64 * (h % 2) + 64)
            e.matmul(ps[:, h, 0:SEQ], m.sb_t[part, 2 + h // 2, 0:P], m.sb_t[part, h // 2, :], start=True, stop=True)
            ins = e.matmul(ps[:, h, SEQ:SEQ + P], m.sb_t[part, 2 + h // 2, P:SEQ], m.sb_t[part, h // 2, P:SEQ],
                           start=True, stop=True)
        ins.then_inc(s.z_done, 1)
        e.wait_ge(s.moba_kept, r)
        e.wait_ge(s.z_l, r)
        for h in range(4):
            low = m.z0[:, h, :]
            e.matmul(ps[:, 4 + h, 0:SEQ], m.after, low[:, 0:SEQ], start=True, stop=False)
            e.matmul(ps[:, 4 + h, P:SEQ], m.ones, low[:, SEQ:SEQ + P], start=False, stop=True)
            ins = e.matmul(ps[:, 4 + h, SEQ:SEQ + P], m.after, low[:, SEQ:SEQ + P], start=False, stop=True,
                           skip_group_check=True)
        ins.then_inc(s.tail_done, 1)
        e.wait_ge(s.sb_a, r)
        for h in range(4):
            vcol = C_SB + 2 * GROUP + h * HD
            self.two_blocks(ps[:, 0, :], h, m.z1[:, h, :], lambda t: proj[:, t, vcol:vcol + HD])
        self.last.then_inc(s.sb_o, 1)
        e.wait_ge(s.sb_o_kept, r)
        self.attention("moba", 2)
        e.wait_ge(s.mla_ready, r)
        for h in range(8):
            for t in range(TT):
                ins = e.transpose(ps[0:QK, h // 2, (h % 2) * 256 + t * P:(h % 2) * 256 + (t + 1) * P],
                                  m.qk96[:, t, h, :], ident)
        ins.then_inc(s.mla_turned, 1)
        e.wait_ge(s.mla_kept, r)
        self.attention("mla", 2)
        e.wait_ge(s.xc_done, r)
        e.wait_ge(s.z_arg, r)
        for j in range(2):
            for t in range(TT):
                ins = e.transpose(ps[:, 7, t * 256 + j * P:t * 256 + (j + 1) * P], m.xc[:, j, t * P:(t + 1) * P], ident)
        ins.then_inc(s.xh_turned, 1)
        e.wait_ge(s.a_ready, r)
        e.wait_ge(s.out_kept, self.p0)
        for t in range(TT):
            for h in range(4):
                e.matmul(ps[:, 5 + t, h * P:(h + 1) * P], m.a[:, t, h:h + 1].to_broadcast([P, P]), m.upto, start=True, stop=True)
            ins = e.matmul(ps[:, 4, 256 + t * 4:256 + t * 4 + 4], m.upto, m.a[:, t, :], start=True, stop=True)
        ins.then_inc(s.cum_done, 1)
        for g in range(2):
            part = slice(64 * g, 64 * g + 64)
            e.matmul(ps[:, g, 0:SEQ], m.xc[part, 2, 0:P], m.xc[part, 3, :], start=True, stop=True)
            ins = e.matmul(ps[:, g, SEQ:SEQ + P], m.xc[part, 2, P:SEQ], m.xc[part, 3, P:SEQ], start=True, stop=True)
        ins.then_inc(s.gram_done, 1)
        e.wait_ge(s.w_ready, r)
        for h in range(4):
            self.two_blocks(ps[:, 2, :], h, m.z0[:, h, :], lambda t: m.xdt[:, t, h * HD:(h + 1) * HD])
        self.last.then_inc(s.ssm_y, 1)

    def two_blocks(self, bank, h, w, rhs):
        e, c = self.e, slice(h * HD, (h + 1) * HD)
        e.matmul(bank[:, h * HD:(h + 1) * HD], w[:, 0:P], rhs(0), start=True, stop=True)
        e.matmul(bank[:, 256 + h * HD:256 + (h + 1) * HD], w[:, P:2 * P], rhs(0), start=True, stop=False)
        self.last = e.matmul(bank[:, 256 + h * HD:256 + (h + 1) * HD], w[:, 2 * P:3 * P], rhs(1), start=False, stop=True)


class Scalar(Program):
    def act(self, *a, **k):
        return self.nc.scalar.activation(*a, **k)

    def link(self, ins):
        self.steps_made += 1
        ins.then_inc(self.s.act_step, 1)
        self.e.wait_ge(self.s.act_step, self.steps_made)

    def split(self, b, i):
        m, s = self.m, self.s
        c = self.c0 + b + AHEAD
        if isinstance(i, int) and c >= self.total:
            return
        slot = c % RING
        self.at(s.landed[slot], 16 * (c // RING + 1), i, 16)
        self.at(s.chunk_done, c + 1 - RING, i, RING)
        self.act(m.whi[:, slot, :], m.raw[:, slot, :], ACT.Copy).then_inc(s.split_hi, 1)

    def start(self):
        e, m, s = self.e, self.m, self.s
        for b in range(-AHEAD, 0):
            self.split(b, 0)
        e.wait_ge(s.rows_turned, 1)
        self.act(m.cols[:, :].rearrange("p (r c) -> p r c", c=P), m.ps[:, 0:ROW_TILES, 0:P], ACT.Copy).then_inc(s.rows_kept, 1)
        e.wait_ge(s.rows_kept, 1)
        e.wait_ge(s.angles, 1)
        self.act(m.trig[:, :], m.ang[:, :], ACT.Sin).then_inc(s.sines, 1)

    def norm(self, gain):
        e, m, s = self.e, self.m, self.s
        r = self.round("norm")
        if r == 1:
            e.wait_ge(s.x_in, 16)
        for t in range(TT):
            if r > 1:
                e.wait_ge(s.residual, 2 * (r - 1) - 1 + t)
            self.act(m.junk(t), m.x[:, t, :], ACT.Square, accum_out=m.ss[:, t:t + 1]).then_inc(s.squares, 1)
        self.turn("xn", gain, "normed")

    def turn(self, src, gain, ready):
        e, m, s = self.e, self.m, self.s
        r = self.round("turn")
        if r == 1:
            e.wait_ge(s.rows_kept, 1)
        for b in range(4):
            e.wait_ge(s.turned, 4 * (r - 1) + b + 1)
            if gain is None:
                ins = self.act(m.h_hi[:, 2 * b:2 * b + 2, :], m.ps[:, b, :].rearrange("p (k c) -> p k c", k=2), ACT.Copy)
            else:
                for k in range(2):
                    f = 2 * b + k
                    ins = self.act(m.h_hi[:, f, :], m.ps[:, b, k * 256:(k + 1) * 256], ACT.Copy,
                                   scale=m.cols[:, gain + f:gain + f + 1])
            ins.then_inc(s.hi_turned, 1)

    def chunk_ready(self, b, i):
        self.at(self.s.chunk_done, self.c0 + b + 1, i, RING)

    def product_tokens(self, what, l, n, _):
        e, m, s = self.e, self.m, self.s
        dest = {"in1": lambda: m.proj, "out1": lambda: m.xn, "b_o": lambda: m.xn, "a_o": lambda: m.xn, "c_o": lambda: m.xn,
                "a_v": lambda: m.v, "c_v": lambda: m.v, "b_in": lambda: m.b_uv}[what]()
        func = ACT.Gelu if what == "b_in" else ACT.Copy

        def body(b, i):
            self.split(b, i)
            self.chunk_ready(b, i)
            w = 256
            if what == "in1" and b == n - 1:
                w = IN - 256 * (n - 1)
            j = b if isinstance(i, int) else i * RING + b
            self.act(dest[:, :, bass.ds(j * 256, w)], m.ps[:, self.bank(b), :].rearrange("p (t c) -> p t c", t=2)[:, :, 0:w],
                     func).then_inc(s.bank_free, 1)
        self.steps(n, body, peel=n if what == "in1" else 0)
        self.advance(n)

    def product_features(self, what, l, n):
        e, m, s = self.e, self.m, self.s
        for half in range(2):

            def body(b, i):
                self.split(b, i)
                self.chunk_ready(b, i)
                j = (b if isinstance(i, int) else i * RING + b) * 2
                self.act(m.qk[:, bass.ds(j + n * half, 2), :],
                         m.ps[:, self.bank(b), :].rearrange("p (k c) -> p k c", k=2), ACT.Copy,
                         scale=HD ** -0.5 if half == 0 else 1.0).then_inc(s.bank_free, 1)
            self.steps(n // 2, body, peel=0)
            self.advance(n // 2)

    def hidden(self, kind, l):
        e, m, s = self.e, self.m, self.s

        def hi(b, i):
            self.gated(kind, b, i)
            j = b if isinstance(i, int) else i * RING + b
            self.act(m.hid_hi[:, bass.ds(j, 1), :], m.hid[:, b % RING:b % RING + 1, :], ACT.Copy).then_inc(s.hid_hi, 1)

        def body(b, i):
            self.chunk_ready(b, i)
            if b >= RING:
                self.gated(kind, b - RING, i)
            j = b if isinstance(i, int) else i * RING + b
            gate = m.ps[:, self.bank(b), 0:256]
            if kind == "ffn1":
                for g in range(2):
                    w = ROWS["ffn_conv_w"] + (l * 3 + 2) * 2 * FT + g * FT
                    bias = ROWS["ffn_conv_b"] + l * 2 * FT + g * FT
                    ins = self.act(m.u[:, b % RING, g, :], m.ps[:, self.bank(b), g * 256:(g + 1) * 256], ACT.Identity,
                                   bias=m.cols[:, bass.ds(j + bias, 1)], scale=m.cols[:, bass.ds(j + w, 1)])
                ins.then_inc(s.seeded, 1)
                if b > 0:
                    hi(b - 1, i)
                self.split(b, i)
                self.at(s.bank_free, self.b0 + b + 1, i, RING)
                self.act(m.silu[:, b % RING, :], m.u[:, b % RING, 0, :], ACT.Silu).then_inc(s.silu, 1)
            else:
                self.act(m.silu[:, b % RING, :], gate, ACT.Silu).then_inc(s.silu, 1)
                if b > 0:
                    hi(b - 1, i)
                self.split(b, i)
        self.steps(FT, body, peel=4)
        hi(FT - 1, 0)
        self.after_hidden(kind)

    def down(self, kind, l):
        for b in range(FT // 2):
            self.split(b, 0)
        self.advance(FT // 2, banks=False)

    def post_norm(self, source, weight, plain=False):
        e, m, s = self.e, self.m, self.s
        if plain:
            return
        r = self.round("post")
        if source == "psum":
            e.wait_ge(s.chunk_done, self.c0)
        else:
            e.wait_ge(s.bank_free, self.b0)
        for t in range(TT):
            src = m.acc(t) if source == "psum" else m.xn[:, t, :]
            self.act(m.junk(t), src, ACT.Square, accum_out=m.ss2[:, t:t + 1]).then_inc(s.m_squares, 1)

    def bias_tables(self, kind, l):
        e, m, s = self.e, self.m, self.s
        if kind == "c":
            e.wait_ge(s.lam_dots, self.round("lam"))
            self.act(m.lam_d[:, 0:2], m.lam_d[:, 0:2], ACT.Exp).then_inc(s.lam_exps, 1)

    def attention(self, kind, n):
        e, m, s = self.e, self.m, self.s

        def body(b, i):
            par = b % 2
            self.at(s.maxed, self.p0 + b + 1, i, 2)
            for h in range(2):
                for t in range(2):
                    cols = slice(0, P) if t == 0 else slice(P, P + SEQ)
                    ins = self.act(m.prob[:, par, h, cols], m.prob[:, par, h, cols], ACT.Exp,
                                   bias=m.negmax[:, par, h, t:t + 1], accum_out=m.sums[:, par, h, t:t + 1])
            ins.then_inc(s.exps, 1)
            parts = 1 if kind == "c" else 2
            self.at(s.probs_turned, self.p0 + b + 1, i, 2)
            self.at(s.pair_out, self.p0 + b - 1, i, 2)
            self.act(m.prob_t[:, par, 0:parts, :], m.ps[:, 2:2 + parts, 0:3 * P], ACT.Copy).then_inc(s.turned_copied, 1)
        self.steps(n, body, unroll=2, peel=2, last=1)
        self.p0 += n

    def sub_norm(self, i):
        e, m, s = self.e, self.m, self.s
        r = self.round("sub")
        e.wait_ge(s.out_kept, self.p0)
        for t in range(TT):
            self.act(m.sub_squares(t), m.xn[:, t, :], ACT.Square).then_inc(s.sub_sq, 1)

    def gmlp(self, l):
        e, m, s = self.e, self.m, self.s
        r = self.round("gmlp")
        e.wait_ge(s.ln_centred, r)
        for t in range(TT):
            ins = self.act(m.junk(t), m.b_v[:, t, :], ACT.Square, accum_out=m.ss2[:, t:t + 1])
        ins.then_inc(s.ln_squares, 1)

    def mixers(self, l):
        e, m, s = self.e, self.m, self.s
        r = self.round("mixers")
        ps, proj = m.ps, m.proj
        cst = m
        e.wait_ge(s.bank_free, self.b0)
        self.act(m.z0f[:, 0:1024].rearrange("p (t c) -> p t c", t=2), proj[:, :, 0:512], ACT.Square).then_inc(s.moba_sq, 1)
        self.act(m.z1f[:, 0:640].rearrange("p (t c) -> p t c", t=2), proj[:, :, C_CQ:C_KR], ACT.Square).then_inc(s.c_sq, 1)
        e.wait_ge(s.sb_turned, r)
        self.act(m.sb_t[:, 0:2, :], view(ps[:, 2, :], a=2), ACT.Copy, scale=HD ** -0.5)
        self.act(m.sb_t[:, 2:4, :], view(ps[:, 3, :], a=2), ACT.Copy).then_inc(s.sb_kept, 1)
        e.wait_ge(s.xbc_turned, r)
        for j in range(2):
            ins = self.act(m.xt[:, 2 * j:2 * j + 2, 3:3 + SEQ], view(ps[:, 4 + j, :], a=2), ACT.Copy)
        ins.then_inc(s.xbc_kept, 1)
        e.wait_ge(s.c_turned, r)
        self.act(m.c_t[:, 0, :], ps[:, 6, 0:256], ACT.Copy)
        self.act(m.c_t[0:64, 1, :], ps[0:64, 6, 256:512], ACT.Copy)
        self.act(m.c_t[:, 2, :], ps[:, 7, 0:256], ACT.Copy).then_inc(s.c_kept, 1)
        e.wait_ge(s.up_done, r)
        for t in range(TT):
            self.act(m.qk96[:, t, 0:4, :], ps[:, t, 0:4 * QK].rearrange("p (h c) -> p h c", h=4), ACT.Copy)
            kv = ps[:, 4 + t, :].rearrange("p (h c) -> p h c", h=4)
            self.act(m.qk96[:, t, 4:8, 0:NOPE], kv[:, :, 0:NOPE], ACT.Copy)
            for h in range(4):
                self.act(m.qk96[:, t, 4 + h, NOPE:QK], proj[:, t, C_KR:C_KR + ROPE], ACT.Copy)
            ins = self.act(m.v_mla[:, t, :].rearrange("p (h c) -> p h c", h=4), kv[:, :, NOPE:], ACT.Copy)
        ins.then_inc(s.up_used, 1)
        e.wait_ge(s.up_used, r)
        e.wait_ge(s.moba_ready, r)
        self.act(m.z1f[:, :].rearrange("p (t c) -> p t c", t=2), m.qk96[:, :, :, :].rearrange("p t h c -> p t (h c)"), ACT.Square).then_inc(s.mla_sq, 1)
        e.wait_ge(s.moba_turned, r)
        self.act(m.moba_t[:, 0:2, :], view(ps[:, 6, :], a=2), ACT.Copy, scale=HD ** -0.5)
        self.act(m.moba_t[:, 2:4, :], view(ps[:, 7, :], a=2), ACT.Copy).then_inc(s.moba_kept, 1)
        z = ps[:, 0:4, 0:3 * P]
        e.wait_ge(s.z_done, r)
        self.link(self.act(m.z0[:, :, :], z, ACT.Abs))
        self.link(self.act(m.z0[:, :, :], m.z0[:, :, :], ACT.Exp, scale=-1.0))
        self.act(m.z0[:, :, :], m.z0[:, :, :], ACT.Ln, bias=1.0).then_inc(s.z_ln, 1)
        e.wait_ge(s.z_arg, r)
        self.act(m.z1[:, :, :], m.z1[:, :, :], ACT.Exp).then_inc(s.z_exp, 1)
        e.wait_ge(s.dt_raw, r)
        self.act(m.dt[:, 1, :], m.dt[:, 0, :], ACT.Abs).then_inc(s.dt_abs, 1)
        e.wait_ge(s.dt_abs, r)
        self.act(m.dt[:, 2, :], m.dt[:, 1, :], ACT.Exp, scale=-1.0).then_inc(s.dt_e, 1)
        self.act(m.ahead[:, :], m.wide_("a_log"), ACT.Exp).then_inc(s.a_exp, 1)
        e.wait_ge(s.dt_u, r)
        self.act(m.dt[:, 4, :], m.dt[:, 3, :], ACT.Ln).then_inc(s.dt_ln, 1)
        self.attention("moba", 2)
        e.wait_ge(s.mla_turned, r)
        for b in range(4):
            ins = self.act(m.mla_t[0:QK, 2 * b:2 * b + 2, :], view(ps[0:QK, b, :], a=2), ACT.Copy,
                           scale=QK ** -0.5 if b < 2 else 1.0)
        ins.then_inc(s.mla_kept, 1)
        self.attention("mla", 2)
        e.wait_ge(s.convd, r)
        self.act(m.xc[:, :, :], m.conv[:, :, :], ACT.Silu).then_inc(s.xc_done, 1)
        self.act(m.zs[:, :, :], proj[:, :, C_Z:C_Z + GROUP], ACT.Silu).then_inc(s.z_silu, 1)
        e.wait_ge(s.xh_turned, r)
        self.act(m.xh[:, :, :], view(ps[:, 7, :], a=2), ACT.Copy).then_inc(s.xh_kept, 1)
        e.wait_ge(s.expo, r)
        self.act(m.z0[:, :, :], m.z0[:, :, :], ACT.Exp).then_inc(s.expo_done, 1)
        e.wait_ge(s.y_sum, r)
        for t in range(TT):
            ins = self.act(m.ps[:, 3, t * 256:(t + 1) * 256], m.y[:, t, :], ACT.Square, accum_out=m.ss2[:, t:t + 1])
        ins.then_inc(s.ssm_sq, 1)
        e.wait_ge(s.sb_o_kept, r)
        e.wait_ge(s.out_kept, self.p0)
        self.act(m.z1f[:, :].rearrange("p (t c) -> p t c", t=2), m.xn[:, :, 0:768], ACT.Square).then_inc(s.head_sq, 1)


class Vector(Program):
    def link(self, ins):
        self.steps_made += 1
        ins.then_inc(self.s.dve_step, 1)
        self.e.wait_ge(self.s.dve_step, self.steps_made)

    def split(self, b, i):
        m, s = self.m, self.s
        c = self.c0 + b + AHEAD
        if isinstance(i, int) and c >= self.total:
            return
        slot = c % RING
        self.at(s.split_hi, c + 1, i, RING)
        self.e.tensor_tensor(m.wlo[:, slot, :], m.raw[:, slot, :], m.whi[:, slot, :].bitcast(F32),
                             ALU.subtract).then_inc(s.split_lo, 1)

    def start(self):
        e, m, s = self.e, self.m, self.s
        self.link(e.memset(m.xt[:, :, 0:3], 0.0))
        for b in range(-AHEAD, 0):
            self.split(b, 0)
        e.wait_ge(s.params_in, 16)
        e.wait_ge(s.pos_in, 16)
        self.link(e.tensor_copy(m.pos[:, :], m.pos_i[:, :]))
        half = {"64": HD // 2, "32": ROPE // 2}
        at = 0
        for name, n in half.items():
            for quarter in range(2):
                for t in range(TT):
                    ins = e.tensor_scalar(m.ang0[:, at + t * n:at + (t + 1) * n], m.cst("inv" + name), m.pos[:, t:t + 1], None, ALU.mult)
                at += TT * n
        self.link(ins)
        n_all, n_cos = at, None
        magic = 1.5 * 2.0 ** 23
        at = 0
        for name, n in half.items():
            for quarter in range(2):
                w = slice(at, at + TT * n)
                ins = e.tensor_scalar(m.turns[:, w], m.ang0[:, w], 1 / (2 * np.pi), 0.25 * quarter, ALU.mult, ALU.add)
                at += TT * n
        self.link(ins)
        self.link(e.tensor_scalar(m.turns[:, :], m.turns[:, :], magic, -magic, ALU.add, ALU.add))
        rest = 2 * np.pi
        for bits in (8, 8, 8, 24):
            scale = 2.0 ** (bits - 1 - np.floor(np.log2(rest)))
            part = float(np.float32(np.floor(rest * scale) / scale))
            rest -= part
            self.link(e.scalar_tensor_tensor(m.ang0[:, :], m.turns[:, :], -part, m.ang0[:, :], ALU.mult, ALU.add))
        at = 0
        for name, n in half.items():
            w = slice(at + TT * n, at + 2 * TT * n)
            ins = e.tensor_scalar(m.ang0[:, w], m.ang0[:, w], float(np.pi / 2), None, ALU.add)
            at += 2 * TT * n
        self.link(ins)
        lim = 3.1415925
        e.tensor_scalar(m.ang[:, :], m.ang0[:, :], lim, -lim, ALU.min, ALU.max).then_inc(s.angles, 1)
        e.wait_ge(s.ext_in, 16)
        e.tensor_scalar(m.ext[:, 2 * REL + 1:], m.cst("ones")[0:32, 0:127], m.ext[:, 2 * REL:2 * REL + 1], None,
                        ALU.mult).then_inc(s.ext_out, 1)

    def norm(self, gain):
        e, m, s = self.e, self.m, self.s
        r = self.round("norm")
        e.wait_ge(s.squares, 2 * r)
        e.tensor_scalar(m.ms[:, :], m.ss[:, :], 1.0 / D, EPS, ALU.mult, ALU.add).then_inc(s.meansq, 1)
        e.wait_ge(s.rstd, r)
        for t in range(TT):
            ins = e.tensor_scalar(m.xn[:, t, :], m.x[:, t, :], m.rs[:, t:t + 1], None, ALU.mult)
        ins.then_inc(s.normed, 1)
        self.turn("xn", gain, "normed")

    def turn(self, src, gain, ready):
        e, m, s = self.e, self.m, self.s
        r = self.round("turn")
        if r == 1:
            e.wait_ge(s.rows_kept, 1)
        for b in range(4):
            e.wait_ge(s.hi_turned, 4 * (r - 1) + b + 1)
            if gain is None:
                ins = e.tensor_tensor(m.h_lo[:, 2 * b:2 * b + 2, :], view(m.ps[:, b, :], a=2),
                                      m.h_hi[:, 2 * b:2 * b + 2, :].bitcast(F32), ALU.subtract)
            else:
                for k in range(2):
                    f = 2 * b + k
                    ins = e.scalar_tensor_tensor(m.h_lo[:, f, :], m.ps[:, b, k * 256:(k + 1) * 256], m.cols[:, gain + f:gain + f + 1],
                                                 m.h_hi[:, f, :].bitcast(F32), ALU.mult, ALU.subtract)
            ins.then_inc(s.features, 1)

    def product_tokens(self, what, l, n, _):
        self.steps(n, self.split, peel=n if what == "in1" else 0)
        self.advance(n)

    def product_features(self, what, l, n):
        self.steps(n, self.split, peel=0)
        self.advance(n)

    def hidden(self, kind, l):
        e, m, s = self.e, self.m, self.s

        def lo(b, i):
            self.at(s.hid_hi, self.f0 + b + 1, i, RING)
            j = b if isinstance(i, int) else i * RING + b
            e.tensor_tensor(m.hid_lo[:, bass.ds(j, 1), :], m.hid[:, b % RING:b % RING + 1, :],
                            m.hid_hi[:, bass.ds(j, 1), :].bitcast(F32), ALU.subtract).then_inc(s.hid_ready, 1)

        def body(b, i):
            j = b if isinstance(i, int) else i * RING + b
            bank = m.ps[:, self.bank(b), :]
            if kind == "ffn1":
                self.at(s.seeded, self.v0 + b + 1, i, RING)
                for tap in range(2):
                    back = 2 - tap
                    for g in range(2):
                        w = ROWS["ffn_conv_w"] + (l * 3 + tap) * 2 * FT + g * FT
                        u = m.u[:, b % RING, g, back:]
                        ins = e.scalar_tensor_tensor(u, bank[:, g * 256:(g + 1) * 256 - back],
                                                     m.cols[:, bass.ds(j + w, 1)], u, ALU.mult, ALU.add)
                    if tap == 0:
                        ins.then_inc(s.conv_half, 1)
                        self.at(s.conv_half, self.v0 + b + 1, i, RING)
                ins.then_inc(s.bank_free, 1)
                up, done = m.u[:, b % RING, 1, :], s.gated
            else:
                up, done = bank[:, 256:512], s.bank_free
            if b > 0:
                lo(b - 1, i)
            self.split(b, i)
            self.at(s.silu, self.f0 + b + 1, i, RING)
            if kind == "ffn1":
                self.at(s.bank_free, self.b0 + b + 1, i, RING)
            e.tensor_tensor(m.hid[:, b % RING, :], m.silu[:, b % RING, :], up, ALU.mult).then_inc(done, 1)
        self.steps(FT, body, peel=4)
        lo(FT - 1, 0)
        self.after_hidden(kind)

    def down(self, kind, l):
        for b in range(FT // 2):
            self.split(b, 0)
        self.advance(FT // 2, banks=False)
    def post_norm(self, source, weight, plain=False):
        e, m, s = self.e, self.m, self.s

        def src(t):
            return m.acc(t) if source == "psum" else m.xn[:, t, :]
        if plain:
            if source == "psum":
                e.wait_ge(s.chunk_done, self.c0)
            else:
                e.wait_ge(s.bank_free, self.b0)
            for t in range(TT):
                e.tensor_tensor(m.x[:, t, :], src(t), m.x[:, t, :], ALU.add).then_inc(s.residual, 1)
            return
        r = self.round("post")
        e.wait_ge(s.m_squares, 2 * r)
        e.tensor_scalar(m.ms2[:, 0:2], m.ss2[:, :], 1.0 / D, EPS, ALU.mult, ALU.add).then_inc(s.m_meansq, 1)
        e.wait_ge(s.gain_in[r % 2], 16 * ((r + 1) // 2))
        e.wait_ge(s.m_rstd, r)
        for t in range(TT):
            self.link(e.scalar_tensor_tensor(m.xn[:, t, :], src(t), m.rs2[:, t:t + 1], m.gain[:, r % 2, :], ALU.mult, ALU.mult))
            e.scalar_tensor_tensor(m.x[:, t, :], m.xn[:, t, :], weight, m.x[:, t, :], ALU.mult, ALU.add).then_inc(s.residual, 1)

    def bias_tables(self, kind, l):
        e, m, s = self.e, self.m, self.s
        if kind == "c":
            r = self.round("lam")
            e.wait_ge(s.lam_in, 32 * r)
            for j in range(2):
                ins = e.tensor_tensor_reduce(m.lam_x[:, j * 64:(j + 1) * 64], m.lam[:, 2 * j, :], m.lam[:, 2 * j + 1, :], 1.0, 0.0,
                                             ALU.mult, ALU.add, m.lam_d[:, j:j + 1])
            ins.then_inc(s.lam_dots, 1)
            e.wait_ge(s.lam_exps, r)
            self.link(e.tensor_tensor(m.lam_d[:, 2:3], m.lam_d[:, 0:1], m.lam_d[:, 1:2], ALU.subtract))
            self.link(e.tensor_scalar(m.lam_d[:, 3:4], m.lam_d[:, 2:3], -1.0, -LAMBDA_INIT, ALU.mult, ALU.add))

    def attention(self, kind, n):
        e, m, s = self.e, self.m, self.s
        if kind in ("a", "c"):
            e.wait_ge(s.bias_ready, self.round("bias"))

        def mask(b, i):
            par = b % 2
            self.at(s.scores, self.p0 + b + 1, i, 2)
            self.at(s.probs_turned, self.p0 + b - 1, i, 2)
            for h in range(2):
                sc, out = m.ps[:, h, 0:3 * P], m.prob[:, par, h, :]
                if kind in ("a", "c"):
                    j = b if isinstance(i, int) else i * 2 + b
                    tab = (m.bias[:, bass.ds(j * 2 + h, 1), :] if kind == "a" else m.bias[:, bass.ds(j, 1), :])
                    tab = tab.rearrange("p o c -> p (o c)")
                    e.tensor_tensor(out[:, 0:P], sc[:, 0:P], tab[:, 0:P][:, ::-1], ALU.add)
                    ins = e.tensor_tensor(out[:, P:], sc[:, P:], tab[:, ::-1], ALU.add)
                else:
                    ins = e.tensor_tensor(out, sc, m.cst("causal"), ALU.add)
            ins.then_inc(s.masked, 1)
            self.at(s.masked, self.p0 + b + 1, i, 2)
            e.tensor_reduce(m.negmax[:, par, :, 0:1], m.prob[:, par, :, 0:P], AX, ALU.max, negate=True)
            e.tensor_reduce(m.negmax[:, par, :, 1:2], m.prob[:, par, :, P:], AX, ALU.max, negate=True).then_inc(s.maxed, 1)

        def weigh(b, i):
            par = b % 2
            self.at(s.exps, self.p0 + b + 1, i, 2)
            e.reciprocal(m.rsum[:, par, 0:4], m.sums[:, par, :, :].rearrange("p h t -> p (h t)")).then_inc(s.recips, 1)
            if kind != "c":
                return
            self.at(s.recips, self.p0 + b + 1, i, 2)
            e.tensor_scalar(m.rsum[:, par, 4:6], m.rsum[:, par, 2:4], m.lam_d[:, 3:4], None, ALU.mult)
            for t, cols in ((0, slice(0, P)), (1, slice(P, 3 * P))):
                ins = e.tensor_scalar(m.prob[:, par, 0, cols], m.prob[:, par, 0, cols], m.rsum[:, par, t:t + 1], None, ALU.mult)
            ins.then_inc(s.weighed, 1)
            self.at(s.weighed, self.m0 + b + 1, i, 2)
            for t, cols in ((0, slice(0, P)), (1, slice(P, 3 * P))):
                ins = e.scalar_tensor_tensor(m.prob[:, par, 0, cols], m.prob[:, par, 1, cols], m.rsum[:, par, 4 + t:5 + t],
                                             m.prob[:, par, 0, cols], ALU.mult, ALU.add)
            ins.then_inc(s.mixed, 1)

        def keep(b, i):
            par = b % 2
            self.at(s.pair_out, self.p0 + b + 1, i, 2)
            self.at(s.recips, self.p0 + b + 1, i, 2)
            j = b if isinstance(i, int) else i * 2 + b
            base = 256 if kind == "mla" else 0
            out = m.xn[:, :, bass.ds(j * P + base, P)]
            acc = m.ps[:, 4, 0:256].rearrange("p (t c) -> p t c", t=2)
            if kind == "c":
                e.tensor_copy(out, acc).then_inc(s.out_kept, 1)
            else:
                r = m.rsum[:, par, 0:4].rearrange("p (h t) -> p t h", t=2).unsqueeze(3).to_broadcast([P, 2, 2, HD])
                e.tensor_tensor(out.rearrange("p t (h c) -> p t h c", h=2), acc.rearrange("p t (h c) -> p t h c", h=2), r,
                                ALU.mult).then_inc(s.out_kept, 1)

        def body(b, i):
            if kind == "c":
                weigh(b, i)
            if not (isinstance(i, int) and b == n - 1):
                mask(b + 1, i)
            if kind != "c":
                weigh(b, i)
            keep(b, i)
        mask(0, 0)
        self.steps(n, body, unroll=2, peel=n)
        self.p0 += n
        self.m0 += n if kind == "c" else 0

    m0 = 0

    def rms(self, src, heads, width, st, ready, rstd, r):
        e, m = self.e, self.m
        self.link(e.tensor_reduce(m.st[:, st:st + heads], src, AX, ALU.add))
        e.tensor_scalar(m.st[:, st:st + heads], m.st[:, st:st + heads], 1.0 / width, EPS, ALU.mult, ALU.add).then_inc(ready, 1)
        e.wait_ge(rstd, r)

    def sub_norm(self, i):
        e, m, s = self.e, self.m, self.s
        r = self.round("sub")
        e.wait_ge(s.sub_sq, 2 * r)
        self.rms(m.sub_squares(None), 16, P, 0, s.sub_ms, s.sub_rstd, r)
        v = m.xn[:, :, :].rearrange("p t (h c) -> p (t h) c", h=8)
        self.link(e.tensor_tensor(v, v, m.st[:, 0:16].unsqueeze(2).to_broadcast([P, 16, P]), ALU.mult))
        e.scalar_tensor_tensor(v, v, 1.0 - LAMBDA_INIT, m.sub_g[:, :].unsqueeze(1).to_broadcast([P, 16, P]), ALU.mult,
                               ALU.mult).then_inc(s.attended, 1)

    def gmlp(self, l):
        e, m, s = self.e, self.m, self.s
        r = self.round("gmlp")
        e.wait_ge(s.bank_free, self.b0)
        self.link(e.tensor_reduce(m.st[:, 0:2], m.b_uv[:, :, D:2 * D], AX, ALU.add))
        self.link(e.tensor_scalar(m.st[:, 0:2], m.st[:, 0:2], 1.0 / D, None, ALU.mult))
        for t in range(TT):
            ins = e.tensor_scalar(m.b_v[:, t, :], m.b_v[:, t, :], m.st[:, t:t + 1], None, ALU.subtract)
        ins.then_inc(s.ln_centred, 1)
        e.wait_ge(s.bw_turned, r)
        for g in range(2):
            e.tensor_tensor(m.b_wt[:, 4 * g:4 * g + 4, :], view(m.ps[:, 4 + g, :], a=4),
                            m.cst("upto").unsqueeze(1).to_broadcast([P, 4, P]), ALU.mult).then_inc(s.bw_kept, 1)
        e.wait_ge(s.ln_squares, r)
        e.tensor_scalar(m.st[:, 2:4], m.ss2[:, :], 1.0 / D, EPS, ALU.mult, ALU.add).then_inc(s.ln_ms, 1)
        e.wait_ge(s.ln_rstd, r)
        e.wait_ge(s.b_rows_in, 32 * r)
        for t in range(TT):
            self.link(e.scalar_tensor_tensor(m.b_v[:, t, :], m.b_v[:, t, :], m.st[:, 4 + t:5 + t], m.b_rows[:, 0, :], ALU.mult, ALU.mult))
            ins = e.tensor_tensor(m.b_v[:, t, :], m.b_v[:, t, :], m.b_rows[:, 1, :], ALU.add)
        ins.then_inc(s.v_normed, 1)
        e.wait_ge(s.gated_sums, r)
        for t in range(TT):
            for g in range(8):
                c = slice(g * P, (g + 1) * P)
                ins = e.scalar_tensor_tensor(m.xn[:, t, c], m.ps[:, 2 * t + g // 4, (g % 4) * P:(g % 4 + 1) * P],
                                             m.cols[:, ROWS["b_b_s"] + g:ROWS["b_b_s"] + g + 1], m.b_uv[:, t, c], ALU.add, ALU.mult)
        ins.then_inc(s.b_y, 1)

    def rope(self, src, dst, tmp, kind, n):
        e, m = self.e, self.m
        at = {"64": 0, "32": 4 * HD // 2}[kind]
        sin, cos = (m.trig[:, at + q * 2 * n:at + (q + 1) * 2 * n].rearrange("p (t c) -> p t c", t=2).unsqueeze(2)
                    .to_broadcast([P, 2, 8, n]) for q in range(2))
        x1, x2 = src[:, :, :, 0:n], src[:, :, :, n:2 * n]
        w = 2 * 8 * n
        t = [tmp[:, q * w:(q + 1) * w].rearrange("p (t h c) -> p t h c", t=2, h=8) for q in range(4)]
        e.tensor_tensor(t[0], x1, cos, ALU.mult)
        e.tensor_tensor(t[1], x2, sin, ALU.mult)
        e.tensor_tensor(t[2], x1, sin, ALU.mult)
        self.link(e.tensor_tensor(t[3], x2, cos, ALU.mult))
        e.tensor_tensor(dst[:, :, :, 0:n], t[0], t[1], ALU.subtract)
        return e.tensor_tensor(dst[:, :, :, n:2 * n], t[2], t[3], ALU.add)

    def mixers(self, l):
        e, m, s = self.e, self.m, self.s
        r = self.round("mixers")
        ps, proj = m.ps, m.proj

        def four(ap, h=8):
            return ap.rearrange("p t (h c) -> p t h c", h=h)

        def gains(ap, h, w):
            return ap.unsqueeze(1).unsqueeze(1).to_broadcast([P, 2, h, w])
        e.wait_ge(s.bank_free, self.b0)
        e.wait_ge(s.wide_in, 16 * len(WIDE) * r)
        e.wait_ge(s.moba_sq, r)
        e.tensor_reduce(m.st[:, 0:16], m.z0f[:, 0:1024].rearrange("p (h c) -> p h c", c=HD), AX, ALU.add)
        e.wait_ge(s.c_sq, r)
        csq = m.z1f[:, 0:640].rearrange("p (t c) -> p t c", t=2)
        e.tensor_reduce(m.st[:, 16:18], csq[:, :, 0:QR], AX, ALU.add)
        self.link(e.tensor_reduce(m.st[:, 18:20], csq[:, :, QR:QR + KVR], AX, ALU.add))
        e.tensor_scalar(m.st[:, 0:16], m.st[:, 0:16], 1.0 / HD, EPS, ALU.mult, ALU.add)
        e.tensor_scalar(m.st[:, 16:18], m.st[:, 16:18], 1.0 / QR, EPS, ALU.mult, ALU.add)
        e.tensor_scalar(m.st[:, 18:20], m.st[:, 18:20], 1.0 / KVR, EPS, ALU.mult, ALU.add).then_inc(s.c_ms, 1)
        e.wait_ge(s.c_rstd, r)
        for at, col, w, g in ((16, 0, QR, "q_norm"), (18, QR, KVR, "kv_norm")):
            for t in range(TT):
                ins = e.scalar_tensor_tensor(m.cn[:, t, col:col + w], proj[:, t, C_CQ + col:C_CQ + col + w],
                                             m.st[:, at + t:at + t + 1], m.wide_(g), ALU.mult, ALU.mult)
        ins.then_inc(s.c_ready, 1)
        q0 = m.z0f[:, 0:1024].rearrange("p (t h c) -> p t h c", t=2, h=8)
        self.link(e.tensor_tensor(q0, four(proj[:, :, 0:512]),
                                  m.st[:, 0:16].rearrange("p (t h) -> p t h", t=2).unsqueeze(3).to_broadcast([P, 2, 8, HD]), ALU.mult))
        for x in range(2):
            ins = e.tensor_tensor(q0[:, :, 4 * x:4 * x + 4, :], q0[:, :, 4 * x:4 * x + 4, :],
                                  gains(m.wide_("moba_g")[:, x * HD:(x + 1) * HD], 4, HD), ALU.mult)
        self.link(ins)
        self.rope(q0, four(m.qk_rot[:, :, :]), m.rope_tmp, "64", HD // 2).then_inc(s.moba_ready, 1)
        e.tensor_tensor(m.dt[:, 0, :].rearrange("p (t h) -> p t h", t=2), proj[:, :, C_DT:C_DT + 4],
                        m.wide_("dt_bias").unsqueeze(1).to_broadcast([P, 2, 4]), ALU.add).then_inc(s.dt_raw, 1)
        e.wait_ge(s.xbc_kept, r)
        for tap in (3, 2, 1, 0):
            for j in range(4):
                w = ROWS["ssm_conv_w"] + (l * 4 + tap) * 4 + j
                wc = m.cols[:, w:w + 1]
                if tap == 3:
                    bias = ROWS["ssm_conv_b"] + l * 4 + j
                    ins = e.tensor_scalar(m.conv[:, j, :], m.xt[:, j, 3:3 + SEQ], wc, m.cols[:, bias:bias + 1], ALU.mult, ALU.add)
                else:
                    ins = e.scalar_tensor_tensor(m.conv[:, j, :], m.xt[:, j, tap:tap + SEQ], wc, m.conv[:, j, :], ALU.mult, ALU.add)
            if tap:
                self.link(ins)
            else:
                ins.then_inc(s.convd, 1)
        e.wait_ge(s.mla_sq, r)
        self.rms(m.z1f[:, :].rearrange("p (h c) -> p h c", c=QK), 16, QK, 20, s.mla_ms, s.mla_rstd, r)
        qk = m.qk96[:, :, :, :]
        self.link(e.tensor_tensor(qk, qk, m.st[:, 20:36].rearrange("p (t h) -> p t h", t=2).unsqueeze(3).to_broadcast([P, 2, 8, QK]), ALU.mult))
        for x in range(2):
            ins = e.tensor_tensor(qk[:, :, 4 * x:4 * x + 4, :], qk[:, :, 4 * x:4 * x + 4, :],
                                  gains(m.wide_("qk_g")[:, x * QK:(x + 1) * QK], 4, QK), ALU.mult)
        self.link(ins)
        self.rope(qk[:, :, :, NOPE:], qk[:, :, :, NOPE:], m.rope_tmp, "32", ROPE // 2).then_inc(s.mla_ready, 1)
        z, strict = ps[:, 0:4, 0:3 * P], m.cst("strict").unsqueeze(1).to_broadcast([P, 4, 3 * P])
        e.wait_ge(s.z_ln, r)
        self.link(e.scalar_tensor_tensor(m.z1[:, :, :], z, 0.0, m.z0[:, :, :], ALU.min, ALU.subtract))
        self.link(e.tensor_tensor(m.z0[:, :, :], m.z1[:, :, :], z, ALU.subtract))
        e.tensor_tensor(m.z0[:, :, :], m.z0[:, :, :], strict, ALU.mult).then_inc(s.z_l, 1)
        e.wait_ge(s.tail_done, r)
        e.tensor_tensor(m.z1[:, :, :], m.z1[:, :, :], ps[:, 4:8, 0:3 * P], ALU.add).then_inc(s.z_arg, 1)
        e.wait_ge(s.dt_e, r)
        e.tensor_scalar(m.dt[:, 3, :], m.dt[:, 2, :], 1.0, None, ALU.add).then_inc(s.dt_u, 1)
        tiny = 1e-20
        e.wait_ge(s.dt_ln, r)
        e.scalar_tensor_tensor(m.dt[:, 5, :], m.dt[:, 4, :], tiny, m.dt[:, 2, :], ALU.add, ALU.mult)
        self.link(e.tensor_scalar(m.dt[:, 6, :], m.dt[:, 3, :], -1.0, tiny, ALU.add, ALU.add))
        self.link(e.reciprocal(m.dt[:, 7, :], m.dt[:, 6, :]))
        self.link(e.tensor_tensor(m.dt[:, 5, :], m.dt[:, 5, :], m.dt[:, 7, :], ALU.mult))
        self.link(e.scalar_tensor_tensor(m.dt[:, 1, :], m.dt[:, 0, :], 0.0, m.dt[:, 5, :], ALU.max, ALU.add))
        e.scalar_tensor_tensor(m.a[:, :, :], m.dt[:, 1, :].rearrange("p (t h) -> p t h", t=2), -1.0,
                               m.ahead[:, :].unsqueeze(1).to_broadcast([P, 2, 4]), ALU.mult, ALU.mult).then_inc(s.a_ready, 1)
        e.wait_ge(s.z_exp, r)
        e.tensor_tensor(m.z1[:, :, :], m.z1[:, :, :], strict, ALU.mult).then_inc(s.sb_a, 1)
        e.wait_ge(s.sb_o, r)
        e.tensor_copy(m.xn[:, :, 512:768], view(ps[:, 0, :], a=2)).then_inc(s.sb_o_kept, 1)
        self.attention("moba", 2)
        self.attention("mla", 2)
        e.wait_ge(s.xh_kept, r)

        def wide4(ap):
            return ap.rearrange("p (t h) -> p t h", t=2).unsqueeze(3).to_broadcast([P, 2, 4, HD])
        e.tensor_tensor(four(m.xdt[:, :, :], 4), four(m.xh[:, :, :], 4), wide4(m.dt[:, 1, :]), ALU.mult)
        e.tensor_tensor(four(m.y[:, :, :], 4), four(m.xh[:, :, :], 4), gains(m.wide_("ssm_d"), 1, 4).rearrange("p t o h -> p t (o h)")
                        .unsqueeze(3).to_broadcast([P, 2, 4, HD]), ALU.mult)
        e.wait_ge(s.cum_done, r)
        self.link(e.tensor_scalar(m.neg[:, 0:8], ps[:, 4, 256:264], -1.0, None, ALU.mult))
        self.link(e.tensor_tensor(m.neg[:, 8:12], ps[:, 5, P - 1::P], m.neg[:, 0:4], ALU.add))
        for h in range(4):
            row = [ps[:, 5 + t, h * P:(h + 1) * P] for t in range(TT)]
            e.scalar_tensor_tensor(m.z0[:, h, 0:P], row[0], m.neg[:, h:h + 1], m.cst("upto_add"), ALU.add, ALU.add)
            e.tensor_scalar(m.z0[:, h, P:2 * P], row[1], m.neg[:, 8 + h:9 + h], None, ALU.add)
            ins = e.scalar_tensor_tensor(m.z0[:, h, 2 * P:], row[1], m.neg[:, 4 + h:5 + h], m.cst("upto_add"), ALU.add, ALU.add)
        ins.then_inc(s.expo, 1)
        e.wait_ge(s.expo_done, r)
        e.wait_ge(s.gram_done, r)
        for g in range(2):
            w = m.z0[:, 2 * g:2 * g + 2, :]
            ins = e.tensor_tensor(w, w, ps[:, g, 0:3 * P].unsqueeze(1).to_broadcast([P, 2, 3 * P]), ALU.mult)
        ins.then_inc(s.w_ready, 1)
        e.wait_ge(s.ssm_y, r)
        self.link(e.tensor_tensor(m.y[:, :, :], m.y[:, :, :], view(ps[:, 2, :], a=2), ALU.add))
        e.wait_ge(s.z_silu, r)
        e.tensor_tensor(m.y[:, :, :], m.y[:, :, :], m.zs[:, :, :], ALU.mult).then_inc(s.y_sum, 1)
        e.wait_ge(s.head_sq, r)
        self.rms(m.z1f[:, :].rearrange("p (h c) -> p h c", c=HD), 24, HD, 36, s.head_ms, s.head_rstd, r)
        o = four(m.xn[:, :, 0:768], 12)
        self.link(e.tensor_tensor(o, o, m.st[:, 36:60].rearrange("p (t h) -> p t h", t=2).unsqueeze(3).to_broadcast([P, 2, 12, HD]), ALU.mult))
        e.tensor_tensor(m.xn[:, :, 0:768], m.xn[:, :, 0:768], m.wide_("head_g").unsqueeze(1).to_broadcast([P, 2, 768]), ALU.mult)
        e.wait_ge(s.ssm_sq, r)
        e.tensor_scalar(m.ms2[:, 0:2], m.ss2[:, :], 1.0 / GROUP, EPS, ALU.mult, ALU.add).then_inc(s.ssm_ms, 1)
        e.wait_ge(s.ssm_rstd, r)
        for t in range(TT):
            ins = e.scalar_tensor_tensor(m.xn[:, t, 768:D], m.y[:, t, :], m.rs2[:, t:t + 1], m.wide_("ssm_norm"), ALU.mult, ALU.mult)
        ins.then_inc(s.heads_ready, 1)


class Pool(Program):

    def power(self, out, in_, n):
        return self.e.tensor_tensor(out, in_, self.m.cst("minus_half")[:, 0:n], ALU.pow)

    def row(self, dst, src):
        return self.e.dma_start(dst, src.unsqueeze(0).to_broadcast([P] + list(src.shape)))

    def start(self):
        e, m, s, d = self.e, self.m, self.s, self.d
        e.dma_start(m.consts[:, :], d.consts).then_inc(s.params_in, 16)
        e.dma_start(m.pos_i[:, :], d.positions.rearrange("o (t p) -> p (o t)", p=P),
                    allow_slow_non_contiguous=True).then_inc(s.pos_in, 16)
        e.memset(m.rows[:, ROW_TILES - 1, :], 0.0).then_inc(s.pool_step, 1)
        e.wait_ge(s.pool_step, 1)
        src = {"mix_norm_g": d.mix_norm_g.rearrange("l (k c) -> (l k) c", c=P),
               "ffn_norm_g": d.ffn_norm_g.rearrange("l (k c) -> (l k) c", c=P),
               "norm_g": d.norm_g.rearrange("l n (k c) -> (l n k) c", c=P),
               "ssm_conv_w": d.ssm_conv_w.rearrange("l w (k c) -> (l w k) c", c=P),
               "ssm_conv_b": d.ssm_conv_b.rearrange("l (k c) -> (l k) c", c=P),
               "ffn_conv_w": d.ffn_conv_w.rearrange("l w (k c) -> (l w k) c", c=P),
               "ffn_conv_b": d.ffn_conv_b.rearrange("l (k c) -> (l k) c", c=P),
               "b_b_s": d.b_b_s.rearrange("l g c -> (l g) c")}
        for name, first, last, tile, part in row_pieces():
            a = src[name]
            e.dma_start(m.rows[part:part + last - first, tile, :], a[first:last, :]).then_inc(s.rows_in, 16)
        e.dma_start(m.ext[:, 0:2 * REL + 1], d.a_rel_bias.rearrange("l h c -> (l h) c")).then_inc(s.ext_in, 16)
        self.layer_rows(0)
        e.wait_ge(s.ext_out, 1)
        e.dma_start(d.ext_dram, m.ext[:, :]).then_inc(s.ext_stored, 16)
        e.wait_ge(s.ext_stored, 16)

    def layer_rows(self, l):
        m, s, d = self.m, self.s, self.d
        src = {"moba_g": d.moba_qk_g[l].rearrange("a c -> (a c)"), "q_norm": d.mla_q_norm_g[l], "kv_norm": d.mla_kv_norm_g[l],
               "qk_g": d.mla_qk_g[l].rearrange("a c -> (a c)"), "dt_bias": d.ssm_dt_bias[l], "a_log": d.ssm_a_log[l],
               "ssm_d": d.ssm_d[l], "ssm_norm": d.ssm_norm_g[l], "head_g": d.head_out_g[l].rearrange("a h c -> (a h c)")}
        for name in WIDE:
            self.row(m.wide_(name), src[name]).then_inc(s.wide_in, 16)
        self.e.dma_start(m.w_uq[:, 0, :], d.mla_w_uq[l][0:P, :]).then_inc(s.w_in_small, 16)
        self.e.dma_start(m.w_uq[0:QR - P, 1, :], d.mla_w_uq[l][P:QR, :]).then_inc(s.w_in_small, 16)
        self.e.dma_start(m.w_ukv[:, :], d.mla_w_ukv[l]).then_inc(s.w_in_small, 16)

    def load_gain(self, layer, which):
        k = len(self.gains)
        self.gains.append(None)
        if k >= 2:
            self.e.wait_ge(self.s.residual, self.gains[k - 2])
        self.row(self.m.gain[:, (k + 1) % 2, :], self.d.norm_g[layer][which]).then_inc(self.s.gain_in[(k + 1) % 2], 16)

    def norm(self, gain):
        s, m = self.s, self.m
        r = self.round("norm")
        if r == 1:
            self.e.wait_ge(s.params_in, 16)
        self.e.wait_ge(s.meansq, r)
        self.power(m.rs[:, :], m.ms[:, :], 2).then_inc(s.rstd, 1)

    def post_norm(self, source, weight, plain=False):
        m, s = self.m, self.s
        self.sums += TT
        if plain:
            return
        r = self.round("post")
        self.gains[r - 1] = self.sums
        self.e.wait_ge(s.m_meansq, r)
        self.power(m.rs2[:, :], m.ms2[:, :], 2).then_inc(s.m_rstd, 1)

    sums = 0

    def product_tokens(self, what, l, n, _): self.advance(n)
    def product_features(self, what, l, n): self.advance(n)

    def hidden(self, kind, l):
        self.after_hidden(kind)

    def down(self, kind, l):
        self.advance(FT // 2, banks=False)

    def bias_tables(self, kind, l):
        e, m, s, d = self.e, self.m, self.s, self.d
        r = self.round("bias")
        e.wait_ge(s.chunk_done, self.c0)
        if kind == "a":
            w = 3 * P
            for part in range(4):
                src = bass.AP(d.ext_dram.tensor, (l * 16 + part * 4) * w + 1, [[1, P], [w, 4], [1, SEQ]])
                e.dma_start(m.bias[:, part * 4:part * 4 + 4, :], src).then_inc(s.bias_in, 16)
            self.bias_loads = self.round("bias_a") * 64
            e.wait_ge(s.bias_in, self.bias_loads)
            n = 16
        else:
            n = 8
            for h in range(n):
                ins = e.tensor_scalar(m.bias[:, h, :], m.cst("dist"), 2.0 ** (-8.0 * (h + 1) / 8), 0.0, ALU.mult, ALU.add)
            ins.then_inc(s.pool_step, 1)
            self.made = self.round("pool_bias")
            e.wait_ge(s.pool_step, 1 + self.made)
            self.row(m.lam[:, :, :], d.c_lambda[l]).then_inc(s.lam_in, 16)
            self.row(m.sub_g[:, :], d.c_subln_g[l]).then_inc(s.lam_in, 16)
        e.memset(m.bias[0:CHUNK, 0:n, 0:CHUNK], BIG).then_inc(s.bias_ready, 1)

    def attention(self, kind, n): pass

    def sub_norm(self, i):
        s, m = self.s, self.m
        r = self.round("sub")
        self.e.wait_ge(s.sub_ms, r)
        self.power(m.st[:, 0:16], m.st[:, 0:16], 16).then_inc(s.sub_rstd, 1)

    def gmlp(self, l):
        e, m, s, d = self.e, self.m, self.s, self.d
        r = self.round("gmlp")
        e.wait_ge(s.chunk_done, self.c0 - 8)
        e.dma_start(m.b_w[:, :, :], d.b_w_s[l].rearrange("g t s -> t g s")).then_inc(s.bw_in, 16)
        self.row(m.b_rows[:, 0, :], d.b_ln_g[l]).then_inc(s.b_rows_in, 16)
        self.row(m.b_rows[:, 1, :], d.b_ln_b[l]).then_inc(s.b_rows_in, 16)
        e.wait_ge(s.ln_ms, r)
        self.power(m.st[:, 4:6], m.st[:, 2:4], 2).then_inc(s.ln_rstd, 1)

    def mixers(self, l):
        e, m, s = self.e, self.m, self.s
        r = self.round("mixers")
        e.wait_ge(s.c_ms, r)
        self.power(m.st[:, 0:20], m.st[:, 0:20], 20).then_inc(s.c_rstd, 1)
        e.wait_ge(s.mla_ms, r)
        self.power(m.st[:, 20:36], m.st[:, 20:36], 16).then_inc(s.mla_rstd, 1)
        e.wait_ge(s.head_ms, r)
        self.power(m.st[:, 36:60], m.st[:, 36:60], 24).then_inc(s.head_rstd, 1)
        e.wait_ge(s.ssm_ms, r)
        self.power(m.rs2[:, :], m.ms2[:, :], 2).then_inc(s.ssm_rstd, 1)
        e.wait_ge(s.heads_ready, r)
        if l == 0:
            self.layer_rows(1)


LAMBDA_INIT = 0.8 - 0.6 * float(np.exp(-0.3 * 2))


def row_pieces():
    out = []
    for name, n in _rows:
        done = 0
        while done < n:
            at = ROWS[name] + done
            k = min(n - done, P - at % P)
            out.append((name, done, done + k, at // P, at % P))
            done += k
    return out


def chunks_of(stage):
    if stage[0] == "mix1":
        return -(-IN // 256) + 4
    if stage[0] == "mix2":
        return 12 if stage[1] % 3 == 1 else 16
    return FT + FT // 2


class Dram:

    def __init__(self, t):
        self.x = t["x"]
        self.positions = t["positions"]
        self.mix_norm_g = t["mix_norm_g"]
        self.w_in = t["w_in"]
        self.moba_qk_g = t["moba_qk_g"]
        self.mla_q_norm_g = t["mla_q_norm_g"]
        self.mla_kv_norm_g = t["mla_kv_norm_g"]
        self.mla_w_uq = t["mla_w_uq"]
        self.mla_w_ukv = t["mla_w_ukv"]
        self.mla_qk_g = t["mla_qk_g"]
        self.ssm_conv_w = t["ssm_conv_w"]
        self.ssm_conv_b = t["ssm_conv_b"]
        self.ssm_dt_bias = t["ssm_dt_bias"]
        self.ssm_a_log = t["ssm_a_log"]
        self.ssm_d = t["ssm_d"]
        self.ssm_norm_g = t["ssm_norm_g"]
        self.head_out_g = t["head_out_g"]
        self.w_out = t["w_out"]
        self.ffn_norm_g = t["ffn_norm_g"]
        self.ffn_w_in = t["ffn_w_in"]
        self.ffn_conv_w = t["ffn_conv_w"]
        self.ffn_conv_b = t["ffn_conv_b"]
        self.ffn_w_out = t["ffn_w_out"]
        self.norm_g = t["norm_g_2"]
        self.ff1_w_in = t["ff1_w_in_2"]
        self.ff1_w_out = t["ff1_w_out_2"]
        self.ff2_w_in = t["ff2_w_in_2"]
        self.ff2_w_out = t["ff2_w_out_2"]
        self.a_w_qkv = t["a_w_qkv_2"]
        self.a_rel_bias = t["a_rel_bias_2"]
        self.a_w_o = t["a_w_o_2"]
        self.b_w_in = t["b_w_in_2"]
        self.b_ln_g = t["b_ln_g_2"]
        self.b_ln_b = t["b_ln_b_2"]
        self.b_w_s = t["b_w_s_2"]
        self.b_b_s = t["b_b_s_2"]
        self.b_w_o = t["b_w_o_2"]
        self.c_w_qkv = t["c_w_qkv_2"]
        self.c_lambda = t["c_lambda_2"]
        self.c_subln_g = t["c_subln_g_2"]
        self.c_w_o = t["c_w_o_2"]
        self.consts = t["consts"]
        self.out = t["out"]
        self.ext_dram = t["ext_dram"]


def build(nc, d):
    with ExitStack() as ctx:
        m = Memory()

        def sb(stack, name, shape, dt=F32):
            return stack.enter_context(nc.sbuf_tensor(name, shape, dt))

        m.raw = sb(ctx, "raw", [P, RING, CW])
        m.whi = sb(ctx, "whi", [P, RING, CW], F32R)
        m.wlo = sb(ctx, "wlo", [P, RING, CW], F32R)
        m.x = sb(ctx, "x", [P, TT, D])
        m.xn = sb(ctx, "xn", [P, TT, D])
        m.consts = sb(ctx, "consts", [P, CONSTS.shape[1]])
        m.cols = sb(ctx, "cols", [P, ROW_TILES * P])
        m.trig = sb(ctx, "trig", [P, 192])
        m.ss = sb(ctx, "ss", [P, 2])
        m.ms = sb(ctx, "ms", [P, 2])
        m.rs = sb(ctx, "rs", [P, 2])
        m.ss2 = sb(ctx, "ss2", [P, 2])
        m.ms2 = sb(ctx, "ms2", [P, 2])
        m.rs2 = sb(ctx, "rs2", [P, 2])
        m.st = sb(ctx, "st", [P, 60])
        m.lam_d = sb(ctx, "lam_d", [P, 4])
        m.neg = sb(ctx, "neg", [P, 12])
        m.ahead = sb(ctx, "ahead", [P, 4])
        m.pos = sb(ctx, "pos", [P, 2])
        m.pos_i = sb(ctx, "pos_i", [P, 2], I32)
        m.negmax = sb(ctx, "negmax", [P, 2, 2, 2])
        m.sums = sb(ctx, "sums", [P, 2, 2, 2])
        m.rsum = sb(ctx, "rsum", [P, 2, 6])
        m.dt = sb(ctx, "dt", [P, 8, 8])
        m.a = sb(ctx, "a", [P, TT, 4])

        def shared(name, *layouts):
            size, made = 0, []
            for layout in layouts:
                with ExitStack() as inner:
                    used = 0
                    for args in layout:
                        made.append(sb(inner, *args))
                        used += int(np.prod(args[1][1:])) * 4
                    size = max(size, used)
            sb(ctx, name, [P, size // 4])
            return made

        (m.h_hi, m.h_lo, m.qk_rot, m.sb_t, m.moba_t, m.cn) = shared(
            "mem_features",
            [("h_hi", [P, KT, SEQ], F32R), ("h_lo", [P, KT, SEQ], F32R)],
            [("qk_rot", [P, TT, 512]), ("sb_t", [P, 4, SEQ]), ("moba_t", [P, 4, SEQ]), ("cn", [P, TT, QR + KVR])])
        (m.hid_hi, m.hid_lo, m.proj, m.z0, m.z1, m.mla_t, m.xh, m.qk, m.v, m.bias, m.b_uv, m.b_w, m.b_wt, m.b_rows) = shared(
            "mem_hidden",
            [("hid_hi", [P, FT, SEQ], F32R), ("hid_lo", [P, FT, SEQ], F32R)],
            [("proj", [P, TT, IN]), ("z0", [P, 4, 3 * P]), ("z1", [P, 4, 3 * P]), ("mla_t", [P, 8, SEQ]), ("xh", [P, TT, GROUP])],
            [("qk", [P, 16, SEQ]), ("v", [P, TT, D]), ("bias", [P, 16, SEQ])],
            [("b_uv", [P, TT, 2 * D]), ("b_w", [P, 8, P]), ("b_wt", [P, 8, P]), ("b_rows", [P, 2, D])])
        (m.u, m.silu, m.hid, m.prob, m.prob_t, m.rope_tmp, m.rows, m.ang0, m.turns, m.ang) = shared(
            "mem_small",
            [("u", [P, RING, 2, SEQ]), ("silu", [P, RING, SEQ]), ("hid", [P, RING, SEQ])],
            [("prob", [P, 2, 2, 3 * P]), ("prob_t", [P, 2, 2, 3 * P])],
            [("rope_tmp", [P, 4 * 2 * 8 * HD // 2])],
            [("rows", [P, ROW_TILES, P]), ("ang0", [P, 192]), ("turns", [P, 192]), ("ang", [P, 192])])
        (m.qk96, m.xdt, m.y, m.zs, m.ext, m.lam, m.lam_x, m.sub_g) = shared(
            "mem_ssm",
            [("qk96", [P, TT, 8, QK])],
            [("xdt", [P, TT, GROUP]), ("y", [P, TT, GROUP]), ("zs", [P, TT, GROUP])],
            [("ext", [32, 3 * P]), ("lam", [P, 4, 64]), ("lam_x", [P, P]), ("sub_g", [P, P])])
        (m.gain, m.wide) = shared(
            "mem_rows",
            [("gain", [P, 2, D])],
            [("wide", [P, N_WIDE])])
        m.v_mla = sb(ctx, "v_mla", [P, TT, GROUP])
        m.c_t = sb(ctx, "c_t", [P, 3, SEQ])
        m.w_uq = sb(ctx, "w_uq", [P, 2, 4 * QK])
        m.w_ukv = sb(ctx, "w_ukv", [P, 512])
        m.xt = sb(ctx, "xt", [P, 4, 3 + SEQ])
        m.xc = sb(ctx, "xc", [P, 4, SEQ])
        m.conv = sb(ctx, "conv", [P, 4, SEQ])
        m.z0f = m.z0[:, :, :].rearrange("p h c -> p (h c)")
        m.z1f = m.z1[:, :, :].rearrange("p h c -> p (h c)")
        m.ps = ctx.enter_context(nc.psum_tensor("ps", [P, 8, 512], F32))
        m.ident = m.consts[:, CONST["ident"][0]:CONST["ident"][1]]
        m.upto = m.consts[:, CONST["upto"][0]:CONST["upto"][1]]
        m.after = m.consts[:, CONST["after"][0]:CONST["after"][1]]
        m.ones = m.consts[:, CONST["ones"][0]:CONST["ones"][1]]
        m.cst = lambda n: m.consts[:, CONST[n][0]:CONST[n][1]]
        m.wide_ = lambda n: m.wide[:, WIDE[n][0]:WIDE[n][1]]
        m.row_loads = len(row_pieces())
        m.acc = lambda t: m.ps[:, 4 + 2 * t:6 + 2 * t, :].rearrange("p b c -> p (b c)")
        m.junk = lambda t: m.ps[:, 2 * t:2 * t + 2, :].rearrange("p b c -> p (b c)")
        m.b_v = m.b_uv[:, :, D:2 * D]
        sq = m.qk[:, 0:8, :].rearrange("p (t k) c -> p t (k c)", t=2)
        m.sub_squares = lambda t: (m.qk[:, 0:8, :].rearrange("p k (h c) -> p (k h) c", c=P) if t is None else sq[:, t, :])

        def q_pair(tensor, tiles):
            def q(i, h, t):
                return tensor[64 * h:64 * h + 64, i, t * P:(t + 1) * P]

            def k(i, h, nk):
                return tensor[64 * h:64 * h + 64, tiles + i, 0:nk * P]
            return q, k
        m.heads = {
            "a": (*q_pair(m.qk, 8), lambda i, h, t: m.v[:, t, i * P + h * HD:i * P + (h + 1) * HD]),
            "c": (*q_pair(m.qk, 8), lambda i, h, t: m.v[:, t, i * P:(i + 1) * P]),
            "moba": (*q_pair(m.moba_t, 2), lambda i, h, t: m.proj[:, t, 512 + i * P + h * HD:512 + i * P + (h + 1) * HD]),
            "mla": (lambda i, h, t: m.mla_t[0:QK, 2 * i + h, t * P:(t + 1) * P],
                    lambda i, h, nk: m.mla_t[0:QK, 4 + 2 * i + h, 0:nk * P],
                    lambda i, h, t: m.v_mla[:, t, i * P + h * HD:i * P + (h + 1) * HD]),
        }

        s = Semaphores(lambda name: ctx.enter_context(nc.semaphore(name)))
        total = sum(chunks_of(stage) for stage in PLAN)

        block = ctx.enter_context(nc.Block())

        def program(cls, eng):
            p = cls(nc, eng, m, s, d)
            p.total = total
            p.gains = []
            walk(p)

        @block.sync
        def _(eng):
            program(Sync, eng)

        @block.gpsimd
        def _(eng):
            program(Pool, eng)

        @block.scalar
        def _(eng):
            program(Scalar, eng)

        @block.vector
        def _(eng):
            program(Vector, eng)

        @block.tensor
        def _(eng):
            program(Tensor, eng)


INPUTS = ["x", "positions", "mix_norm_g", "w_in", "moba_qk_g", "mla_q_norm_g", "mla_kv_norm_g", "mla_w_uq", "mla_w_ukv",
          "mla_qk_g", "ssm_conv_w", "ssm_conv_b", "ssm_dt_bias", "ssm_a_log", "ssm_d", "ssm_norm_g", "head_out_g", "w_out",
          "ffn_norm_g", "ffn_w_in", "ffn_conv_w", "ffn_conv_b", "ffn_w_out", "norm_g_2", "ff1_w_in_2", "ff1_w_out_2",
          "ff2_w_in_2", "ff2_w_out_2", "a_w_qkv_2", "a_rel_bias_2", "a_w_o_2", "b_w_in_2", "b_ln_g_2", "b_ln_b_2", "b_w_s_2",
          "b_b_s_2", "b_w_o_2", "c_w_qkv_2", "c_lambda_2", "c_subln_g_2", "c_w_o_2"]


def kernel(**inputs):
    import concourse.bacc as bacc
    from concourse.bass_utils import run_bass_kernel_spmd

    nc = bacc.Bacc("TRN2", target_bir_lowering=False, num_devices=1)
    arrays, tensors = {}, {}
    for name in INPUTS + ["consts"]:
        a = np.ascontiguousarray(CONSTS if name == "consts" else inputs[name])
        arrays[f"in_{name}"] = a
        tensors[name] = nc.dram_tensor(f"in_{name}", a.shape, mybir.dt.from_np(a.dtype), kind="ExternalInput").ap()
    tensors["out"] = nc.dram_tensor("out_0", (1, SEQ, D), F32, kind="ExternalOutput").ap()
    tensors["ext_dram"] = nc.dram_tensor("ext_rel_bias", (32, 3 * P), F32, kind="Internal").ap()
    build(nc, Dram(tensors))
    return run_bass_kernel_spmd(nc, [arrays], core_ids=[0]).results[0]["out_0"]
```

```python
from contextlib import ExitStack

import numpy as np

import concourse.bass as bass
import concourse.mybir as mybir
from concourse.alu_op_type import AluOpType as ALU

F32 = mybir.dt.float32
F32R = mybir.dt.float32r
I32 = mybir.dt.int32
ACT = mybir.ActivationFunctionType
AX = mybir.AxisListType.X

P = 128
SEQ, D, FF = 256, 1024, 2816
TT = SEQ // P
KT = D // P
FT = FF // P
GROUP, HD = 256, 64
QR, KVR, ROPE, NOPE = 192, 128, 32, 64
QK = NOPE + ROPE
XBC = 512
IN = 3 * GROUP + QR + KVR + ROPE + 3 * GROUP + GROUP + XBC + 4
C_MOBA = 0
C_CQ = 3 * GROUP
C_CKV = C_CQ + QR
C_KR = C_CKV + KVR
C_SB = C_KR + ROPE
C_Z = C_SB + 3 * GROUP
C_XBC = C_Z + GROUP
C_DT = C_XBC + XBC
EPS = 1e-6
BIG = -1e30
CHUNK = 64
REL = 128
THETA = 10000.0

RING = 3
AHEAD = RING - 1
CW = 2048

PLAN = ([(s, l) for l in range(2) for s in ("mix1", "ffn1")]
        + [s for i in range(4) for s in (("swiglu", i, 0), ("mix2", i), ("swiglu", i, 1))])

CONST = {}


def constants():
    parts, at = [], 0

    def add(name, a):
        nonlocal at
        a = np.asarray(a, np.float32)
        parts.append(a)
        CONST[name] = (at, at + a.shape[1])
        at += a.shape[1]

    r, c = np.arange(P)[:, None], np.arange(P)[None, :]
    add("ident", r == c)
    add("upto", r <= c)
    add("after", r > c)
    add("ones", np.ones((P, P)))
    causal = np.where(c <= r, 0, BIG)
    add("causal", np.concatenate([causal, np.zeros((P, P)), causal], 1))
    add("upto_add", np.where(r <= c, 0, BIG))
    strict = (r < c).astype(np.float32)
    add("strict", np.concatenate([strict, np.ones((P, P)), strict], 1))
    add("minus_half", np.full((P, 24), -0.5))
    for name, dim in (("inv64", HD), ("inv32", ROPE)):
        inv = np.float32(1) / (np.float32(THETA) ** (np.arange(0, dim, 2, dtype=np.float32) / np.float32(dim)))
        add(name, np.broadcast_to(inv.astype(np.float32), (P, dim // 2)))
    add("dist", -np.abs(np.arange(P)[:, None] + np.arange(SEQ)[None, :] - 127))
    return np.concatenate(parts, 1)


CONSTS = constants()

ROWS = {}
_rows = [("mix_norm_g", 2 * KT), ("ffn_norm_g", 2 * KT), ("norm_g", 24 * KT), ("ssm_conv_w", 2 * 4 * 4),
         ("ssm_conv_b", 2 * 4), ("ffn_conv_w", 2 * 3 * 2 * FT), ("ffn_conv_b", 2 * 2 * FT), ("b_b_s", 8)]
_at = 0
for _n, _k in _rows:
    ROWS[_n] = _at
    _at += _k
N_ROWS = _at
ROW_TILES = -(-N_ROWS // P)

WIDE = {}
_wide = [("moba_g", 128), ("q_norm", QR), ("kv_norm", KVR), ("qk_g", 2 * QK), ("dt_bias", 4), ("a_log", 4), ("ssm_d", 4),
         ("ssm_norm", GROUP), ("head_g", 3 * GROUP)]
_at = 0
for _n, _k in _wide:
    WIDE[_n] = (_at, _at + _k)
    _at += _k
N_WIDE = _at

class Semaphores:

    def __init__(self, new):
        self.params_in = new("params_in")
        self.rows_in = new("rows_in")
        self.rows_cleared = new("rows_cleared")
        self.rows_turned = new("rows_turned")
        self.rows_kept = new("rows_kept")
        self.pos_in = new("pos_in")
        self.wide_in = new("wide_in")
        self.ext_out = new("ext_out")
        self.ext_in = new("ext_in")
        self.w_in_small = new("w_in_small")
        self.x_in = new("x_in")
        self.angles = new("angles")
        self.sines = new("sines")
        self.out_stored = new("out_stored")
        self.split_hi = new("split_hi")
        self.split_lo = new("split_lo")
        self.chunk_done = new("chunk_done")
        self.bank_free = new("bank_free")
        self.squares = new("squares")
        self.ln_centred = new("ln_centred")
        self.ln_squares = new("ln_squares")
        self.conv_half = new("conv_half")
        self.o_squares = new("o_squares")
        self.diagonals = new("diagonals")
        self.spread = new("spread")
        self.first_tile = new("first_tile")
        self.dist_in = new("dist_in")
        self.rstd = new("rstd")
        self.normed = new("normed")
        self.turned = new("turned")
        self.hi_turned = new("hi_turned")
        self.features = new("features")
        self.silu = new("silu")
        self.seeded = new("seeded")
        self.gated = new("gated")
        self.hid_hi = new("hid_hi")
        self.hid_ready = new("hid_ready")
        self.m_squares = new("m_squares")
        self.m_meansq = new("m_meansq")
        self.m_rstd = new("m_rstd")
        self.residual = new("residual")
        self.scores = new("scores")
        self.masked = new("masked")
        self.maxed = new("maxed")
        self.exps = new("exps")
        self.mixed = new("mixed")
        self.probs_turned = new("probs_turned")
        self.turned_copied = new("turned_copied")
        self.pair_out = new("pair_out")
        self.out_kept = new("out_kept")
        self.bias_ready = new("bias_ready")
        self.attended = new("attended")
        self.lam_in = new("lam_in")
        self.lam_dots = new("lam_dots")
        self.lam_exps = new("lam_exps")
        self.sub_sq = new("sub_sq")
        self.sub_ms = new("sub_ms")
        self.sub_rstd = new("sub_rstd")
        self.b_rows_in = new("b_rows_in")
        self.bw_in = new("bw_in")
        self.bw_turned = new("bw_turned")
        self.bw_kept = new("bw_kept")
        self.ln_ms = new("ln_ms")
        self.ln_rstd = new("ln_rstd")
        self.v_normed = new("v_normed")
        self.gated_sums = new("gated_sums")
        self.b_y = new("b_y")
        self.moba_sq = new("moba_sq")
        self.c_sq = new("c_sq")
        self.c_ms = new("c_ms")
        self.c_rstd = new("c_rstd")
        self.moba_ready = new("moba_ready")
        self.c_ready = new("c_ready")
        self.sb_turned = new("sb_turned")
        self.sb_kept = new("sb_kept")
        self.xbc_turned = new("xbc_turned")
        self.xbc_kept = new("xbc_kept")
        self.moba_turned = new("moba_turned")
        self.moba_kept = new("moba_kept")
        self.c_turned = new("c_turned")
        self.c_kept = new("c_kept")
        self.up_done = new("up_done")
        self.up_used = new("up_used")
        self.mla_sq = new("mla_sq")
        self.mla_ms = new("mla_ms")
        self.mla_rstd = new("mla_rstd")
        self.mla_ready = new("mla_ready")
        self.mla_turned = new("mla_turned")
        self.mla_kept = new("mla_kept")
        self.z_done = new("z_done")
        self.z_ln = new("z_ln")
        self.z_l = new("z_l")
        self.tail_done = new("tail_done")
        self.z_arg = new("z_arg")
        self.z_exp = new("z_exp")
        self.sb_a = new("sb_a")
        self.sb_o = new("sb_o")
        self.sb_o_kept = new("sb_o_kept")
        self.convd = new("convd")
        self.xc_done = new("xc_done")
        self.xh_turned = new("xh_turned")
        self.xh_kept = new("xh_kept")
        self.dt_raw = new("dt_raw")
        self.dt_abs = new("dt_abs")
        self.dt_e = new("dt_e")
        self.dt_u = new("dt_u")
        self.dt_ln = new("dt_ln")
        self.a_exp = new("a_exp")
        self.a_ready = new("a_ready")
        self.cum_done = new("cum_done")
        self.expo = new("expo")
        self.expo_done = new("expo_done")
        self.gram_done = new("gram_done")
        self.w_ready = new("w_ready")
        self.ssm_y = new("ssm_y")
        self.z_silu = new("z_silu")
        self.ssm_sq = new("ssm_sq")
        self.ssm_ms = new("ssm_ms")
        self.ssm_rstd = new("ssm_rstd")
        self.y_sum = new("y_sum")
        self.head_sq = new("head_sq")
        self.head_ms = new("head_ms")
        self.head_rstd = new("head_rstd")
        self.heads_ready = new("heads_ready")
        self.ext_stored = new("ext_stored")
        self.bias_in = new("bias_in")
        self.recips = new("recips")
        self.weighed = new("weighed")
        self.act_step = new("act_step")
        self.dve_step = new("dve_step")
        self.pool_step = new("pool_step")
        self.landed = [new(f"landed{i}") for i in range(RING)]
        self.gain_in = [new(f"gain_in{i}") for i in range(2)]


class Memory:
    pass


def view(t, **k):
    return t.rearrange("p (a b) -> p a b", **k)


class Program:
    def __init__(self, nc, eng, m, s, d):
        self.nc, self.e, self.m, self.s, self.d = nc, eng, m, s, d
        self.c0 = 0
        self.b0 = 0
        self.f0 = 0
        self.v0 = 0
        self.res = 0
        self.x_by_chunk = False
        self.p0 = 0
        self.rounds = {}
        self.steps_made = 0

    def bank(self, b):
        return (self.b0 + b) % RING

    def round(self, name):
        self.rounds[name] = self.rounds.get(name, 0) + 1
        return self.rounds[name]

    def at(self, sem, value, i=0, per_turn=0):
        if isinstance(i, int):
            value += i * per_turn
            if value > 0:
                self.e.wait_ge(sem, value)
        else:
            assert value > 0
            self.e.wait_ge(sem, i * per_turn + value)

    def steps(self, n, body, unroll=RING, peel=1, last=0):
        if self.c0 == 0:
            peel = n
        peel = min(peel, n)
        for b in range(peel):
            body(b, 0)
        turns = (n - peel - last) // unroll
        b = peel
        if turns >= 2:
            with self.e.Fori(0, turns) as i:
                for u in range(unroll):
                    body(peel + u, i)
            b += turns * unroll
        for b in range(b, n):
            body(b, 0)

    def gated(self, b, i):
        self.at(self.s.gated, self.f0 + b + 1, i, RING)

    def wait_x(self, t, half):
        if self.x_by_chunk:
            self.e.wait_ge(self.s.bank_free, self.b0 - 2 * (1 - half))
        elif self.res:
            self.e.wait_ge(self.s.residual, self.res - 3 + 2 * t + half)
        else:
            self.e.wait_ge(self.s.x_in, 16)

    def renewed(self, source):
        self.x_by_chunk = source == "chunks"
        if not self.x_by_chunk:
            self.res += 2 * TT

    def after_hidden(self, kind):
        self.advance(FT)
        self.f0 += FT
        if kind == "ffn1":
            self.v0 += FT

    def start(self): pass
    def finish(self): pass
    def norm(self, gain, kind): pass
    def turn(self, src, gain, ready): pass
    def post_norm(self, source, weight): self.renewed(source)
    def load_gain(self, layer, which): pass

    def attend(self, kind, l):
        for c in range(12):
            self.attend_chunk(kind, l, c)
            self.attend_pairs(kind, c)
        for c in range(12, values_at(7) + 1):
            self.attend_pairs(kind, c)
        self.p0 += 8
        self.m0 += 8 if kind == "c" else 0
        self.advance(12)

    m0 = 0

    def advance(self, n, banks=True):
        self.c0 += n
        if banks:
            self.b0 += n


def scores_at(b):
    return 3 * (b // 2) + 2


def turned_at(b):
    return scores_at(b) + 1 + b % 2


def values_at(b):
    return turned_at(b) + 1


def places(ready):
    if ready in ("x", "normed"):
        return [(0, 0), (0, 1), (1, 0), (1, 1)]
    return [(0, 0), (1, 0), (0, 1), (1, 1)]


def walk(e):
    e.start()
    for stage in PLAN:
        if stage[0] == "mix1":
            l = stage[1]
            e.norm(ROWS["mix_norm_g"] + l * KT, "tokens")
            e.product_tokens("in1", l, -(-IN // 256), lambda m, j: None)
            e.mixers(l)
            e.turn("mixed", None, "heads_ready")
            e.product_tokens("out1", l, 4, None)
            e.post_norm("chunks", None)
        elif stage[0] == "ffn1":
            l = stage[1]
            e.norm(ROWS["ffn_norm_g"] + l * KT, "scaled")
            e.hidden("ffn1", l)
            e.down("ffn1", l)
            e.post_norm("psum", None)
        elif stage[0] == "swiglu":
            _, i, w = stage
            e.load_gain(i, 4 * w + 1)
            e.norm(ROWS["norm_g"] + (i * 6 + 4 * w) * KT, "features")
            e.hidden("swiglu", (i, w))
            e.down("swiglu", (i, w))
            e.post_norm("psum", 0.5)
        else:
            i = stage[1]
            e.load_gain(i, 3)
            e.norm(ROWS["norm_g"] + (i * 6 + 2) * KT, "tokens" if i % 3 == 1 else "features")
            if i % 3 == 1:
                e.product_tokens("b_in", i // 3, 8, None)
                e.gmlp(i // 3)
                e.turn("xn", None, "b_y")
                e.product_tokens("b_o", i // 3, 4, None)
            else:
                kind = "a" if i % 3 == 0 else "c"
                e.bias_tables(kind, i // 3)
                e.attend(kind, i // 3)
                if kind == "c":
                    e.sub_norm(i)
                e.turn("xn", None, "attended" if kind == "c" else "out_kept")
                e.product_tokens(kind + "_o", i // 3, 4, None)
            e.post_norm("product", 1.0)
    e.finish()


class Sync(Program):

    def start(self):
        e, m, s, d = self.e, self.m, self.s, self.d
        e.dma_start(m.x[:, :, :], d.x.rearrange("o (t p) c -> p (o t) c", p=P)).then_inc(s.x_in, 16)

    def chunk(self, b, i, dst_src):
        c = self.c0 + b
        self.at(self.s.split_lo, c + 1 - RING, i, RING)
        dst, src = dst_src(self.m.raw[:, c % RING, :], b if isinstance(i, int) else i * RING + b)
        self.e.dma_start(dst, src).then_inc(self.s.landed[c % RING], 16)

    def columns(self, w, col, n):
        wv = w.rearrange("(k p) c -> p k c", p=P)

        def pick(raw, j):
            return (raw[:, :].rearrange("p (k c) -> p k c", k=KT), wv[:, :, bass.ds(j * 256 + col, 256)])
        return lambda b, i: self.chunk(b, i, pick)

    def product_tokens(self, what, l, n, _):
        d = self.d
        if what == "in1":
            full = self.columns(d.w_in[l], 0, n)
            for b in range(n - 1):
                full(b, 0)
            rest = IN - 256 * (n - 1)
            wv = d.w_in[l].rearrange("(k p) c -> p k c", p=P)
            self.chunk(n - 1, 0, lambda raw, j: (raw[:, 0:KT * 256].rearrange("p (k c) -> p k c", k=KT)[:, :, 0:rest],
                                                 wv[:, :, 256 * (n - 1):IN]))
        else:
            w, col = {"out1": (d.w_out, 0), "b_in": (d.b_w_in, 0), "b_o": (d.b_w_o, 0), "a_v": (d.a_w_qkv, 2 * D),
                      "a_o": (d.a_w_o, 0), "c_v": (d.c_w_qkv, 2 * D), "c_o": (d.c_w_o, 0)}[what]
            self.steps(n, self.columns(w[l], col, n), peel=0)
        self.advance(n)

    def attend(self, kind, l):
        w = self.d.a_w_qkv if kind == "a" else self.d.c_w_qkv
        for c in range(12):
            self.columns(w[l], (c % 3) * D + (c // 3) * 256 - c * 256, 12)(c, 0)
        self.advance(12)

    def weights_of(self, kind, l):
        d = self.d
        if kind == "ffn1":
            return d.ffn_w_in[l], d.ffn_w_out[l]
        i, w = l
        return (d.ff2_w_in[i], d.ff2_w_out[i]) if w else (d.ff1_w_in[i], d.ff1_w_out[i])

    def hidden(self, kind, l):
        w = self.weights_of(kind, l)[0].rearrange("(k p) (h n c) -> p h k n c", p=P, h=2, c=P)

        def pick(raw, j):
            return (raw[:, :].rearrange("p (h k n c) -> p h k n c", h=2, k=KT, n=1), w[:, :, :, bass.ds(j, 1), :])
        self.steps(FT, lambda b, i: self.chunk(b, i, pick), peel=0)
        self.advance(FT)

    def down(self, kind, l):
        w = self.weights_of(kind, l)[1].rearrange("(n k p) c -> p n k c", p=P, k=2)

        def pick(raw, j):
            return (raw[:, :].rearrange("p (n k c) -> p n k c", n=1, k=2), w[:, bass.ds(j, 1), :, :])
        self.steps(FT // 2, lambda b, i: self.chunk(b, i, pick), peel=0)
        self.advance(FT // 2, banks=False)

    def mixers(self, l): pass
    def gmlp(self, l): pass
    def bias_tables(self, kind, l): pass
    def attention(self, kind, n): pass
    def sub_norm(self, i): pass

    def finish(self):
        e, m, s = self.e, self.m, self.s
        for t in range(TT):
            self.wait_x(t, 1)
        e.dma_start(self.d.out.rearrange("o (t p) c -> p (o t) c", p=P), m.x[:, :, :]).then_inc(s.out_stored, 16)
        e.wait_ge(s.out_stored, 16)


class Tensor(Program):
    def start(self):
        e, m, s = self.e, self.m, self.s
        e.wait_ge(s.params_in, 16)
        e.wait_ge(s.rows_in, 16 * m.row_loads)
        for r in range(ROW_TILES):
            ins = e.transpose(m.ps[:, r, 0:P], m.rows[:, r, :], m.ident)
        ins.then_inc(s.rows_turned, 1)

    def turn(self, src, gain, ready):
        e, m, s = self.e, self.m, self.s
        a = m.x if src == "x" else m.xn
        if ready == "out_kept":
            e.wait_ge(s.out_kept, self.p0)
        elif ready == "b_y":
            e.wait_ge(s.b_y, self.round("b_y"))
        elif ready != "x":
            r = self.round(ready)
        if self.round("turn") == 1:
            e.wait_ge(s.rows_kept, 1)
        for n, (t, half) in enumerate(places(ready)):
            if ready == "x":
                self.wait_x(t, half)
            elif ready == "normed":
                e.wait_ge(s.normed, 2 * TT * (r - 1) + n + 1)
            elif ready == "attended":
                e.wait_ge(s.attended, 4 * (r - 1) + n + 1)
            elif ready == "heads_ready":
                e.wait_ge(s.heads_ready, 2 * (r - 1) + half + 1)
            for k in range(4):
                f = 4 * half + k
                ins = e.transpose(m.ps[:, 4 + n, k * P:(k + 1) * P], a[:, t, f * P:(f + 1) * P], m.ident)
            ins.then_inc(s.turned, 1)

    def norm(self, gain, kind):
        self.turn("xn" if kind == "scaled" else "x", gain, "normed" if kind == "scaled" else "x")

    def begin_product(self):
        self.turns = self.round("features")

    def first_features(self, k):
        if k % 4 == 0:
            self.e.wait_ge(self.s.features, 4 * (self.turns - 1) + 2 + 2 * (k // 4))

    def spread(self):
        e, m, s = self.e, self.m, self.s
        r = self.round("spread")
        e.wait_ge(s.diagonals, TT * r)
        for t in range(TT):
            ins = e.matmul(m.ps[:, 3, t * P:(t + 1) * P], m.ones, m.diag[:, t, :], start=True, stop=True)
        ins.then_inc(s.spread, 1)

    def chunk_start(self, b, i):
        self.at(self.s.split_lo, self.c0 + b + 1, i, RING)
        self.at(self.s.bank_free, self.b0 + b + 1 - RING, i, RING)

    def tokens_chunk(self, b, i, w=256, between=None):
        e, m, s = self.e, self.m, self.s
        self.chunk_start(b, i)
        c = self.c0 + b
        whi = m.whi[:, c % RING, :].rearrange("p (k c) -> p k c", k=KT)
        wlo = m.wlo[:, c % RING, :].rearrange("p (k c) -> p k c", k=KT)
        for t in range(TT):
            if t == 1 and between is not None:
                between()
            out = m.ps[:, self.bank(b), t * 256:t * 256 + w]
            for k in range(KT):
                if b == 0 and t == 0 and isinstance(i, int):
                    self.first_features(k)
                hi, lo = m.h_hi[:, k, t * P:(t + 1) * P], m.h_lo[:, k, t * P:(t + 1) * P]
                e.matmul(out, hi, whi[:, k, 0:w], start=(k == 0), stop=False)
                e.matmul(out, hi, wlo[:, k, 0:w], start=False, stop=False)
                ins = e.matmul(out, lo, whi[:, k, 0:w], start=False, stop=(k == KT - 1))
        ins.then_inc(s.chunk_done, 1)

    def product_tokens(self, what, l, n, _):
        self.begin_product()
        self.steps(n, lambda b, i: self.tokens_chunk(b, i, IN - 256 * b if what == "in1" and b == n - 1 else 256),
                   peel=n if what == "in1" or n == 4 else 1)
        self.advance(n)

    def features_chunk(self, b, i, w_of, spread=True):
        e, m, s = self.e, self.m, self.s
        self.chunk_start(b, i)
        c = self.c0 + b
        for f in range(2):
            out = m.ps[:, self.bank(b), f * 256:(f + 1) * 256]
            for k in range(KT):
                if b == 0 and f == 0 and isinstance(i, int):
                    self.first_features(k)
                hi, lo = w_of(m.whi[:, c % RING, :], f, k), w_of(m.wlo[:, c % RING, :], f, k)
                e.matmul(out, hi, m.h_hi[:, k, :], start=(k == 0), stop=False)
                e.matmul(out, hi, m.h_lo[:, k, :], start=False, stop=False)
                ins = e.matmul(out, lo, m.h_hi[:, k, :], start=False, stop=(k == KT - 1))
        ins.then_inc(s.chunk_done, 1)
        if b == 0 and isinstance(i, int) and spread:
            self.spread()

    def attend_chunk(self, kind, l, c):
        if c == 0:
            self.begin_product()
        if c % 3 < 2:
            self.features_chunk(c, 0, lambda w, f, k: w[:, k * 256 + f * P:k * 256 + (f + 1) * P])
        else:
            self.tokens_chunk(c, 0, between=lambda: self.pair_scores(kind, 2 * (c // 3)))

    def pair_scores(self, kind, b):
        self.e.wait_ge(self.s.bank_free, self.b0 + 3 * (b // 2) + 2)
        self.scores(kind, b)

    def attend_pairs(self, kind, c):
        for b in range(8):
            if values_at(b) == c:
                self.e.wait_ge(self.s.bank_free, self.b0 + 3 * (b // 2) + 3)
                self.values(kind, b)
        for b in range(8):
            if turned_at(b) == c:
                self.turn_probs(kind, b)
        for b in range(1, 8, 2):
            if scores_at(b) == c:
                self.pair_scores(kind, b)

    def hidden(self, kind, l):
        self.begin_product()

        def w_of(w, f, k):
            return w[:, (f * KT + k) * P:(f * KT + k + 1) * P]
        self.steps(FT, lambda b, i: self.features_chunk(b, i, w_of, kind == "swiglu"), peel=1)
        self.after_hidden(kind)

    def down(self, kind, l):
        e, m, s = self.e, self.m, self.s
        for b in range(FT // 2):
            c = self.c0 + b
            self.at(s.split_lo, c + 1)
            self.at(s.hid_ready, self.f0 - FT + 2 * b + 2)
            whi = m.whi[:, c % RING, :].rearrange("p (k c) -> p k c", k=2)
            wlo = m.wlo[:, c % RING, :].rearrange("p (k c) -> p k c", k=2)
            for t in range(TT):
                for k in range(2):
                    f = 2 * b + k
                    hi, lo = m.hid_hi[:, f, t * P:(t + 1) * P], m.hid_lo[:, f, t * P:(t + 1) * P]
                    for x, w in ((hi, whi), (hi, wlo), (lo, whi)):
                        for h in range(2):
                            ins = e.matmul(m.ps[:, 4 + 2 * t + h, :], x, w[:, k, h * 512:(h + 1) * 512],
                                           start=(f == 0 and x is hi and w is whi),
                                           stop=(f == FT - 1 and x is lo))
                if b == FT // 2 - 1 and t == 0:
                    ins.then_inc(s.first_tile, 1)
            ins.then_inc(s.chunk_done, 1)
        self.advance(FT // 2, banks=False)

    def scores(self, kind, b):
        e, m, s = self.e, self.m, self.s
        (q, k, _), bank = m.heads[kind], m.score_bank[kind]
        self.at(s.masked, self.p0 + b)
        for h in range(2):
            e.matmul(m.ps[:, bank + h, 0:P], q(b, h, 0), k(b, h, 1), start=True, stop=True)
            ins = e.matmul(m.ps[:, bank + h, P:P + SEQ], q(b, h, 1), k(b, h, 2), start=True, stop=True)
        ins.then_inc(s.scores, 1)

    def turn_probs(self, kind, b):
        e, m, s = self.e, self.m, self.s
        if kind == "c":
            self.at(s.mixed, self.m0 + b + 1)
        else:
            self.at(s.exps, self.p0 + b + 1)
        self.at(s.turned_copied, self.p0 + b)
        for h in range(1 if kind == "c" else 2):
            for j in range(3):
                ins = e.transpose(m.ps[:, m.turn_bank[kind] + h, j * P:(j + 1) * P], m.prob[:, b % 2, h, j * P:(j + 1) * P],
                                  m.ident)
        ins.then_inc(s.probs_turned, 1)

    def values(self, kind, b):
        e, m, s = self.e, self.m, self.s
        v, out = m.heads[kind][2], m.ps[:, m.out_bank[kind], 0:SEQ]
        self.at(s.turned_copied, self.p0 + b + 1)
        self.at(s.out_kept, self.p0 + b)
        parts = 1 if kind == "c" else 2
        w = P // parts
        for h in range(parts):
            pt = m.prob_t[:, b % 2, h, :]
            t0, t1 = out[:, h * w:(h + 1) * w], out[:, P + h * w:P + (h + 1) * w]
            e.matmul(t0, pt[:, 0:P], v(b, h, 0), start=True, stop=True)
            e.matmul(t1, pt[:, P:2 * P], v(b, h, 0), start=True, stop=False)
            ins = e.matmul(t1, pt[:, 2 * P:3 * P], v(b, h, 1), start=False, stop=True)
        ins.then_inc(s.pair_out, 1)

    def attention(self, kind, n):
        self.scores(kind, 0)
        for b in range(n):
            if b < n - 1:
                self.scores(kind, b + 1)
            self.turn_probs(kind, b)
            self.values(kind, b)
        self.p0 += n

    def bias_tables(self, kind, l): pass
    def sub_norm(self, i): pass

    def gmlp(self, l):
        e, m, s = self.e, self.m, self.s
        r = self.round("gmlp")
        e.wait_ge(s.bw_in, 16 * r)
        e.wait_ge(s.bank_free, self.b0)
        for g in range(8):
            ins = e.transpose(m.ps[:, 4 + g // 4, (g % 4) * P:(g % 4 + 1) * P], m.b_w[:, g, :], m.ident)
        ins.then_inc(s.bw_turned, 1)
        e.wait_ge(s.bw_kept, 2 * r)
        e.wait_ge(s.v_normed, r)
        for t in range(TT):
            for g in range(8):
                ins = e.matmul(m.ps[:, 2 * t + g // 4, (g % 4) * P:(g % 4 + 1) * P], m.b_wt[:, g, :],
                               m.b_v[:, t, g * P:(g + 1) * P], start=True, stop=True)
        ins.then_inc(s.gated_sums, 1)

    def mixers(self, l):
        e, m, s = self.e, self.m, self.s
        r = self.round("mixers")
        ps, proj, ident = m.ps, m.proj, m.ident
        e.wait_ge(s.bank_free, self.b0)
        for x in range(2):
            for j in range(2):
                for t in range(TT):
                    col = C_SB + x * GROUP + j * P
                    ins = e.transpose(ps[:, 2 + x, j * 256 + t * P:j * 256 + (t + 1) * P], proj[:, t, col:col + P], ident)
        ins.then_inc(s.sb_turned, 1)
        for j in range(4):
            for t in range(TT):
                col = C_XBC + j * P
                ins = e.transpose(ps[:, 4 + j // 2, (j % 2) * 256 + t * P:(j % 2) * 256 + (t + 1) * P],
                                  proj[:, t, col:col + P], ident)
        ins.then_inc(s.xbc_turned, 1)
        e.wait_ge(s.c_ready, r)
        for t in range(TT):
            e.transpose(ps[:, 6, t * P:(t + 1) * P], m.cn[:, t, 0:P], ident)
            e.transpose(ps[0:64, 6, 256 + t * P:256 + (t + 1) * P], m.cn[:, t, P:QR], ident)
            ins = e.transpose(ps[:, 7, t * P:(t + 1) * P], m.cn[:, t, QR:QR + KVR], ident)
        ins.then_inc(s.c_turned, 1)
        e.wait_ge(s.w_in_small, 48 * r)
        e.wait_ge(s.c_kept, r)
        e.wait_ge(s.xbc_kept, r)
        for t in range(TT):
            tok = slice(t * P, (t + 1) * P)
            e.matmul(ps[:, t, 0:4 * QK], m.c_t[:, 0, tok], m.w_uq[:, 0, :], start=True, stop=False)
            e.matmul(ps[:, t, 0:4 * QK], m.c_t[0:64, 1, tok], m.w_uq[0:64, 1, :], start=False, stop=True)
            ins = e.matmul(ps[:, 4 + t, :], m.c_t[:, 2, tok], m.w_ukv[:, :], start=True, stop=True)
        ins.then_inc(s.up_done, 1)
        e.wait_ge(s.moba_ready, r)
        e.wait_ge(s.c_kept, r)
        for x in range(2):
            for j in range(2):
                for t in range(TT):
                    col = x * GROUP + j * P
                    ins = e.transpose(ps[:, 6 + x, j * 256 + t * P:j * 256 + (t + 1) * P], m.qk_rot[:, t, col:col + P], ident)
        ins.then_inc(s.moba_turned, 1)
        e.wait_ge(s.up_used, r)
        e.wait_ge(s.sb_kept, r)
        for h in range(4):
            part = slice(64 * (h % 2), 64 * (h % 2) + 64)
            e.matmul(ps[:, h, 0:SEQ], m.sb_t[part, 2 + h // 2, 0:P], m.sb_t[part, h // 2, :], start=True, stop=True)
            ins = e.matmul(ps[:, h, SEQ:SEQ + P], m.sb_t[part, 2 + h // 2, P:SEQ], m.sb_t[part, h // 2, P:SEQ],
                           start=True, stop=True)
        ins.then_inc(s.z_done, 1)
        e.wait_ge(s.moba_kept, r)
        e.wait_ge(s.z_l, r)
        for h in range(4):
            low = m.z0[:, h, :]
            e.matmul(ps[:, 4 + h, 0:SEQ], m.after, low[:, 0:SEQ], start=True, stop=False)
            e.matmul(ps[:, 4 + h, P:SEQ], m.ones, low[:, SEQ:SEQ + P], start=False, stop=True)
            ins = e.matmul(ps[:, 4 + h, SEQ:SEQ + P], m.after, low[:, SEQ:SEQ + P], start=False, stop=True,
                           skip_group_check=True)
        ins.then_inc(s.tail_done, 1)
        e.wait_ge(s.sb_a, r)
        for h in range(4):
            vcol = C_SB + 2 * GROUP + h * HD
            self.two_blocks(ps[:, 0, :], h, m.z1[:, h, :], lambda t: proj[:, t, vcol:vcol + HD])
        self.last.then_inc(s.sb_o, 1)
        e.wait_ge(s.sb_o_kept, r)
        self.attention("moba", 2)
        e.wait_ge(s.mla_ready, r)
        for h in range(8):
            for t in range(TT):
                ins = e.transpose(ps[0:QK, h // 2, (h % 2) * 256 + t * P:(h % 2) * 256 + (t + 1) * P],
                                  m.qk96[:, t, h, :], ident)
        ins.then_inc(s.mla_turned, 1)
        e.wait_ge(s.mla_kept, r)
        self.attention("mla", 2)
        e.wait_ge(s.xc_done, r)
        e.wait_ge(s.z_arg, r)
        for j in range(2):
            for t in range(TT):
                ins = e.transpose(ps[:, 7, t * 256 + j * P:t * 256 + (j + 1) * P], m.xc[:, j, t * P:(t + 1) * P], ident)
        ins.then_inc(s.xh_turned, 1)
        e.wait_ge(s.a_ready, r)
        e.wait_ge(s.out_kept, self.p0)
        for t in range(TT):
            for h in range(4):
                e.matmul(ps[:, 5 + t, h * P:(h + 1) * P], m.a[:, t, h:h + 1].to_broadcast([P, P]), m.upto, start=True, stop=True)
            ins = e.matmul(ps[:, 4, 256 + t * 4:256 + t * 4 + 4], m.upto, m.a[:, t, :], start=True, stop=True)
        ins.then_inc(s.cum_done, 1)
        for g in range(2):
            part = slice(64 * g, 64 * g + 64)
            e.matmul(ps[:, g, 0:SEQ], m.xc[part, 2, 0:P], m.xc[part, 3, :], start=True, stop=True)
            ins = e.matmul(ps[:, g, SEQ:SEQ + P], m.xc[part, 2, P:SEQ], m.xc[part, 3, P:SEQ], start=True, stop=True)
        ins.then_inc(s.gram_done, 1)
        e.wait_ge(s.w_ready, r)
        for h in range(4):
            self.two_blocks(ps[:, 2, :], h, m.z0[:, h, :], lambda t: m.xdt[:, t, h * HD:(h + 1) * HD])
        self.last.then_inc(s.ssm_y, 1)

    def two_blocks(self, bank, h, w, rhs):
        e, c = self.e, slice(h * HD, (h + 1) * HD)
        e.matmul(bank[:, h * HD:(h + 1) * HD], w[:, 0:P], rhs(0), start=True, stop=True)
        e.matmul(bank[:, 256 + h * HD:256 + (h + 1) * HD], w[:, P:2 * P], rhs(0), start=True, stop=False)
        self.last = e.matmul(bank[:, 256 + h * HD:256 + (h + 1) * HD], w[:, 2 * P:3 * P], rhs(1), start=False, stop=True)


class Scalar(Program):
    def act(self, *a, **k):
        return self.nc.scalar.activation(*a, **k)

    def link(self, ins):
        self.steps_made += 1
        ins.then_inc(self.s.act_step, 1)
        self.e.wait_ge(self.s.act_step, self.steps_made)

    def split(self, b, i):
        m, s = self.m, self.s
        c = self.c0 + b + AHEAD
        if isinstance(i, int) and c >= self.total:
            return
        slot = c % RING
        self.at(s.landed[slot], 16 * (c // RING + 1), i, 16)
        self.at(s.chunk_done, c + 1 - RING, i, RING)
        self.act(m.whi[:, slot, :], m.raw[:, slot, :], ACT.Copy).then_inc(s.split_hi, 1)

    def start(self):
        e, m, s, d = self.e, self.m, self.s, self.d
        e.dma_start(m.consts[:, :], d.consts[:, 0:CONST["dist"][0]]).then_inc(s.params_in, 16)
        e.wait_ge(s.rows_cleared, 1)
        src = {"mix_norm_g": d.mix_norm_g.rearrange("l (k c) -> (l k) c", c=P),
               "ffn_norm_g": d.ffn_norm_g.rearrange("l (k c) -> (l k) c", c=P),
               "norm_g": d.norm_g.rearrange("l n (k c) -> (l n k) c", c=P),
               "ssm_conv_w": d.ssm_conv_w.rearrange("l w (k c) -> (l w k) c", c=P),
               "ssm_conv_b": d.ssm_conv_b.rearrange("l (k c) -> (l k) c", c=P),
               "ffn_conv_w": d.ffn_conv_w.rearrange("l w (k c) -> (l w k) c", c=P),
               "ffn_conv_b": d.ffn_conv_b.rearrange("l (k c) -> (l k) c", c=P),
               "b_b_s": d.b_b_s.rearrange("l g c -> (l g) c")}
        for name, first, last, tile, part in row_pieces():
            a = src[name]
            e.dma_start(m.rows[part:part + last - first, tile, :], a[first:last, :]).then_inc(s.rows_in, 16)
        e.dma_start(m.pos_i[:, :], d.positions.rearrange("o (t p) -> p (o t)", p=P),
                    allow_slow_non_contiguous=True).then_inc(s.pos_in, 16)
        for b in range(-AHEAD, 0):
            self.split(b, 0)
        e.wait_ge(s.rows_turned, 1)
        self.act(m.cols[:, :].rearrange("p (r c) -> p r c", c=P), m.ps[:, 0:ROW_TILES, 0:P], ACT.Copy).then_inc(s.rows_kept, 1)
        e.wait_ge(s.rows_kept, 1)
        e.wait_ge(s.angles, 1)
        self.act(m.trig[:, :], m.ang[:, :], ACT.Sin).then_inc(s.sines, 1)

    def norm(self, gain, kind):
        e, m, s = self.e, self.m, self.s
        r = self.round("norm")
        if r == 1:
            e.wait_ge(s.sines, 1)

        def square(t):
            self.wait_x(t, 1)
            self.act(m.junk[:, t, :], m.x[:, t, :], ACT.Square, scale=D ** -0.5,
                     accum_out=m.ss[:, t:t + 1]).then_inc(s.squares, 1)
        if kind == "scaled":
            for t in range(TT):
                square(t)
            self.turn("xn", gain, "normed")
        else:
            self.turn("x", gain, "x", square)

    def turn(self, src, gain, ready, between=lambda t: None):
        e, m, s = self.e, self.m, self.s
        r = self.round("turn")
        if r == 1:
            e.wait_ge(s.rows_kept, 1)
        for n, (t, half) in enumerate(places(ready)):
            e.wait_ge(s.turned, 4 * (r - 1) + n + 1)
            tok, ps = slice(t * P, (t + 1) * P), view(m.ps[:, 4 + n, :], a=4)
            if gain is None:
                ins = self.act(m.h_hi[:, 4 * half:4 * half + 4, tok], ps, ACT.Copy)
            else:
                for k in range(4):
                    f = 4 * half + k
                    ins = self.act(m.h_hi[:, f, tok], ps[:, k, :], ACT.Copy, scale=m.cols[:, gain + f:gain + f + 1])
            ins.then_inc(s.hi_turned, 1)
            if half == 1:
                between(t)

    def chunk_ready(self, b, i):
        self.at(self.s.chunk_done, self.c0 + b + 1, i, RING)

    def product_tokens(self, what, l, n, _):
        e, m, s = self.e, self.m, self.s

        def body(b, i):
            self.split(b, i)
            if what == "out1":
                return
            self.chunk_ready(b, i)
            if what in ("a_o", "b_o", "c_o"):
                for t in range(TT):
                    ins = self.act(m.junk[:, t, b * 256:(b + 1) * 256], m.ps[:, self.bank(b), t * 256:(t + 1) * 256], ACT.Square,
                                   scale=D ** -0.5, accum_out=m.ss2[:, t, b:b + 1])
                ins.then_inc(s.o_squares, 1)
                return
            if b == 0 and isinstance(i, int):
                e.wait_ge(s.rstd, TT * self.rounds["norm"])
                self.at(s.bank_free, self.b0)
            dest = {"in1": lambda: m.proj, "a_v": lambda: m.v, "c_v": lambda: m.v, "b_in": lambda: m.b_uv}[what]()
            w = 256
            if what == "in1" and b == n - 1:
                w = IN - 256 * (n - 1)
            j = b if isinstance(i, int) else i * RING + b
            for t in range(TT):
                ins = self.act(dest[:, t, bass.ds(j * 256, w)], m.ps[:, self.bank(b), t * 256:t * 256 + w],
                               ACT.Gelu if what == "b_in" else ACT.Copy, scale=m.rs[:, t:t + 1])
            ins.then_inc(s.bank_free, 1)
        self.steps(n, body, peel=n if what == "in1" or n == 4 else 1)
        self.advance(n)

    def attend_chunk(self, kind, l, c):
        self.split(c, 0)
        if c == 2 and kind == "c":
            self.lambda_exps()
        for b in range(0, 8, 2):
            if scores_at(b) == c:
                self.exps(kind, b)

    def attend_pairs(self, kind, c):
        for b in range(8):
            if values_at(b) == c and kind == "c":
                self.square_out(b)
        for b in range(8):
            if turned_at(b) == c:
                self.keep_turned(kind, b)
        for b in range(1, 8, 2):
            if scores_at(b) == c:
                self.exps(kind, b)

    def square_out(self, b):
        m, s = self.m, self.s
        self.at(s.pair_out, self.p0 + b + 1)
        for t in range(TT):
            at = 8 * (b // 4) + 4 * t + b % 4
            ins = self.act(m.sub_x[:, t, :], m.ps[:, m.out_bank["c"], t * P:(t + 1) * P], ACT.Square, scale=0.125,
                           accum_out=m.st[:, at:at + 1])
        ins.then_inc(s.sub_sq, 1)

    def hidden(self, kind, l):
        e, m, s = self.e, self.m, self.s

        def hi(b, i):
            self.gated(b, i)
            j = b if isinstance(i, int) else i * RING + b
            self.act(m.hid_hi[:, bass.ds(j, 1), :], m.hid[:, b % RING:b % RING + 1, :], ACT.Copy).then_inc(s.hid_hi, 1)

        def silu(b, i):
            self.at(s.bank_free, self.b0 + b + 1, i, RING)
            self.gated(b - RING, i)
            self.act(m.silu[:, b % RING, :], m.u[:, b % RING, 0, :], ACT.Silu).then_inc(s.silu, 1)

        def body(b, i):
            self.split(b, i)
            if kind == "ffn1":
                self.chunk_ready(b, i)
                self.gated(b - RING, i)
                j = b if isinstance(i, int) else i * RING + b
                for g in range(2):
                    w = ROWS["ffn_conv_w"] + (l * 3 + 2) * 2 * FT + g * FT
                    bias = ROWS["ffn_conv_b"] + l * 2 * FT + g * FT
                    ins = self.act(m.u[:, b % RING, g, :], m.ps[:, self.bank(b), g * 256:(g + 1) * 256], ACT.Identity,
                                   bias=m.cols[:, bass.ds(j + bias, 1)], scale=m.cols[:, bass.ds(j + w, 1)])
                ins.then_inc(s.seeded, 1)
            if b > 0:
                silu(b - 1, i)
            if b > 1:
                hi(b - 2, i)
        self.steps(FT, body, peel=4)
        silu(FT - 1, 0)
        hi(FT - 2, 0)
        hi(FT - 1, 0)
        self.after_hidden(kind)

    def down(self, kind, l):
        self.round("down")
        for b in range(FT // 2):
            self.split(b, 0)
        self.advance(FT // 2, banks=False)

    def post_norm(self, source, weight):
        e, m, s = self.e, self.m, self.s
        if source == "psum" and weight is not None:
            r = self.round("post_psum")
            for t in range(TT):
                if t == 0:
                    e.wait_ge(s.first_tile, self.rounds["down"])
                else:
                    e.wait_ge(s.chunk_done, self.c0)
                for half in range(2):
                    self.act(m.junk[:, t, half * 512:(half + 1) * 512], m.ps[:, 4 + 2 * t + half, :], ACT.Square,
                             scale=D ** -0.5, accum_out=m.ss2[:, t, half:half + 1]).then_inc(s.m_squares, 1)
        self.renewed(source)

    def bias_tables(self, kind, l): pass

    def lambda_exps(self):
        m, s = self.m, self.s
        self.e.wait_ge(s.lam_dots, self.round("lam"))
        self.act(m.lam_d[:, 0:2], m.lam_d[:, 0:2], ACT.Exp).then_inc(s.lam_exps, 1)

    def exps(self, kind, b):
        m, s, par = self.m, self.s, b % 2
        self.at(s.maxed, self.p0 + b + 1)
        for h in range(2):
            for t in range(2):
                cols = slice(0, P) if t == 0 else slice(P, P + SEQ)
                ins = self.act(m.prob[:, par, h, cols], m.prob[:, par, h, cols], ACT.Exp,
                               bias=m.negmax[:, par, h, t:t + 1], accum_out=m.sums[:, par, h, t:t + 1])
        ins.then_inc(s.exps, 1)

    def keep_turned(self, kind, b):
        m, s, par, bank = self.m, self.s, b % 2, self.m.turn_bank[kind]
        parts = 1 if kind == "c" else 2
        self.at(s.probs_turned, self.p0 + b + 1)
        self.at(s.pair_out, self.p0 + b - 1)
        self.act(m.prob_t[:, par, 0:parts, :], m.ps[:, bank:bank + parts, 0:3 * P], ACT.Copy).then_inc(s.turned_copied, 1)

    def attention(self, kind, n):
        for b in range(n):
            self.exps(kind, b)
            self.keep_turned(kind, b)
        self.p0 += n

    def sub_norm(self, i): pass

    def gmlp(self, l):
        e, m, s = self.e, self.m, self.s
        r = self.round("gmlp")
        e.wait_ge(s.ln_centred, r)
        for t in range(TT):
            ins = self.act(m.junk[:, t, :], m.b_v[:, t, :], ACT.Square, accum_out=m.ss3[:, t:t + 1])
        ins.then_inc(s.ln_squares, 1)

    def mixers(self, l):
        e, m, s = self.e, self.m, self.s
        r = self.round("mixers")
        ps, proj = m.ps, m.proj
        cst = m
        e.wait_ge(s.bank_free, self.b0)
        self.act(m.z0f[:, 0:1024].rearrange("p (t c) -> p t c", t=2), proj[:, :, 0:512], ACT.Square).then_inc(s.moba_sq, 1)
        self.act(m.z1f[:, 0:640].rearrange("p (t c) -> p t c", t=2), proj[:, :, C_CQ:C_KR], ACT.Square).then_inc(s.c_sq, 1)
        e.wait_ge(s.sb_turned, r)
        self.act(m.sb_t[:, 0:2, :], view(ps[:, 2, :], a=2), ACT.Copy, scale=HD ** -0.5)
        self.act(m.sb_t[:, 2:4, :], view(ps[:, 3, :], a=2), ACT.Copy).then_inc(s.sb_kept, 1)
        e.wait_ge(s.xbc_turned, r)
        for j in range(2):
            ins = self.act(m.xt[:, 2 * j:2 * j + 2, 3:3 + SEQ], view(ps[:, 4 + j, :], a=2), ACT.Copy)
        ins.then_inc(s.xbc_kept, 1)
        e.wait_ge(s.c_turned, r)
        self.act(m.c_t[:, 0, :], ps[:, 6, 0:256], ACT.Copy)
        self.act(m.c_t[0:64, 1, :], ps[0:64, 6, 256:512], ACT.Copy)
        self.act(m.c_t[:, 2, :], ps[:, 7, 0:256], ACT.Copy).then_inc(s.c_kept, 1)
        e.wait_ge(s.up_done, r)
        for t in range(TT):
            self.act(m.qk96[:, t, 0:4, :], ps[:, t, 0:4 * QK].rearrange("p (h c) -> p h c", h=4), ACT.Copy)
            kv = ps[:, 4 + t, :].rearrange("p (h c) -> p h c", h=4)
            self.act(m.qk96[:, t, 4:8, 0:NOPE], kv[:, :, 0:NOPE], ACT.Copy)
            for h in range(4):
                self.act(m.qk96[:, t, 4 + h, NOPE:QK], proj[:, t, C_KR:C_KR + ROPE], ACT.Copy)
            ins = self.act(m.v_mla[:, t, :].rearrange("p (h c) -> p h c", h=4), kv[:, :, NOPE:], ACT.Copy)
        ins.then_inc(s.up_used, 1)
        e.wait_ge(s.up_used, r)
        e.wait_ge(s.moba_ready, r)
        self.act(m.z1f[:, :].rearrange("p (t c) -> p t c", t=2), m.qk96[:, :, :, :].rearrange("p t h c -> p t (h c)"), ACT.Square).then_inc(s.mla_sq, 1)
        e.wait_ge(s.moba_turned, r)
        self.act(m.moba_t[:, 0:2, :], view(ps[:, 6, :], a=2), ACT.Copy, scale=HD ** -0.5)
        self.act(m.moba_t[:, 2:4, :], view(ps[:, 7, :], a=2), ACT.Copy).then_inc(s.moba_kept, 1)
        e.wait_ge(s.convd, r)
        self.act(m.xc[:, :, :], m.conv[:, :, :], ACT.Silu).then_inc(s.xc_done, 1)
        z = ps[:, 0:4, 0:3 * P]
        e.wait_ge(s.z_done, r)
        self.link(self.act(m.z0[:, :, :], z, ACT.Abs))
        self.link(self.act(m.z0[:, :, :], m.z0[:, :, :], ACT.Exp, scale=-1.0))
        self.act(m.z0[:, :, :], m.z0[:, :, :], ACT.Ln, bias=1.0).then_inc(s.z_ln, 1)
        e.wait_ge(s.z_arg, r)
        self.act(m.z1[:, :, :], m.z1[:, :, :], ACT.Exp).then_inc(s.z_exp, 1)
        e.wait_ge(s.dt_raw, r)
        self.act(m.dt[:, 1, :], m.dt[:, 0, :], ACT.Abs).then_inc(s.dt_abs, 1)
        e.wait_ge(s.dt_abs, r)
        self.act(m.dt[:, 2, :], m.dt[:, 1, :], ACT.Exp, scale=-1.0).then_inc(s.dt_e, 1)
        self.act(m.ahead[:, :], m.wide_("a_log"), ACT.Exp).then_inc(s.a_exp, 1)
        e.wait_ge(s.dt_u, r)
        self.act(m.dt[:, 4, :], m.dt[:, 3, :], ACT.Ln).then_inc(s.dt_ln, 1)
        self.attention("moba", 2)
        e.wait_ge(s.mla_turned, r)
        for b in range(4):
            ins = self.act(m.mla_t[0:QK, 2 * b:2 * b + 2, :], view(ps[0:QK, b, :], a=2), ACT.Copy,
                           scale=QK ** -0.5 if b < 2 else 1.0)
        ins.then_inc(s.mla_kept, 1)
        self.attention("mla", 2)
        e.wait_ge(s.sb_o_kept, r)
        e.wait_ge(s.out_kept, self.p0)
        self.act(m.z1f[:, :].rearrange("p (t c) -> p t c", t=2), m.xn[:, :, 0:768], ACT.Square).then_inc(s.head_sq, 1)
        self.act(m.zs[:, :, :], proj[:, :, C_Z:C_Z + GROUP], ACT.Silu).then_inc(s.z_silu, 1)
        e.wait_ge(s.xh_turned, r)
        self.act(m.xh[:, :, :], view(ps[:, 7, :], a=2), ACT.Copy).then_inc(s.xh_kept, 1)
        e.wait_ge(s.expo, r)
        self.act(m.z0[:, :, :], m.z0[:, :, :], ACT.Exp).then_inc(s.expo_done, 1)
        e.wait_ge(s.y_sum, r)
        for t in range(TT):
            ins = self.act(m.ps[:, 3, t * 256:(t + 1) * 256], m.y[:, t, :], ACT.Square, accum_out=m.ss3[:, t:t + 1])
        ins.then_inc(s.ssm_sq, 1)


class Vector(Program):
    def link(self, ins):
        self.steps_made += 1
        ins.then_inc(self.s.dve_step, 1)
        self.e.wait_ge(self.s.dve_step, self.steps_made)

    def split(self, b, i):
        m, s = self.m, self.s
        c = self.c0 + b + AHEAD
        if isinstance(i, int) and c >= self.total:
            return
        slot = c % RING
        self.at(s.split_hi, c + 1, i, RING)
        self.e.tensor_tensor(m.wlo[:, slot, :], m.raw[:, slot, :], m.whi[:, slot, :].bitcast(F32),
                             ALU.subtract).then_inc(s.split_lo, 1)

    def start(self):
        e, m, s = self.e, self.m, self.s
        e.memset(m.rows[:, ROW_TILES - 1, :], 0.0).then_inc(s.rows_cleared, 1)
        self.link(e.memset(m.xt[:, :, 0:3], 0.0))
        for b in range(-AHEAD, 0):
            self.split(b, 0)
        e.wait_ge(s.params_in, 16)
        e.wait_ge(s.pos_in, 16)
        self.link(e.tensor_copy(m.pos[:, :], m.pos_i[:, :]))
        half = {"64": HD // 2, "32": ROPE // 2}
        at = 0
        for name, n in half.items():
            for quarter in range(2):
                for t in range(TT):
                    ins = e.tensor_scalar(m.ang0[:, at + t * n:at + (t + 1) * n], m.cst("inv" + name), m.pos[:, t:t + 1], None, ALU.mult)
                at += TT * n
        self.link(ins)
        n_all, n_cos = at, None
        magic = 1.5 * 2.0 ** 23
        at = 0
        for name, n in half.items():
            for quarter in range(2):
                w = slice(at, at + TT * n)
                ins = e.tensor_scalar(m.turns[:, w], m.ang0[:, w], 1 / (2 * np.pi), 0.25 * quarter, ALU.mult, ALU.add)
                at += TT * n
        self.link(ins)
        self.link(e.tensor_scalar(m.turns[:, :], m.turns[:, :], magic, -magic, ALU.add, ALU.add))
        rest = 2 * np.pi
        for bits in (8, 8, 8, 24):
            scale = 2.0 ** (bits - 1 - np.floor(np.log2(rest)))
            part = float(np.float32(np.floor(rest * scale) / scale))
            rest -= part
            self.link(e.scalar_tensor_tensor(m.ang0[:, :], m.turns[:, :], -part, m.ang0[:, :], ALU.mult, ALU.add))
        at = 0
        for name, n in half.items():
            w = slice(at + TT * n, at + 2 * TT * n)
            ins = e.tensor_scalar(m.ang0[:, w], m.ang0[:, w], float(np.pi / 2), None, ALU.add)
            at += 2 * TT * n
        self.link(ins)
        lim = 3.1415925
        e.tensor_scalar(m.ang[:, :], m.ang0[:, :], lim, -lim, ALU.min, ALU.max).then_inc(s.angles, 1)
        e.wait_ge(s.ext_in, 16)
        e.tensor_scalar(m.ext[:, 2 * REL + 1:], m.cst("ones")[0:32, 0:127], m.ext[:, 2 * REL:2 * REL + 1], None,
                        ALU.mult).then_inc(s.ext_out, 1)

    def norm(self, gain, kind):
        e, m, s = self.e, self.m, self.s
        r = self.round("norm")
        if kind == "scaled":
            for t in range(TT):
                e.wait_ge(s.rstd, TT * (r - 1) + t + 1)
                for half in range(2):
                    c = slice(half * 512, (half + 1) * 512)
                    e.tensor_scalar(m.xn[:, t, c], m.x[:, t, c], m.rs[:, t:t + 1], None, ALU.mult).then_inc(s.normed, 1)
        self.turn("x", gain, "x")
        if kind == "features":
            for t in range(TT):
                e.wait_ge(s.rstd, TT * (r - 1) + t + 1)
                e.tensor_scalar(m.diag[:, t, :], m.ident, m.rs[:, t:t + 1], None, ALU.mult).then_inc(s.diagonals, 1)

    def take_spread(self):
        self.e.wait_ge(self.s.spread, self.round("spread"))
        self.link(self.e.tensor_copy(self.m.rb[:, :], self.m.ps[:, 3, 0:SEQ]))

    def turn(self, src, gain, ready):
        e, m, s = self.e, self.m, self.s
        r = self.round("turn")
        if r == 1:
            e.wait_ge(s.rows_kept, 1)
        for half in range(2):
            for t in range(TT):
                n = places(ready).index((t, half))
                e.wait_ge(s.hi_turned, 4 * (r - 1) + n + 1)
                tok, ps = slice(t * P, (t + 1) * P), view(m.ps[:, 4 + n, :], a=4)
                if gain is None:
                    f = slice(4 * half, 4 * half + 4)
                    ins = e.tensor_tensor(m.h_lo[:, f, tok], ps, m.h_hi[:, f, tok].bitcast(F32), ALU.subtract)
                else:
                    for k in range(4):
                        f = 4 * half + k
                        ins = e.scalar_tensor_tensor(m.h_lo[:, f, tok], ps[:, k, :], m.cols[:, gain + f:gain + f + 1],
                                                     m.h_hi[:, f, tok].bitcast(F32), ALU.mult, ALU.subtract)
                ins.then_inc(s.features, 1)

    def product_tokens(self, what, l, n, _):
        e, m, s = self.e, self.m, self.s
        post = what in ("a_o", "b_o", "c_o")
        if post:
            r = self.round("o_squares")
            g = self.rounds.get("post", 0) + 1
            e.wait_ge(s.gain_in[g % 2], 16 * ((g + 1) // 2))

        def body(b, i):
            self.split(b, i)
            c = slice(b * 256, (b + 1) * 256)
            ps = view(m.ps[:, self.bank(b), :], a=2)
            if post:
                e.wait_ge(s.o_squares, 4 * (r - 1) + b + 1)
                e.tensor_tensor(m.xn[:, :, c], ps, m.gain[:, g % 2, c].unsqueeze(1).to_broadcast([P, TT, 256]),
                                ALU.mult).then_inc(s.bank_free, 1)
            elif what == "out1":
                e.wait_ge(s.chunk_done, self.c0 + b + 1)
                e.tensor_tensor(m.x[:, :, c], ps, m.x[:, :, c], ALU.add).then_inc(s.bank_free, 1)
        self.steps(n, body, peel=n if what == "in1" or n == 4 else 1)
        self.advance(n)

    def attend_chunk(self, kind, l, c):
        e, m, s = self.e, self.m, self.s
        rb = m.rb[:, :].unsqueeze(1).to_broadcast([P, 2, SEQ])
        for b in range(8):
            if turned_at(b) == c:
                self.weigh(kind, b)
        self.split(c, 0)
        if c == 2:
            e.wait_ge(s.bias_ready, self.round("bias"))
            if kind == "c":
                self.mixing_factor()
        for b in range(0, 8, 2):
            if scores_at(b) == c:
                self.mask(kind, b)
        e.wait_ge(s.chunk_done, self.c0 + c + 1)
        if c == 0:
            self.take_spread()
        j, x = c // 3, c % 3
        if x < 2:
            e.scalar_tensor_tensor(m.qk[:, 8 * x + 2 * j:8 * x + 2 * j + 2, :], view(m.ps[:, self.bank(c), :], a=2),
                                   HD ** -0.5 if x == 0 else 1.0, rb, ALU.mult, ALU.mult).then_inc(s.bank_free, 1)
        else:
            for t in range(TT):
                ins = e.tensor_scalar(m.v[:, t, j * 256:(j + 1) * 256], m.ps[:, self.bank(c), t * 256:(t + 1) * 256],
                                      m.rs[:, t:t + 1], None, ALU.mult)
            ins.then_inc(s.bank_free, 1)

    def attend_pairs(self, kind, c):
        for b in range(8):
            if turned_at(b) == c and c >= 12:
                self.weigh(kind, b)
        for b in range(8):
            if values_at(b) == c:
                self.keep_out(kind, b)
                if b == 5 and kind == "c":
                    self.scale_out(0)
        for b in range(1, 8, 2):
            if scores_at(b) == c:
                self.mask(kind, b)

    def hidden(self, kind, l):
        e, m, s = self.e, self.m, self.s

        def lo(b, i):
            self.at(s.hid_hi, self.f0 + b + 1, i, RING)
            j = b if isinstance(i, int) else i * RING + b
            e.tensor_tensor(m.hid_lo[:, bass.ds(j, 1), :], m.hid[:, b % RING:b % RING + 1, :],
                            m.hid_hi[:, bass.ds(j, 1), :].bitcast(F32), ALU.subtract).then_inc(s.hid_ready, 1)

        def multiply(b, i):
            self.at(s.silu, self.f0 + b + 1, i, RING)
            e.tensor_tensor(m.hid[:, b % RING, :], m.silu[:, b % RING, :], m.u[:, b % RING, 1, :],
                            ALU.mult).then_inc(s.gated, 1)

        def body(b, i):
            j = b if isinstance(i, int) else i * RING + b
            bank = m.ps[:, self.bank(b), :]
            self.split(b, i)
            if kind == "ffn1":
                self.at(s.seeded, self.v0 + b + 1, i, RING)
                for tap in range(2):
                    back = 2 - tap
                    for g in range(2):
                        w = ROWS["ffn_conv_w"] + (l * 3 + tap) * 2 * FT + g * FT
                        u = m.u[:, b % RING, g, back:]
                        ins = e.scalar_tensor_tensor(u, bank[:, g * 256:(g + 1) * 256 - back],
                                                     m.cols[:, bass.ds(j + w, 1)], u, ALU.mult, ALU.add)
                    if tap == 0:
                        ins.then_inc(s.conv_half, 1)
                        self.at(s.conv_half, self.v0 + b + 1, i, RING)
                ins.then_inc(s.bank_free, 1)
            else:
                self.at(s.chunk_done, self.c0 + b + 1, i, RING)
                if b == 0:
                    self.take_spread()
                self.gated(b - RING, i)
                e.tensor_tensor(m.u[:, b % RING, :, :], view(bank, a=2), m.rb[:, :].unsqueeze(1).to_broadcast([P, 2, SEQ]),
                                ALU.mult).then_inc(s.bank_free, 1)
            if b > 0:
                self.at(s.bank_free, self.b0 + b + 1, i, RING)
                multiply(b - 1, i)
            if b > 1:
                lo(b - 2, i)
        self.steps(FT, body, peel=4)
        multiply(FT - 1, 0)
        lo(FT - 2, 0)
        lo(FT - 1, 0)
        self.after_hidden(kind)

    def down(self, kind, l):
        self.round("down")
        for b in range(FT // 2):
            self.split(b, 0)
        self.advance(FT // 2, banks=False)
    def post_norm(self, source, weight):
        e, m, s = self.e, self.m, self.s
        r = self.round("post") if weight is not None else 0
        q = self.round("post_psum") if weight is not None and source == "psum" else 0
        if q:
            e.wait_ge(s.gain_in[r % 2], 16 * ((r + 1) // 2))
        for t in range(TT if source != "chunks" else 0):
            if source == "psum" and weight is None:
                if t == 0:
                    e.wait_ge(s.first_tile, self.rounds["down"])
                else:
                    e.wait_ge(s.chunk_done, self.c0)
                for half in range(2):
                    c = slice(half * 512, (half + 1) * 512)
                    e.tensor_tensor(m.x[:, t, c], m.ps[:, 4 + 2 * t + half, :], m.x[:, t, c], ALU.add).then_inc(s.residual, 1)
                continue
            if q:
                for half in range(2):
                    c = slice(half * 512, (half + 1) * 512)
                    e.wait_ge(s.m_squares, 4 * (q - 1) + 2 * t + half + 1)
                    ins = e.scalar_tensor_tensor(m.xn[:, t, c], m.ps[:, 4 + 2 * t + half, :], weight, m.gain[:, r % 2, c],
                                                 ALU.mult, ALU.mult)
                self.link(ins)
            elif t == 0:
                e.wait_ge(s.bank_free, self.b0)
            e.wait_ge(s.m_rstd, TT * (r - 1) + t + 1)
            for half in range(2):
                c = slice(half * 512, (half + 1) * 512)
                e.scalar_tensor_tensor(m.x[:, t, c], m.xn[:, t, c], m.rs2[:, t:t + 1], m.x[:, t, c], ALU.mult,
                                       ALU.add).then_inc(s.residual, 1)
        self.renewed(source)

    def bias_tables(self, kind, l): pass

    def mixing_factor(self):
        e, m, s = self.e, self.m, self.s
        r = self.round("lam")
        e.wait_ge(s.lam_in, 32 * r)
        for j in range(2):
            ins = e.tensor_tensor_reduce(m.lam_x[:, j * 64:(j + 1) * 64], m.lam[:, 2 * j, :], m.lam[:, 2 * j + 1, :], 1.0, 0.0,
                                         ALU.mult, ALU.add, m.lam_d[:, j:j + 1])
        ins.then_inc(s.lam_dots, 1)
        e.wait_ge(s.lam_exps, r)
        self.link(e.tensor_tensor(m.lam_d[:, 2:3], m.lam_d[:, 0:1], m.lam_d[:, 1:2], ALU.subtract))
        self.link(e.tensor_scalar(m.lam_d[:, 3:4], m.lam_d[:, 2:3], -1.0, -LAMBDA_INIT, ALU.mult, ALU.add))

    def mask(self, kind, b):
        e, m, s, par = self.e, self.m, self.s, b % 2
        self.at(s.scores, self.p0 + b + 1)
        self.at(s.probs_turned, self.p0 + b - 1)
        for h in range(2):
            sc, out = m.ps[:, m.score_bank[kind] + h, 0:3 * P], m.prob[:, par, h, :]
            if kind in ("a", "c"):
                tab = m.bias[:, b * 2 + h, :] if kind == "a" else m.bias[:, b, :]
                e.tensor_tensor(out[:, 0:P], sc[:, 0:P], tab[:, 0:P][:, ::-1], ALU.add)
                ins = e.tensor_tensor(out[:, P:], sc[:, P:], tab[:, ::-1], ALU.add)
            else:
                ins = e.tensor_tensor(out, sc, m.cst("causal"), ALU.add)
        ins.then_inc(s.masked, 1)
        self.at(s.masked, self.p0 + b + 1)
        e.tensor_reduce(m.negmax[:, par, :, 0:1], m.prob[:, par, :, 0:P], AX, ALU.max, negate=True)
        e.tensor_reduce(m.negmax[:, par, :, 1:2], m.prob[:, par, :, P:], AX, ALU.max, negate=True).then_inc(s.maxed, 1)

    def weigh(self, kind, b):
        e, m, s, par = self.e, self.m, self.s, b % 2
        self.at(s.exps, self.p0 + b + 1)
        e.reciprocal(m.rsum[:, par, 0:4], m.sums[:, par, :, :].rearrange("p h t -> p (h t)")).then_inc(s.recips, 1)
        if kind != "c":
            return
        self.at(s.recips, self.p0 + b + 1)
        e.tensor_scalar(m.rsum[:, par, 4:6], m.rsum[:, par, 2:4], m.lam_d[:, 3:4], None, ALU.mult)
        for t, cols in ((0, slice(0, P)), (1, slice(P, 3 * P))):
            ins = e.tensor_scalar(m.prob[:, par, 0, cols], m.prob[:, par, 0, cols], m.rsum[:, par, t:t + 1], None, ALU.mult)
        ins.then_inc(s.weighed, 1)
        self.at(s.weighed, self.m0 + b + 1)
        for t, cols in ((0, slice(0, P)), (1, slice(P, 3 * P))):
            ins = e.scalar_tensor_tensor(m.prob[:, par, 0, cols], m.prob[:, par, 1, cols], m.rsum[:, par, 4 + t:5 + t],
                                         m.prob[:, par, 0, cols], ALU.mult, ALU.add)
        ins.then_inc(s.mixed, 1)

    def keep_out(self, kind, b):
        e, m, s, par = self.e, self.m, self.s, b % 2
        self.at(s.pair_out, self.p0 + b + 1)
        self.at(s.recips, self.p0 + b + 1)
        base = 256 if kind == "mla" else 0
        out = m.xn[:, :, b * P + base:(b + 1) * P + base]
        acc = view(m.ps[:, m.out_bank[kind], 0:SEQ], a=2)
        if kind == "c":
            self.at(s.sub_sq, self.m0 + b + 1)
            e.scalar_tensor_tensor(out, acc, 1.0 - LAMBDA_INIT, m.sub_g[:, :].unsqueeze(1).to_broadcast([P, TT, P]), ALU.mult,
                                   ALU.mult).then_inc(s.out_kept, 1)
        else:
            r = m.rsum[:, par, 0:4].rearrange("p (h t) -> p t h", t=2).unsqueeze(3).to_broadcast([P, 2, 2, HD])
            e.tensor_tensor(out.rearrange("p t (h c) -> p t h c", h=2), acc.rearrange("p t (h c) -> p t h c", h=2), r,
                            ALU.mult).then_inc(s.out_kept, 1)

    def attention(self, kind, n):
        self.mask(kind, 0)
        for b in range(n):
            if b < n - 1:
                self.mask(kind, b + 1)
            self.weigh(kind, b)
            self.keep_out(kind, b)
        self.p0 += n

    def rms(self, src, heads, width, st, ready, rstd, r):
        e, m = self.e, self.m
        self.link(e.tensor_reduce(m.st[:, st:st + heads], src, AX, ALU.add))
        e.tensor_scalar(m.st[:, st:st + heads], m.st[:, st:st + heads], 1.0 / width, EPS, ALU.mult, ALU.add).then_inc(ready, 1)
        e.wait_ge(rstd, r)

    def scale_out(self, half):
        e, m, s = self.e, self.m, self.s
        e.wait_ge(s.sub_rstd, self.round("sub"))
        self.at(s.out_kept, self.p0 + 4 * half + 4)
        for t in range(TT):
            v = m.xn[:, t, half * 512:(half + 1) * 512].rearrange("p (h c) -> p h c", h=4)
            at = 8 * half + 4 * t
            e.tensor_tensor(v, v, m.st[:, at:at + 4].unsqueeze(2).to_broadcast([P, 4, P]), ALU.mult).then_inc(s.attended, 1)

    def sub_norm(self, i):
        self.p0 -= 8
        self.scale_out(1)
        self.p0 += 8

    def gmlp(self, l):
        e, m, s = self.e, self.m, self.s
        r = self.round("gmlp")
        e.wait_ge(s.bank_free, self.b0)
        self.link(e.tensor_reduce(m.st[:, 0:2], m.b_uv[:, :, D:2 * D], AX, ALU.add))
        self.link(e.tensor_scalar(m.st[:, 0:2], m.st[:, 0:2], 1.0 / D, None, ALU.mult))
        for t in range(TT):
            ins = e.tensor_scalar(m.b_v[:, t, :], m.b_v[:, t, :], m.st[:, t:t + 1], None, ALU.subtract)
        ins.then_inc(s.ln_centred, 1)
        e.wait_ge(s.bw_turned, r)
        for g in range(2):
            e.tensor_tensor(m.b_wt[:, 4 * g:4 * g + 4, :], view(m.ps[:, 4 + g, :], a=4),
                            m.cst("upto").unsqueeze(1).to_broadcast([P, 4, P]), ALU.mult).then_inc(s.bw_kept, 1)
        e.wait_ge(s.ln_squares, r)
        e.tensor_scalar(m.st[:, 2:4], m.ss3[:, :], 1.0 / D, EPS, ALU.mult, ALU.add).then_inc(s.ln_ms, 1)
        e.wait_ge(s.ln_rstd, r)
        e.wait_ge(s.b_rows_in, 32 * r)
        for t in range(TT):
            self.link(e.scalar_tensor_tensor(m.b_v[:, t, :], m.b_v[:, t, :], m.st[:, 4 + t:5 + t], m.b_rows[:, 0, :], ALU.mult, ALU.mult))
            ins = e.tensor_tensor(m.b_v[:, t, :], m.b_v[:, t, :], m.b_rows[:, 1, :], ALU.add)
        ins.then_inc(s.v_normed, 1)
        e.wait_ge(s.gated_sums, r)
        for t in range(TT):
            for g in range(8):
                c = slice(g * P, (g + 1) * P)
                ins = e.scalar_tensor_tensor(m.xn[:, t, c], m.ps[:, 2 * t + g // 4, (g % 4) * P:(g % 4 + 1) * P],
                                             m.cols[:, ROWS["b_b_s"] + g:ROWS["b_b_s"] + g + 1], m.b_uv[:, t, c], ALU.add, ALU.mult)
        ins.then_inc(s.b_y, 1)

    def rope(self, src, dst, tmp, kind, n):
        e, m = self.e, self.m
        at = {"64": 0, "32": 4 * HD // 2}[kind]
        sin, cos = (m.trig[:, at + q * 2 * n:at + (q + 1) * 2 * n].rearrange("p (t c) -> p t c", t=2).unsqueeze(2)
                    .to_broadcast([P, 2, 8, n]) for q in range(2))
        x1, x2 = src[:, :, :, 0:n], src[:, :, :, n:2 * n]
        w = 2 * 8 * n
        t = [tmp[:, q * w:(q + 1) * w].rearrange("p (t h c) -> p t h c", t=2, h=8) for q in range(4)]
        e.tensor_tensor(t[0], x1, cos, ALU.mult)
        e.tensor_tensor(t[1], x2, sin, ALU.mult)
        e.tensor_tensor(t[2], x1, sin, ALU.mult)
        self.link(e.tensor_tensor(t[3], x2, cos, ALU.mult))
        e.tensor_tensor(dst[:, :, :, 0:n], t[0], t[1], ALU.subtract)
        return e.tensor_tensor(dst[:, :, :, n:2 * n], t[2], t[3], ALU.add)

    def mixers(self, l):
        e, m, s = self.e, self.m, self.s
        r = self.round("mixers")
        ps, proj = m.ps, m.proj

        def four(ap, h=8):
            return ap.rearrange("p t (h c) -> p t h c", h=h)

        def gains(ap, h, w):
            return ap.unsqueeze(1).unsqueeze(1).to_broadcast([P, 2, h, w])
        e.wait_ge(s.bank_free, self.b0)
        e.wait_ge(s.wide_in, 16 * len(WIDE) * r)
        e.wait_ge(s.moba_sq, r)
        e.tensor_reduce(m.st[:, 0:16], m.z0f[:, 0:1024].rearrange("p (h c) -> p h c", c=HD), AX, ALU.add)
        e.wait_ge(s.c_sq, r)
        csq = m.z1f[:, 0:640].rearrange("p (t c) -> p t c", t=2)
        e.tensor_reduce(m.st[:, 16:18], csq[:, :, 0:QR], AX, ALU.add)
        self.link(e.tensor_reduce(m.st[:, 18:20], csq[:, :, QR:QR + KVR], AX, ALU.add))
        e.tensor_scalar(m.st[:, 0:16], m.st[:, 0:16], 1.0 / HD, EPS, ALU.mult, ALU.add)
        e.tensor_scalar(m.st[:, 16:18], m.st[:, 16:18], 1.0 / QR, EPS, ALU.mult, ALU.add)
        e.tensor_scalar(m.st[:, 18:20], m.st[:, 18:20], 1.0 / KVR, EPS, ALU.mult, ALU.add).then_inc(s.c_ms, 1)
        e.wait_ge(s.c_rstd, r)
        for at, col, w, g in ((16, 0, QR, "q_norm"), (18, QR, KVR, "kv_norm")):
            for t in range(TT):
                ins = e.scalar_tensor_tensor(m.cn[:, t, col:col + w], proj[:, t, C_CQ + col:C_CQ + col + w],
                                             m.st[:, at + t:at + t + 1], m.wide_(g), ALU.mult, ALU.mult)
        ins.then_inc(s.c_ready, 1)
        q0 = m.z0f[:, 0:1024].rearrange("p (t h c) -> p t h c", t=2, h=8)
        self.link(e.tensor_tensor(q0, four(proj[:, :, 0:512]),
                                  m.st[:, 0:16].rearrange("p (t h) -> p t h", t=2).unsqueeze(3).to_broadcast([P, 2, 8, HD]), ALU.mult))
        for x in range(2):
            ins = e.tensor_tensor(q0[:, :, 4 * x:4 * x + 4, :], q0[:, :, 4 * x:4 * x + 4, :],
                                  gains(m.wide_("moba_g")[:, x * HD:(x + 1) * HD], 4, HD), ALU.mult)
        self.link(ins)
        self.rope(q0, four(m.qk_rot[:, :, :]), m.rope_tmp, "64", HD // 2).then_inc(s.moba_ready, 1)
        e.tensor_tensor(m.dt[:, 0, :].rearrange("p (t h) -> p t h", t=2), proj[:, :, C_DT:C_DT + 4],
                        m.wide_("dt_bias").unsqueeze(1).to_broadcast([P, 2, 4]), ALU.add).then_inc(s.dt_raw, 1)
        e.wait_ge(s.xbc_kept, r)
        for tap in (3, 2, 1, 0):
            for j in range(4):
                w = ROWS["ssm_conv_w"] + (l * 4 + tap) * 4 + j
                wc = m.cols[:, w:w + 1]
                if tap == 3:
                    bias = ROWS["ssm_conv_b"] + l * 4 + j
                    ins = e.tensor_scalar(m.conv[:, j, :], m.xt[:, j, 3:3 + SEQ], wc, m.cols[:, bias:bias + 1], ALU.mult, ALU.add)
                else:
                    ins = e.scalar_tensor_tensor(m.conv[:, j, :], m.xt[:, j, tap:tap + SEQ], wc, m.conv[:, j, :], ALU.mult, ALU.add)
            if tap:
                self.link(ins)
            else:
                ins.then_inc(s.convd, 1)
        e.wait_ge(s.mla_sq, r)
        self.rms(m.z1f[:, :].rearrange("p (h c) -> p h c", c=QK), 16, QK, 20, s.mla_ms, s.mla_rstd, r)
        qk = m.qk96[:, :, :, :]
        self.link(e.tensor_tensor(qk, qk, m.st[:, 20:36].rearrange("p (t h) -> p t h", t=2).unsqueeze(3).to_broadcast([P, 2, 8, QK]), ALU.mult))
        for x in range(2):
            ins = e.tensor_tensor(qk[:, :, 4 * x:4 * x + 4, :], qk[:, :, 4 * x:4 * x + 4, :],
                                  gains(m.wide_("qk_g")[:, x * QK:(x + 1) * QK], 4, QK), ALU.mult)
        self.link(ins)
        self.rope(qk[:, :, :, NOPE:], qk[:, :, :, NOPE:], m.rope_tmp, "32", ROPE // 2).then_inc(s.mla_ready, 1)
        z, strict = ps[:, 0:4, 0:3 * P], m.cst("strict").unsqueeze(1).to_broadcast([P, 4, 3 * P])
        e.wait_ge(s.z_ln, r)
        self.link(e.scalar_tensor_tensor(m.z1[:, :, :], z, 0.0, m.z0[:, :, :], ALU.min, ALU.subtract))
        self.link(e.tensor_tensor(m.z0[:, :, :], m.z1[:, :, :], z, ALU.subtract))
        e.tensor_tensor(m.z0[:, :, :], m.z0[:, :, :], strict, ALU.mult).then_inc(s.z_l, 1)
        e.wait_ge(s.tail_done, r)
        e.tensor_tensor(m.z1[:, :, :], m.z1[:, :, :], ps[:, 4:8, 0:3 * P], ALU.add).then_inc(s.z_arg, 1)
        e.wait_ge(s.dt_e, r)
        e.tensor_scalar(m.dt[:, 3, :], m.dt[:, 2, :], 1.0, None, ALU.add).then_inc(s.dt_u, 1)
        tiny = 1e-20
        e.wait_ge(s.dt_ln, r)
        e.scalar_tensor_tensor(m.dt[:, 5, :], m.dt[:, 4, :], tiny, m.dt[:, 2, :], ALU.add, ALU.mult)
        self.link(e.tensor_scalar(m.dt[:, 6, :], m.dt[:, 3, :], -1.0, tiny, ALU.add, ALU.add))
        self.link(e.reciprocal(m.dt[:, 7, :], m.dt[:, 6, :]))
        self.link(e.tensor_tensor(m.dt[:, 5, :], m.dt[:, 5, :], m.dt[:, 7, :], ALU.mult))
        self.link(e.scalar_tensor_tensor(m.dt[:, 1, :], m.dt[:, 0, :], 0.0, m.dt[:, 5, :], ALU.max, ALU.add))
        e.scalar_tensor_tensor(m.a[:, :, :], m.dt[:, 1, :].rearrange("p (t h) -> p t h", t=2), -1.0,
                               m.ahead[:, :].unsqueeze(1).to_broadcast([P, 2, 4]), ALU.mult, ALU.mult).then_inc(s.a_ready, 1)
        e.wait_ge(s.z_exp, r)
        e.tensor_tensor(m.z1[:, :, :], m.z1[:, :, :], strict, ALU.mult).then_inc(s.sb_a, 1)
        e.wait_ge(s.sb_o, r)
        e.tensor_copy(m.xn[:, :, 512:768], view(ps[:, 0, :], a=2)).then_inc(s.sb_o_kept, 1)
        self.attention("moba", 2)
        self.attention("mla", 2)
        e.wait_ge(s.xh_kept, r)

        def wide4(ap):
            return ap.rearrange("p (t h) -> p t h", t=2).unsqueeze(3).to_broadcast([P, 2, 4, HD])
        e.tensor_tensor(four(m.xdt[:, :, :], 4), four(m.xh[:, :, :], 4), wide4(m.dt[:, 1, :]), ALU.mult)
        e.tensor_tensor(four(m.y[:, :, :], 4), four(m.xh[:, :, :], 4), gains(m.wide_("ssm_d"), 1, 4).rearrange("p t o h -> p t (o h)")
                        .unsqueeze(3).to_broadcast([P, 2, 4, HD]), ALU.mult)
        e.wait_ge(s.cum_done, r)
        self.link(e.tensor_scalar(m.neg[:, 0:8], ps[:, 4, 256:264], -1.0, None, ALU.mult))
        self.link(e.tensor_tensor(m.neg[:, 8:12], ps[:, 5, P - 1::P], m.neg[:, 0:4], ALU.add))
        for h in range(4):
            row = [ps[:, 5 + t, h * P:(h + 1) * P] for t in range(TT)]
            e.scalar_tensor_tensor(m.z0[:, h, 0:P], row[0], m.neg[:, h:h + 1], m.cst("upto_add"), ALU.add, ALU.add)
            e.tensor_scalar(m.z0[:, h, P:2 * P], row[1], m.neg[:, 8 + h:9 + h], None, ALU.add)
            ins = e.scalar_tensor_tensor(m.z0[:, h, 2 * P:], row[1], m.neg[:, 4 + h:5 + h], m.cst("upto_add"), ALU.add, ALU.add)
        ins.then_inc(s.expo, 1)
        e.wait_ge(s.head_sq, r)
        self.rms(m.z1f[:, :].rearrange("p (h c) -> p h c", c=HD), 24, HD, 36, s.head_ms, s.head_rstd, r)
        o = four(m.xn[:, :, 0:768], 12)
        self.link(e.tensor_tensor(o, o, m.st[:, 36:60].rearrange("p (t h) -> p t h", t=2).unsqueeze(3).to_broadcast([P, 2, 12, HD]), ALU.mult))
        e.tensor_tensor(m.xn[:, :, 0:768], m.xn[:, :, 0:768], m.wide_("head_g").unsqueeze(1).to_broadcast([P, 2, 768]), ALU.mult).then_inc(s.heads_ready, 1)
        e.wait_ge(s.expo_done, r)
        e.wait_ge(s.gram_done, r)
        for g in range(2):
            w = m.z0[:, 2 * g:2 * g + 2, :]
            ins = e.tensor_tensor(w, w, ps[:, g, 0:3 * P].unsqueeze(1).to_broadcast([P, 2, 3 * P]), ALU.mult)
        ins.then_inc(s.w_ready, 1)
        e.wait_ge(s.ssm_y, r)
        self.link(e.tensor_tensor(m.y[:, :, :], m.y[:, :, :], view(ps[:, 2, :], a=2), ALU.add))
        e.wait_ge(s.z_silu, r)
        e.tensor_tensor(m.y[:, :, :], m.y[:, :, :], m.zs[:, :, :], ALU.mult).then_inc(s.y_sum, 1)
        e.wait_ge(s.ssm_sq, r)
        e.tensor_scalar(m.ms2[:, 0:2], m.ss3[:, :], 1.0 / GROUP, EPS, ALU.mult, ALU.add).then_inc(s.ssm_ms, 1)
        e.wait_ge(s.ssm_rstd, r)
        for t in range(TT):
            ins = e.scalar_tensor_tensor(m.xn[:, t, 768:D], m.y[:, t, :], m.rs2[:, t:t + 1], m.wide_("ssm_norm"), ALU.mult, ALU.mult)
        ins.then_inc(s.heads_ready, 1)


class Pool(Program):

    def power(self, out, in_, n):
        return self.e.tensor_tensor(out, in_, self.m.cst("minus_half")[:, 0:n], ALU.pow)

    def row(self, dst, src):
        return self.e.dma_start(dst, src.unsqueeze(0).to_broadcast([P] + list(src.shape)))

    def start(self):
        e, m, s, d = self.e, self.m, self.s, self.d
        e.dma_start(m.ext[:, 0:2 * REL + 1], d.a_rel_bias.rearrange("l h c -> (l h) c")).then_inc(s.ext_in, 16)
        self.layer_rows(0)
        e.wait_ge(s.ext_out, 1)
        e.dma_start(d.ext_dram, m.ext[:, :]).then_inc(s.ext_stored, 16)
        e.wait_ge(s.ext_stored, 16)

    def layer_rows(self, l):
        m, s, d = self.m, self.s, self.d
        src = {"moba_g": d.moba_qk_g[l].rearrange("a c -> (a c)"), "q_norm": d.mla_q_norm_g[l], "kv_norm": d.mla_kv_norm_g[l],
               "qk_g": d.mla_qk_g[l].rearrange("a c -> (a c)"), "dt_bias": d.ssm_dt_bias[l], "a_log": d.ssm_a_log[l],
               "ssm_d": d.ssm_d[l], "ssm_norm": d.ssm_norm_g[l], "head_g": d.head_out_g[l].rearrange("a h c -> (a h c)")}
        for name in WIDE:
            self.row(m.wide_(name), src[name]).then_inc(s.wide_in, 16)
        self.e.dma_start(m.w_uq[:, 0, :], d.mla_w_uq[l][0:P, :]).then_inc(s.w_in_small, 16)
        self.e.dma_start(m.w_uq[0:QR - P, 1, :], d.mla_w_uq[l][P:QR, :]).then_inc(s.w_in_small, 16)
        self.e.dma_start(m.w_ukv[:, :], d.mla_w_ukv[l]).then_inc(s.w_in_small, 16)

    def load_gain(self, layer, which):
        k = len(self.gains)
        self.gains.append(None)
        if k >= 2:
            self.e.wait_ge(self.s.residual, self.gains[k - 2])
        self.row(self.m.gain[:, (k + 1) % 2, :], self.d.norm_g[layer][which]).then_inc(self.s.gain_in[(k + 1) % 2], 16)

    def norm(self, gain, kind):
        s, m = self.s, self.m
        r = self.round("norm")
        if r == 1:
            self.e.wait_ge(s.params_in, 16)
        for t in range(TT):
            self.e.wait_ge(s.squares, TT * (r - 1) + t + 1)
            self.link(self.e.tensor_scalar(m.ms[:, t:t + 1], m.ss[:, t:t + 1], EPS, None, ALU.add))
            self.power(m.rs[:, t:t + 1], m.ms[:, t:t + 1], 1).then_inc(s.rstd, 1)

    def link(self, ins):
        self.steps_made += 1
        ins.then_inc(self.s.pool_step, 1)
        self.e.wait_ge(self.s.pool_step, self.steps_made)

    def post_norm(self, source, weight):
        e, m, s = self.e, self.m, self.s
        self.renewed(source)
        if weight is None:
            return
        r = self.round("post")
        self.gains[r - 1] = self.res
        if r == 1:
            e.wait_ge(s.params_in, 16)
        if source == "product":
            e.wait_ge(s.o_squares, 4 * self.round("o_squares"))
            self.link(e.tensor_tensor(m.ss2[:, :, 0:2], m.ss2[:, :, 0:2], m.ss2[:, :, 2:4], ALU.add))
        else:
            q = self.round("post_psum")
        for t in range(TT):
            if source == "psum":
                e.wait_ge(s.m_squares, 4 * (q - 1) + 2 * t + 2)
            self.link(e.tensor_tensor(m.ms2[:, t:t + 1], m.ss2[:, t, 0:1], m.ss2[:, t, 1:2], ALU.add))
            self.link(e.tensor_scalar(m.ms2[:, t:t + 1], m.ms2[:, t:t + 1], EPS, None, ALU.add))
            self.power(m.rs2[:, t:t + 1], m.ms2[:, t:t + 1], 1).then_inc(s.m_rstd, 1)

    def product_tokens(self, what, l, n, _): self.advance(n)
    def attend_chunk(self, kind, l, c): pass

    def attend_pairs(self, kind, c):
        e, m, s = self.e, self.m, self.s
        for half in range(2):
            if kind == "c" and c == values_at(4 * half + 3):
                e.wait_ge(s.sub_sq, self.m0 + 4 * half + 4)
                st = m.st[:, 8 * half:8 * half + 8]
                self.link(e.tensor_scalar(st, st, 0.5, EPS, ALU.mult, ALU.add))
                self.power(st, st, 8).then_inc(s.sub_rstd, 1)

    def hidden(self, kind, l):
        self.after_hidden(kind)

    def down(self, kind, l):
        self.advance(FT // 2, banks=False)

    def bias_tables(self, kind, l):
        e, m, s, d = self.e, self.m, self.s, self.d
        r = self.round("bias")
        e.wait_ge(s.chunk_done, self.c0)
        if kind == "a":
            w = 3 * P
            for part in range(4):
                src = bass.AP(d.ext_dram.tensor, (l * 16 + part * 4) * w + 1, [[1, P], [w, 4], [1, SEQ]])
                e.dma_start(m.bias[:, part * 4:part * 4 + 4, :], src).then_inc(s.bias_in, 16)
            self.bias_loads = self.round("bias_a") * 64
            e.wait_ge(s.bias_in, self.bias_loads)
            n = 16
        else:
            n = 8
            e.dma_start(m.dist[:, :], d.consts[:, CONST["dist"][0]:CONST["dist"][1]]).then_inc(s.dist_in, 16)
            e.wait_ge(s.dist_in, 16)
            for h in range(n):
                ins = e.tensor_scalar(m.bias[:, h, :], m.dist[:, :], 2.0 ** (-8.0 * (h + 1) / 8), 0.0, ALU.mult, ALU.add)
            self.link(ins)
            self.row(m.lam[:, :, :], d.c_lambda[l]).then_inc(s.lam_in, 16)
            self.row(m.sub_g[:, :], d.c_subln_g[l]).then_inc(s.lam_in, 16)
        e.memset(m.bias[0:CHUNK, 0:n, 0:CHUNK], BIG).then_inc(s.bias_ready, 1)

    def attention(self, kind, n): pass

    def sub_norm(self, i): pass

    def gmlp(self, l):
        e, m, s, d = self.e, self.m, self.s, self.d
        r = self.round("gmlp")
        e.wait_ge(s.chunk_done, self.c0 - 8)
        e.dma_start(m.b_w[:, :, :], d.b_w_s[l].rearrange("g t s -> t g s")).then_inc(s.bw_in, 16)
        self.row(m.b_rows[:, 0, :], d.b_ln_g[l]).then_inc(s.b_rows_in, 16)
        self.row(m.b_rows[:, 1, :], d.b_ln_b[l]).then_inc(s.b_rows_in, 16)
        e.wait_ge(s.ln_ms, r)
        self.power(m.st[:, 4:6], m.st[:, 2:4], 2).then_inc(s.ln_rstd, 1)

    def mixers(self, l):
        e, m, s = self.e, self.m, self.s
        r = self.round("mixers")
        e.wait_ge(s.c_ms, r)
        self.power(m.st[:, 0:20], m.st[:, 0:20], 20).then_inc(s.c_rstd, 1)
        e.wait_ge(s.mla_ms, r)
        self.power(m.st[:, 20:36], m.st[:, 20:36], 16).then_inc(s.mla_rstd, 1)
        e.wait_ge(s.head_ms, r)
        self.power(m.st[:, 36:60], m.st[:, 36:60], 24).then_inc(s.head_rstd, 1)
        e.wait_ge(s.ssm_ms, r)
        self.power(m.rs2[:, :], m.ms2[:, :], 2).then_inc(s.ssm_rstd, 1)
        e.wait_ge(s.heads_ready, 2 * r)
        if l == 0:
            self.layer_rows(1)


LAMBDA_INIT = 0.8 - 0.6 * float(np.exp(-0.3 * 2))


def row_pieces():
    out = []
    for name, n in _rows:
        done = 0
        while done < n:
            at = ROWS[name] + done
            k = min(n - done, P - at % P)
            out.append((name, done, done + k, at // P, at % P))
            done += k
    return out


def chunks_of(stage):
    if stage[0] == "mix1":
        return -(-IN // 256) + 4
    if stage[0] == "mix2":
        return 12 if stage[1] % 3 == 1 else 16
    return FT + FT // 2


class Dram:

    def __init__(self, t):
        self.x = t["x"]
        self.positions = t["positions"]
        self.mix_norm_g = t["mix_norm_g"]
        self.w_in = t["w_in"]
        self.moba_qk_g = t["moba_qk_g"]
        self.mla_q_norm_g = t["mla_q_norm_g"]
        self.mla_kv_norm_g = t["mla_kv_norm_g"]
        self.mla_w_uq = t["mla_w_uq"]
        self.mla_w_ukv = t["mla_w_ukv"]
        self.mla_qk_g = t["mla_qk_g"]
        self.ssm_conv_w = t["ssm_conv_w"]
        self.ssm_conv_b = t["ssm_conv_b"]
        self.ssm_dt_bias = t["ssm_dt_bias"]
        self.ssm_a_log = t["ssm_a_log"]
        self.ssm_d = t["ssm_d"]
        self.ssm_norm_g = t["ssm_norm_g"]
        self.head_out_g = t["head_out_g"]
        self.w_out = t["w_out"]
        self.ffn_norm_g = t["ffn_norm_g"]
        self.ffn_w_in = t["ffn_w_in"]
        self.ffn_conv_w = t["ffn_conv_w"]
        self.ffn_conv_b = t["ffn_conv_b"]
        self.ffn_w_out = t["ffn_w_out"]
        self.norm_g = t["norm_g_2"]
        self.ff1_w_in = t["ff1_w_in_2"]
        self.ff1_w_out = t["ff1_w_out_2"]
        self.ff2_w_in = t["ff2_w_in_2"]
        self.ff2_w_out = t["ff2_w_out_2"]
        self.a_w_qkv = t["a_w_qkv_2"]
        self.a_rel_bias = t["a_rel_bias_2"]
        self.a_w_o = t["a_w_o_2"]
        self.b_w_in = t["b_w_in_2"]
        self.b_ln_g = t["b_ln_g_2"]
        self.b_ln_b = t["b_ln_b_2"]
        self.b_w_s = t["b_w_s_2"]
        self.b_b_s = t["b_b_s_2"]
        self.b_w_o = t["b_w_o_2"]
        self.c_w_qkv = t["c_w_qkv_2"]
        self.c_lambda = t["c_lambda_2"]
        self.c_subln_g = t["c_subln_g_2"]
        self.c_w_o = t["c_w_o_2"]
        self.consts = t["consts"]
        self.out = t["out"]
        self.ext_dram = t["ext_dram"]


def build(nc, d):
    with ExitStack() as ctx:
        m = Memory()

        def sb(stack, name, shape, dt=F32):
            return stack.enter_context(nc.sbuf_tensor(name, shape, dt))

        m.raw = sb(ctx, "raw", [P, RING, CW])
        m.whi = sb(ctx, "whi", [P, RING, CW], F32R)
        m.wlo = sb(ctx, "wlo", [P, RING, CW], F32R)
        m.x = sb(ctx, "x", [P, TT, D])
        m.xn = sb(ctx, "xn", [P, TT, D])
        m.consts = sb(ctx, "consts", [P, CONST["dist"][0]])
        m.cols = sb(ctx, "cols", [P, ROW_TILES * P])
        m.trig = sb(ctx, "trig", [P, 192])
        m.ss = sb(ctx, "ss", [P, 2])
        m.ms = sb(ctx, "ms", [P, 2])
        m.rs = sb(ctx, "rs", [P, 2])
        m.ss2 = sb(ctx, "ss2", [P, 2, 4])
        m.ss3 = sb(ctx, "ss3", [P, 2])
        m.rb = sb(ctx, "rb", [P, SEQ])
        m.ms2 = sb(ctx, "ms2", [P, 2])
        m.rs2 = sb(ctx, "rs2", [P, 2])
        m.st = sb(ctx, "st", [P, 60])
        m.lam_d = sb(ctx, "lam_d", [P, 4])
        m.neg = sb(ctx, "neg", [P, 12])
        m.ahead = sb(ctx, "ahead", [P, 4])
        m.pos = sb(ctx, "pos", [P, 2])
        m.pos_i = sb(ctx, "pos_i", [P, 2], I32)
        m.negmax = sb(ctx, "negmax", [P, 2, 2, 2])
        m.sums = sb(ctx, "sums", [P, 2, 2, 2])
        m.rsum = sb(ctx, "rsum", [P, 2, 6])
        m.dt = sb(ctx, "dt", [P, 8, 8])
        m.a = sb(ctx, "a", [P, TT, 4])

        def shared(name, *layouts):
            size, made = 0, []
            for layout in layouts:
                with ExitStack() as inner:
                    used = 0
                    for args in layout:
                        made.append(sb(inner, *args))
                        used += int(np.prod(args[1][1:])) * 4
                    size = max(size, used)
            sb(ctx, name, [P, size // 4])
            return made

        (m.h_hi, m.h_lo, m.qk_rot, m.sb_t, m.moba_t, m.cn) = shared(
            "mem_features",
            [("h_hi", [P, KT, SEQ], F32R), ("h_lo", [P, KT, SEQ], F32R)],
            [("qk_rot", [P, TT, 512]), ("sb_t", [P, 4, SEQ]), ("moba_t", [P, 4, SEQ]), ("cn", [P, TT, QR + KVR])])
        (m.hid_hi, m.hid_lo, m.proj, m.z0, m.z1, m.mla_t, m.xh, m.qk, m.v, m.bias, m.b_uv, m.b_w, m.b_wt, m.b_rows) = shared(
            "mem_hidden",
            [("hid_hi", [P, FT, SEQ], F32R), ("hid_lo", [P, FT, SEQ], F32R)],
            [("proj", [P, TT, IN]), ("z0", [P, 4, 3 * P]), ("z1", [P, 4, 3 * P]), ("mla_t", [P, 8, SEQ]), ("xh", [P, TT, GROUP])],
            [("qk", [P, 16, SEQ]), ("v", [P, TT, D]), ("bias", [P, 16, SEQ])],
            [("b_uv", [P, TT, 2 * D]), ("b_w", [P, 8, P]), ("b_wt", [P, 8, P]), ("b_rows", [P, 2, D])])
        (m.u, m.silu, m.hid, m.junk, m.diag, m.prob, m.prob_t, m.rope_tmp, m.rows, m.ang0, m.turns, m.ang) = shared(
            "mem_small",
            [("u", [P, RING, 2, SEQ]), ("silu", [P, RING, SEQ]), ("hid", [P, RING, SEQ])],
            [("junk", [P, TT, D]), ("diag", [P, TT, P])],
            [("prob", [P, 2, 2, 3 * P]), ("prob_t", [P, 2, 2, 3 * P])],
            [("rope_tmp", [P, 4 * 2 * 8 * HD // 2])],
            [("rows", [P, ROW_TILES, P]), ("ang0", [P, 192]), ("turns", [P, 192]), ("ang", [P, 192])])
        (m.qk96, m.xdt, m.y, m.zs, m.ext, m.lam, m.lam_x, m.sub_g, m.dist, m.sub_x) = shared(
            "mem_ssm",
            [("qk96", [P, TT, 8, QK])],
            [("xdt", [P, TT, GROUP]), ("y", [P, TT, GROUP]), ("zs", [P, TT, GROUP])],
            [("ext", [32, 3 * P]), ("lam", [P, 4, 64]), ("lam_x", [P, P]), ("sub_g", [P, P]), ("dist", [P, SEQ]), ("sub_x", [P, TT, P])])
        (m.gain, m.wide) = shared(
            "mem_rows",
            [("gain", [P, 2, D])],
            [("wide", [P, N_WIDE])])
        m.v_mla = sb(ctx, "v_mla", [P, TT, GROUP])
        m.c_t = sb(ctx, "c_t", [P, 3, SEQ])
        m.w_uq = sb(ctx, "w_uq", [P, 2, 4 * QK])
        m.w_ukv = sb(ctx, "w_ukv", [P, 512])
        m.xt = sb(ctx, "xt", [P, 4, 3 + SEQ])
        m.xc = sb(ctx, "xc", [P, 4, SEQ])
        m.conv = sb(ctx, "conv", [P, 4, SEQ])
        m.z0f = m.z0[:, :, :].rearrange("p h c -> p (h c)")
        m.z1f = m.z1[:, :, :].rearrange("p h c -> p (h c)")
        m.ps = ctx.enter_context(nc.psum_tensor("ps", [P, 8, 512], F32))
        m.ident = m.consts[:, CONST["ident"][0]:CONST["ident"][1]]
        m.upto = m.consts[:, CONST["upto"][0]:CONST["upto"][1]]
        m.after = m.consts[:, CONST["after"][0]:CONST["after"][1]]
        m.ones = m.consts[:, CONST["ones"][0]:CONST["ones"][1]]
        m.cst = lambda n: m.consts[:, CONST[n][0]:CONST[n][1]]
        m.wide_ = lambda n: m.wide[:, WIDE[n][0]:WIDE[n][1]]
        m.row_loads = len(row_pieces())
        m.b_v = m.b_uv[:, :, D:2 * D]
        def q_pair(tensor, tiles):
            def q(i, h, t):
                return tensor[64 * h:64 * h + 64, i, t * P:(t + 1) * P]

            def k(i, h, nk):
                return tensor[64 * h:64 * h + 64, tiles + i, 0:nk * P]
            return q, k
        m.score_bank = {"a": 4, "c": 4, "moba": 0, "mla": 0}
        m.turn_bank = {"a": 6, "c": 6, "moba": 2, "mla": 2}
        m.out_bank = {"a": 3, "c": 3, "moba": 4, "mla": 4}
        m.heads = {
            "a": (*q_pair(m.qk, 8), lambda i, h, t: m.v[:, t, i * P + h * HD:i * P + (h + 1) * HD]),
            "c": (*q_pair(m.qk, 8), lambda i, h, t: m.v[:, t, i * P:(i + 1) * P]),
            "moba": (*q_pair(m.moba_t, 2), lambda i, h, t: m.proj[:, t, 512 + i * P + h * HD:512 + i * P + (h + 1) * HD]),
            "mla": (lambda i, h, t: m.mla_t[0:QK, 2 * i + h, t * P:(t + 1) * P],
                    lambda i, h, nk: m.mla_t[0:QK, 4 + 2 * i + h, 0:nk * P],
                    lambda i, h, t: m.v_mla[:, t, i * P + h * HD:i * P + (h + 1) * HD]),
        }

        s = Semaphores(lambda name: ctx.enter_context(nc.semaphore(name)))
        total = sum(chunks_of(stage) for stage in PLAN)

        block = ctx.enter_context(nc.Block())

        def program(cls, eng):
            p = cls(nc, eng, m, s, d)
            p.total = total
            p.gains = []
            walk(p)

        @block.sync
        def _(eng):
            program(Sync, eng)

        @block.gpsimd
        def _(eng):
            program(Pool, eng)

        @block.scalar
        def _(eng):
            program(Scalar, eng)

        @block.vector
        def _(eng):
            program(Vector, eng)

        @block.tensor
        def _(eng):
            program(Tensor, eng)


INPUTS = ["x", "positions", "mix_norm_g", "w_in", "moba_qk_g", "mla_q_norm_g", "mla_kv_norm_g", "mla_w_uq", "mla_w_ukv",
          "mla_qk_g", "ssm_conv_w", "ssm_conv_b", "ssm_dt_bias", "ssm_a_log", "ssm_d", "ssm_norm_g", "head_out_g", "w_out",
          "ffn_norm_g", "ffn_w_in", "ffn_conv_w", "ffn_conv_b", "ffn_w_out", "norm_g_2", "ff1_w_in_2", "ff1_w_out_2",
          "ff2_w_in_2", "ff2_w_out_2", "a_w_qkv_2", "a_rel_bias_2", "a_w_o_2", "b_w_in_2", "b_ln_g_2", "b_ln_b_2", "b_w_s_2",
          "b_b_s_2", "b_w_o_2", "c_w_qkv_2", "c_lambda_2", "c_subln_g_2", "c_w_o_2"]


def kernel(**inputs):
    import concourse.bacc as bacc
    from concourse.bass_utils import run_bass_kernel_spmd

    nc = bacc.Bacc("TRN2", target_bir_lowering=False, num_devices=1)
    arrays, tensors = {}, {}
    for name in INPUTS + ["consts"]:
        a = np.ascontiguousarray(CONSTS if name == "consts" else inputs[name])
        arrays[f"in_{name}"] = a
        tensors[name] = nc.dram_tensor(f"in_{name}", a.shape, mybir.dt.from_np(a.dtype), kind="ExternalInput").ap()
    tensors["out"] = nc.dram_tensor("out_0", (1, SEQ, D), F32, kind="ExternalOutput").ap()
    tensors["ext_dram"] = nc.dram_tensor("ext_rel_bias", (32, 3 * P), F32, kind="Internal").ap()
    build(nc, Dram(tensors))
    return run_bass_kernel_spmd(nc, [arrays], core_ids=[0]).results[0]["out_0"]
```

```python
from contextlib import ExitStack

import numpy as np

import concourse.bass as bass
import concourse.mybir as mybir
from concourse.alu_op_type import AluOpType as ALU

F32 = mybir.dt.float32
F32R = mybir.dt.float32r
I32 = mybir.dt.int32
ACT = mybir.ActivationFunctionType
AX = mybir.AxisListType.X

P = 128
SEQ, D, FF = 256, 1024, 2816
TT = SEQ // P
KT = D // P
FT = FF // P
GROUP, HD = 256, 64
QR, KVR, ROPE, NOPE = 192, 128, 32, 64
QK = NOPE + ROPE
XBC = 512
IN = 3 * GROUP + QR + KVR + ROPE + 3 * GROUP + GROUP + XBC + 4
C_MOBA = 0
C_CQ = 3 * GROUP
C_CKV = C_CQ + QR
C_KR = C_CKV + KVR
C_SB = C_KR + ROPE
C_Z = C_SB + 3 * GROUP
C_XBC = C_Z + GROUP
C_DT = C_XBC + XBC
EPS = 1e-6
BIG = -1e30
CHUNK = 64
REL = 128
THETA = 10000.0

RING = 3
AHEAD = RING - 1
CW = 2048

PLAN = ([(s, l) for l in range(2) for s in ("mix1", "ffn1")]
        + [s for i in range(4) for s in (("swiglu", i, 0), ("mix2", i), ("swiglu", i, 1))])

CONST = {}


def constants():
    parts, at = [], 0

    def add(name, a):
        nonlocal at
        a = np.asarray(a, np.float32)
        parts.append(a)
        CONST[name] = (at, at + a.shape[1])
        at += a.shape[1]

    r, c = np.arange(P)[:, None], np.arange(P)[None, :]
    add("ident", r == c)
    add("upto", r <= c)
    add("after", r > c)
    add("ones", np.ones((P, P)))
    causal = np.where(c <= r, 0, BIG)
    add("causal", np.concatenate([causal, np.zeros((P, P)), causal], 1))
    add("upto_add", np.where(r <= c, 0, BIG))
    strict = (r < c).astype(np.float32)
    add("strict", np.concatenate([strict, np.ones((P, P)), strict], 1))
    add("minus_half", np.full((P, 24), -0.5))
    for name, dim in (("inv64", HD), ("inv32", ROPE)):
        inv = np.float32(1) / (np.float32(THETA) ** (np.arange(0, dim, 2, dtype=np.float32) / np.float32(dim)))
        add(name, np.broadcast_to(inv.astype(np.float32), (P, dim // 2)))
    add("dist", -np.abs(np.arange(P)[:, None] + np.arange(SEQ)[None, :] - 127))
    return np.concatenate(parts, 1)


CONSTS = constants()

ROWS = {}
_rows = [("mix_norm_g", 2 * KT), ("ffn_norm_g", 2 * KT), ("norm_g", 24 * KT), ("ssm_conv_w", 2 * 4 * 4),
         ("ssm_conv_b", 2 * 4), ("ffn_conv_w", 2 * 3 * 2 * FT), ("ffn_conv_b", 2 * 2 * FT), ("b_b_s", 8)]
_at = 0
for _n, _k in _rows:
    ROWS[_n] = _at
    _at += _k
N_ROWS = _at
ROW_TILES = -(-N_ROWS // P)

WIDE = {}
_wide = [("moba_g", 128), ("q_norm", QR), ("kv_norm", KVR), ("qk_g", 2 * QK), ("dt_bias", 4), ("a_log", 4), ("ssm_d", 4),
         ("ssm_norm", GROUP), ("head_g", 3 * GROUP)]
_at = 0
for _n, _k in _wide:
    WIDE[_n] = (_at, _at + _k)
    _at += _k
N_WIDE = _at

class Semaphores:

    def __init__(self, new):
        self.params_in = new("params_in")
        self.rows_in = new("rows_in")
        self.rows_cleared = new("rows_cleared")
        self.rows_turned = new("rows_turned")
        self.rows_kept = new("rows_kept")
        self.pos_in = new("pos_in")
        self.wide_in = new("wide_in")
        self.ext_out = new("ext_out")
        self.ext_in = new("ext_in")
        self.w_in_small = new("w_in_small")
        self.x_in = new("x_in")
        self.angles = new("angles")
        self.sines = new("sines")
        self.out_stored = new("out_stored")
        self.split_hi = new("split_hi")
        self.split_lo = new("split_lo")
        self.chunk_done = new("chunk_done")
        self.bank_free = new("bank_free")
        self.squares = new("squares")
        self.ln_centred = new("ln_centred")
        self.ln_squares = new("ln_squares")
        self.conv_half = new("conv_half")
        self.o_squares = new("o_squares")
        self.diagonals = new("diagonals")
        self.spread = new("spread")
        self.first_tile = new("first_tile")
        self.dist_in = new("dist_in")
        self.rstd = new("rstd")
        self.normed = new("normed")
        self.turned = new("turned")
        self.hi_turned = new("hi_turned")
        self.features = new("features")
        self.silu = new("silu")
        self.seeded = new("seeded")
        self.gated = new("gated")
        self.hid_hi = new("hid_hi")
        self.hid_ready = new("hid_ready")
        self.m_squares = new("m_squares")
        self.m_rstd = new("m_rstd")
        self.residual = new("residual")
        self.scores = new("scores")
        self.masked = new("masked")
        self.maxed = new("maxed")
        self.exps = new("exps")
        self.mixed = new("mixed")
        self.probs_turned = new("probs_turned")
        self.turned_copied = new("turned_copied")
        self.pair_out = new("pair_out")
        self.out_kept = new("out_kept")
        self.bias_ready = new("bias_ready")
        self.attended = new("attended")
        self.lam_in = new("lam_in")
        self.lam_dots = new("lam_dots")
        self.lam_exps = new("lam_exps")
        self.sub_sq = new("sub_sq")
        self.sub_rstd = new("sub_rstd")
        self.b_rows_in = new("b_rows_in")
        self.bw_in = new("bw_in")
        self.bw_turned = new("bw_turned")
        self.bw_kept = new("bw_kept")
        self.ln_ms = new("ln_ms")
        self.ln_rstd = new("ln_rstd")
        self.v_normed = new("v_normed")
        self.gated_sums = new("gated_sums")
        self.b_y = new("b_y")
        self.moba_sq = new("moba_sq")
        self.moba_ms = new("moba_ms")
        self.moba_rstd = new("moba_rstd")
        self.z_taken = new("z_taken")
        self.c_sq = new("c_sq")
        self.c_ms = new("c_ms")
        self.c_rstd = new("c_rstd")
        self.moba_ready = new("moba_ready")
        self.c_ready = new("c_ready")
        self.sb_turned = new("sb_turned")
        self.sb_kept = new("sb_kept")
        self.xbc_turned = new("xbc_turned")
        self.xbc_kept = new("xbc_kept")
        self.moba_turned = new("moba_turned")
        self.moba_kept = new("moba_kept")
        self.c_turned = new("c_turned")
        self.c_kept = new("c_kept")
        self.up_done = new("up_done")
        self.up_used = new("up_used")
        self.mla_sq = new("mla_sq")
        self.mla_ms = new("mla_ms")
        self.mla_rstd = new("mla_rstd")
        self.mla_ready = new("mla_ready")
        self.mla_turned = new("mla_turned")
        self.mla_kept = new("mla_kept")
        self.z_done = new("z_done")
        self.z_ln = new("z_ln")
        self.z_l = new("z_l")
        self.tail_done = new("tail_done")
        self.z_arg = new("z_arg")
        self.z_exp = new("z_exp")
        self.sb_a = new("sb_a")
        self.sb_o = new("sb_o")
        self.sb_o_kept = new("sb_o_kept")
        self.convd = new("convd")
        self.xc_done = new("xc_done")
        self.xh_turned = new("xh_turned")
        self.xh_kept = new("xh_kept")
        self.dt_raw = new("dt_raw")
        self.dt_abs = new("dt_abs")
        self.dt_e = new("dt_e")
        self.dt_u = new("dt_u")
        self.dt_ln = new("dt_ln")
        self.a_exp = new("a_exp")
        self.a_ready = new("a_ready")
        self.cum_done = new("cum_done")
        self.expo = new("expo")
        self.expo_done = new("expo_done")
        self.gram_done = new("gram_done")
        self.w_ready = new("w_ready")
        self.ssm_y = new("ssm_y")
        self.z_silu = new("z_silu")
        self.ssm_sq = new("ssm_sq")
        self.ssm_ms = new("ssm_ms")
        self.ssm_rstd = new("ssm_rstd")
        self.y_sum = new("y_sum")
        self.head_sq = new("head_sq")
        self.head_ms = new("head_ms")
        self.head_rstd = new("head_rstd")
        self.heads_ready = new("heads_ready")
        self.ext_stored = new("ext_stored")
        self.bias_in = new("bias_in")
        self.recips = new("recips")
        self.weighed = new("weighed")
        self.act_step = new("act_step")
        self.dve_step = new("dve_step")
        self.pool_step = new("pool_step")
        self.landed = [new(f"landed{i}") for i in range(RING)]
        self.gain_in = [new(f"gain_in{i}") for i in range(2)]


class Memory:
    pass


def view(t, **k):
    return t.rearrange("p (a b) -> p a b", **k)


class Program:
    def __init__(self, nc, eng, m, s, d):
        self.nc, self.e, self.m, self.s, self.d = nc, eng, m, s, d
        self.c0 = 0
        self.b0 = 0
        self.f0 = 0
        self.v0 = 0
        self.res = 0
        self.x_by_chunk = False
        self.p0 = 0
        self.rounds = {}
        self.steps_made = 0

    def bank(self, b):
        return (self.b0 + b) % RING

    def round(self, name):
        self.rounds[name] = self.rounds.get(name, 0) + 1
        return self.rounds[name]

    def at(self, sem, value, i=0, per_turn=0):
        if isinstance(i, int):
            value += i * per_turn
            if value > 0:
                self.e.wait_ge(sem, value)
        else:
            assert value > 0
            self.e.wait_ge(sem, i * per_turn + value)

    def steps(self, n, body, unroll=RING, peel=1, last=0):
        if self.c0 == 0:
            peel = n
        peel = min(peel, n)
        for b in range(peel):
            body(b, 0)
        turns = (n - peel - last) // unroll
        b = peel
        if turns >= 2:
            with self.e.Fori(0, turns) as i:
                for u in range(unroll):
                    body(peel + u, i)
            b += turns * unroll
        for b in range(b, n):
            body(b, 0)

    def gated(self, b, i):
        self.at(self.s.gated, self.f0 + b + 1, i, RING)

    def wait_x(self, t, half):
        if self.x_by_chunk:
            self.e.wait_ge(self.s.bank_free, self.b0 - 2 * (1 - half))
        elif self.res:
            self.e.wait_ge(self.s.residual, self.res - 3 + 2 * t + half)
        else:
            self.e.wait_ge(self.s.x_in, 16)

    def renewed(self, source):
        self.x_by_chunk = source == "chunks"
        if not self.x_by_chunk:
            self.res += 2 * TT

    def after_hidden(self, kind):
        self.advance(FT)
        self.f0 += FT
        if kind == "ffn1":
            self.v0 += FT

    def load_rows(self, which):
        e, m, s, d = self.e, self.m, self.s, self.d
        e.wait_ge(s.rows_cleared, 1)
        src = {"mix_norm_g": d.mix_norm_g.rearrange("l (k c) -> (l k) c", c=P),
               "ffn_norm_g": d.ffn_norm_g.rearrange("l (k c) -> (l k) c", c=P),
               "norm_g": d.norm_g.rearrange("l n (k c) -> (l n k) c", c=P),
               "ssm_conv_w": d.ssm_conv_w.rearrange("l w (k c) -> (l w k) c", c=P),
               "ssm_conv_b": d.ssm_conv_b.rearrange("l (k c) -> (l k) c", c=P),
               "ffn_conv_w": d.ffn_conv_w.rearrange("l w (k c) -> (l w k) c", c=P),
               "ffn_conv_b": d.ffn_conv_b.rearrange("l (k c) -> (l k) c", c=P),
               "b_b_s": d.b_b_s.rearrange("l g c -> (l g) c")}
        for name, first, last, tile, part in row_pieces()[which::2]:
            a = src[name]
            e.dma_start(m.rows[part:part + last - first, tile, :], a[first:last, :]).then_inc(s.rows_in, 16)

    def start(self): pass
    def finish(self): pass
    def norm(self, gain, kind): pass
    def turn(self, src, gain, ready): pass
    def post_norm(self, source, weight): self.renewed(source)
    def load_gain(self, layer, which): pass

    def attend(self, kind, l):
        for c in range(12):
            self.attend_chunk(kind, l, c)
            self.attend_pairs(kind, c)
        for c in range(12, values_at(7) + 1):
            self.attend_pairs(kind, c)
        self.p0 += 8
        self.m0 += 8 if kind == "c" else 0
        self.advance(12)

    m0 = 0

    def advance(self, n, banks=True):
        self.c0 += n
        if banks:
            self.b0 += n


def scores_at(b):
    return 3 * (b // 2) + 2


def turned_at(b):
    return scores_at(b) + 1 + b % 2


def values_at(b):
    return turned_at(b) + 1


IN_CHUNKS = -(-IN // 256)
IN_ORDER = (4, 5, 6, 7, 3, 0, 1, 2, 8, 9, 10)
assert sorted(IN_ORDER) == list(range(IN_CHUNKS))


def places(ready):
    if ready in ("x", "normed", "b_y"):
        return [(0, 0), (0, 1), (1, 0), (1, 1)]
    if ready == "heads_ready":
        return [(0, 1), (1, 1), (0, 0), (1, 0)]
    return [(0, 0), (1, 0), (0, 1), (1, 1)]


def walk(e):
    e.start()
    for stage in PLAN:
        if stage[0] == "mix1":
            l = stage[1]
            e.norm(ROWS["mix_norm_g"] + l * KT, "tokens")
            e.product_tokens("in1", l, IN_CHUNKS)
            e.mixers(l)
            e.turn("mixed", None, "heads_ready")
            e.product_tokens("out1", l, 4)
            e.post_norm("chunks", None)
        elif stage[0] == "ffn1":
            l = stage[1]
            e.norm(ROWS["ffn_norm_g"] + l * KT, "scaled")
            e.hidden("ffn1", l)
            e.down("ffn1", l)
            e.post_norm("psum", None)
        elif stage[0] == "swiglu":
            _, i, w = stage
            e.load_gain(i, 4 * w + 1)
            e.norm(ROWS["norm_g"] + (i * 6 + 4 * w) * KT, "features")
            e.hidden("swiglu", (i, w))
            e.down("swiglu", (i, w))
            e.post_norm("psum", 0.5)
        else:
            i = stage[1]
            e.load_gain(i, 3)
            e.norm(ROWS["norm_g"] + (i * 6 + 2) * KT, "tokens" if i % 3 == 1 else "features")
            if i % 3 == 1:
                e.product_tokens("b_in", i // 3, 8)
                e.gmlp(i // 3)
                e.turn("xn", None, "b_y")
                e.product_tokens("b_o", i // 3, 4)
            else:
                kind = "a" if i % 3 == 0 else "c"
                e.bias_tables(kind, i // 3)
                e.attend(kind, i // 3)
                if kind == "c":
                    e.sub_norm(i)
                e.turn("xn", None, "attended" if kind == "c" else "out_kept")
                e.product_tokens(kind + "_o", i // 3, 4)
            e.post_norm("product", 1.0)
    e.finish()


class Sync(Program):

    def start(self):
        e, m, s, d = self.e, self.m, self.s, self.d
        e.dma_start(m.x[:, :, :], d.x.rearrange("o (t p) c -> p (o t) c", p=P)).then_inc(s.x_in, 16)
        self.load_rows(1)

    def chunk(self, b, i, dst_src):
        c = self.c0 + b
        self.at(self.s.split_lo, c + 1 - RING, i, RING)
        dst, src = dst_src(self.m.raw[:, c % RING, :], b if isinstance(i, int) else i * RING + b)
        self.e.dma_start(dst, src).then_inc(self.s.landed[c % RING], 16)

    def columns(self, w, col, n):
        wv = w.rearrange("(k p) c -> p k c", p=P)

        def pick(raw, j):
            return (raw[:, :].rearrange("p (k c) -> p k c", k=KT), wv[:, :, bass.ds(j * 256 + col, 256)])
        return lambda b, i: self.chunk(b, i, pick)

    def product_tokens(self, what, l, n):
        d = self.d
        if what == "in1":
            for b in range(n - 1):
                self.columns(d.w_in[l], (IN_ORDER[b] - b) * 256, n)(b, 0)
            rest = IN - 256 * (n - 1)
            wv = d.w_in[l].rearrange("(k p) c -> p k c", p=P)
            self.chunk(n - 1, 0, lambda raw, j: (raw[:, 0:KT * 256].rearrange("p (k c) -> p k c", k=KT)[:, :, 0:rest],
                                                 wv[:, :, 256 * (n - 1):IN]))
        else:
            w, col = {"out1": (d.w_out, 0), "b_in": (d.b_w_in, 0), "b_o": (d.b_w_o, 0), "a_v": (d.a_w_qkv, 2 * D),
                      "a_o": (d.a_w_o, 0), "c_v": (d.c_w_qkv, 2 * D), "c_o": (d.c_w_o, 0)}[what]
            if what == "b_in":
                self.steps(4, self.columns(w[l], D, n), peel=0)
                self.advance(4)
                n = 4
            self.steps(n, self.columns(w[l], col, n), peel=0)
        self.advance(n)

    def attend(self, kind, l):
        w = self.d.a_w_qkv if kind == "a" else self.d.c_w_qkv
        for c in range(12):
            self.columns(w[l], (c % 3) * D + (c // 3) * 256 - c * 256, 12)(c, 0)
        self.advance(12)

    def weights_of(self, kind, l):
        d = self.d
        if kind == "ffn1":
            return d.ffn_w_in[l], d.ffn_w_out[l]
        i, w = l
        return (d.ff2_w_in[i], d.ff2_w_out[i]) if w else (d.ff1_w_in[i], d.ff1_w_out[i])

    def hidden(self, kind, l):
        w = self.weights_of(kind, l)[0].rearrange("(k p) (h n c) -> p h k n c", p=P, h=2, c=P)

        def pick(raw, j):
            return (raw[:, :].rearrange("p (h k n c) -> p h k n c", h=2, k=KT, n=1), w[:, :, :, bass.ds(j, 1), :])
        self.steps(FT, lambda b, i: self.chunk(b, i, pick), peel=0)
        self.advance(FT)

    def down(self, kind, l):
        w = self.weights_of(kind, l)[1].rearrange("(n k p) c -> p n k c", p=P, k=2)

        def pick(raw, j):
            return (raw[:, :].rearrange("p (n k c) -> p n k c", n=1, k=2), w[:, bass.ds(j, 1), :, :])
        self.steps(FT // 2, lambda b, i: self.chunk(b, i, pick), peel=0)
        self.advance(FT // 2, banks=False)

    def mixers(self, l): pass
    def gmlp(self, l): pass
    def bias_tables(self, kind, l): pass
    def attention(self, kind, n): pass
    def sub_norm(self, i): pass

    def finish(self):
        e, m, s = self.e, self.m, self.s
        for t in range(TT):
            self.wait_x(t, 1)
        e.dma_start(self.d.out.rearrange("o (t p) c -> p (o t) c", p=P), m.x[:, :, :]).then_inc(s.out_stored, 16)
        e.wait_ge(s.out_stored, 16)


class Tensor(Program):
    def start(self):
        e, m, s = self.e, self.m, self.s
        e.wait_ge(s.params_in, 16)
        e.wait_ge(s.rows_in, 16 * m.row_loads)
        for r in range(ROW_TILES):
            ins = e.transpose(m.ps[:, r, 0:P], m.rows[:, r, :], m.ident)
        ins.then_inc(s.rows_turned, 1)

    def turn(self, src, gain, ready):
        e, m, s = self.e, self.m, self.s
        a = m.x if src == "x" else m.xn
        self.last_first = ready == "heads_ready"
        if ready == "out_kept":
            e.wait_ge(s.out_kept, self.p0)
        elif ready != "x":
            r = self.round(ready)
        if self.round("turn") == 1:
            e.wait_ge(s.rows_kept, 1)
        for n, (t, half) in enumerate(places(ready)):
            if ready == "x":
                self.wait_x(t, half)
            elif ready == "normed":
                e.wait_ge(s.normed, 2 * TT * (r - 1) + n + 1)
            elif ready == "attended":
                e.wait_ge(s.attended, 4 * (r - 1) + n + 1)
            elif ready == "b_y":
                e.wait_ge(s.b_y, 4 * (r - 1) + n + 1)
            elif ready == "heads_ready":
                e.wait_ge(s.heads_ready, 2 * r - half)
            for k in range(4):
                f = 4 * half + k
                ins = e.transpose(m.ps[:, 4 + n, k * P:(k + 1) * P], a[:, t, f * P:(f + 1) * P], m.ident)
            ins.then_inc(s.turned, 1)

    def norm(self, gain, kind):
        self.turn("xn" if kind == "scaled" else "x", gain, "normed" if kind == "scaled" else "x")

    def begin_product(self):
        self.turns = self.round("features")

    def first_features(self, k):
        if k % 4 == 0:
            self.e.wait_ge(self.s.features, 4 * (self.turns - 1) + (4 if self.last_first else 2 + 2 * (k // 4)))

    def spread(self):
        e, m, s = self.e, self.m, self.s
        r = self.round("spread")
        e.wait_ge(s.diagonals, TT * r)
        for t in range(TT):
            ins = e.matmul(m.ps[:, 3, t * P:(t + 1) * P], m.ones, m.diag[:, t, :], start=True, stop=True)
        ins.then_inc(s.spread, 1)

    def chunk_start(self, b, i):
        self.at(self.s.split_lo, self.c0 + b + 1, i, RING)
        self.at(self.s.bank_free, self.b0 + b + 1 - RING, i, RING)

    def tokens_chunk(self, b, i, w=256, between=None):
        e, m, s = self.e, self.m, self.s
        self.chunk_start(b, i)
        c = self.c0 + b
        whi = m.whi[:, c % RING, :].rearrange("p (k c) -> p k c", k=KT)
        wlo = m.wlo[:, c % RING, :].rearrange("p (k c) -> p k c", k=KT)
        for t in range(TT):
            if t == 1 and between is not None:
                between()
            out = m.ps[:, self.bank(b), t * 256:t * 256 + w]
            for k in range(KT):
                if b == 0 and t == 0 and isinstance(i, int):
                    self.first_features(k)
                hi, lo = m.h_hi[:, k, t * P:(t + 1) * P], m.h_lo[:, k, t * P:(t + 1) * P]
                e.matmul(out, hi, whi[:, k, 0:w], start=(k == 0), stop=False)
                e.matmul(out, hi, wlo[:, k, 0:w], start=False, stop=False)
                ins = e.matmul(out, lo, whi[:, k, 0:w], start=False, stop=(k == KT - 1))
        ins.then_inc(s.chunk_done, 1)

    def product_tokens(self, what, l, n):
        self.begin_product()
        if what == "in1":
            for b in range(n):
                self.tokens_chunk(b, 0, min(256, IN - 256 * IN_ORDER[b]))
                self.mixers_early(b, l)
        elif what == "b_in":
            for b in range(n):
                self.tokens_chunk(b, 0)
                if b == 4:
                    self.turn_spatial()
        else:
            self.steps(n, lambda b, i: self.tokens_chunk(b, i), peel=n if n == 4 else 1)
        self.advance(n)

    def features_chunk(self, b, i, w_of, spread=True):
        e, m, s = self.e, self.m, self.s
        self.chunk_start(b, i)
        c = self.c0 + b
        for f in range(2):
            out = m.ps[:, self.bank(b), f * 256:(f + 1) * 256]
            for k in range(KT):
                if b == 0 and f == 0 and isinstance(i, int):
                    self.first_features(k)
                hi, lo = w_of(m.whi[:, c % RING, :], f, k), w_of(m.wlo[:, c % RING, :], f, k)
                e.matmul(out, hi, m.h_hi[:, k, :], start=(k == 0), stop=False)
                e.matmul(out, hi, m.h_lo[:, k, :], start=False, stop=False)
                ins = e.matmul(out, lo, m.h_hi[:, k, :], start=False, stop=(k == KT - 1))
        ins.then_inc(s.chunk_done, 1)
        if b == 0 and isinstance(i, int) and spread:
            self.spread()

    def attend_chunk(self, kind, l, c):
        if c == 0:
            self.begin_product()
        if c % 3 < 2:
            self.features_chunk(c, 0, lambda w, f, k: w[:, k * 256 + f * P:k * 256 + (f + 1) * P])
        else:
            self.tokens_chunk(c, 0, between=lambda: self.pair_scores(kind, 2 * (c // 3)))

    def pair_scores(self, kind, b):
        self.e.wait_ge(self.s.bank_free, self.b0 + 3 * (b // 2) + 2)
        self.scores(kind, b)

    def attend_pairs(self, kind, c):
        for b in range(8):
            if values_at(b) == c:
                self.e.wait_ge(self.s.bank_free, self.b0 + 3 * (b // 2) + 3)
                self.values(kind, b)
        for b in range(8):
            if turned_at(b) == c:
                self.turn_probs(kind, b)
        for b in range(1, 8, 2):
            if scores_at(b) == c:
                self.pair_scores(kind, b)

    def hidden(self, kind, l):
        self.begin_product()

        def w_of(w, f, k):
            return w[:, (f * KT + k) * P:(f * KT + k + 1) * P]
        self.steps(FT, lambda b, i: self.features_chunk(b, i, w_of, kind == "swiglu"), peel=1)
        self.after_hidden(kind)

    def down(self, kind, l):
        e, m, s = self.e, self.m, self.s
        for b in range(FT // 2):
            c = self.c0 + b
            self.at(s.split_lo, c + 1)
            self.at(s.hid_ready, self.f0 - FT + 2 * b + 2)
            whi = m.whi[:, c % RING, :].rearrange("p (k c) -> p k c", k=2)
            wlo = m.wlo[:, c % RING, :].rearrange("p (k c) -> p k c", k=2)
            for t in range(TT):
                for k in range(2):
                    f = 2 * b + k
                    hi, lo = m.hid_hi[:, f, t * P:(t + 1) * P], m.hid_lo[:, f, t * P:(t + 1) * P]
                    for x, w in ((hi, whi), (hi, wlo), (lo, whi)):
                        for h in range(2):
                            ins = e.matmul(m.ps[:, 4 + 2 * t + h, :], x, w[:, k, h * 512:(h + 1) * 512],
                                           start=(f == 0 and x is hi and w is whi),
                                           stop=(f == FT - 1 and x is lo))
                if b == FT // 2 - 1 and t == 0:
                    ins.then_inc(s.first_tile, 1)
            ins.then_inc(s.chunk_done, 1)
        self.advance(FT // 2, banks=False)

    def scores(self, kind, b):
        e, m, s = self.e, self.m, self.s
        (q, k, _), bank = m.heads[kind], m.score_bank[kind]
        self.at(s.masked, self.p0 + b)
        for h in range(2):
            e.matmul(m.ps[:, bank + h, 0:P], q(b, h, 0), k(b, h, 1), start=True, stop=True)
            ins = e.matmul(m.ps[:, bank + h, P:P + SEQ], q(b, h, 1), k(b, h, 2), start=True, stop=True)
        ins.then_inc(s.scores, 1)

    def turn_probs(self, kind, b):
        e, m, s = self.e, self.m, self.s
        if kind == "c":
            self.at(s.mixed, self.m0 + b + 1)
        else:
            self.at(s.exps, self.p0 + b + 1)
        self.at(s.turned_copied, self.p0 + b)
        for h in range(1 if kind == "c" else 2):
            for j in range(3):
                ins = e.transpose(m.ps[:, m.turn_bank[kind] + h, j * P:(j + 1) * P], m.prob[:, b % 2, h, j * P:(j + 1) * P],
                                  m.ident)
        ins.then_inc(s.probs_turned, 1)

    def values(self, kind, b):
        e, m, s = self.e, self.m, self.s
        v, out = m.heads[kind][2], m.ps[:, m.out_bank[kind], 0:SEQ]
        self.at(s.turned_copied, self.p0 + b + 1)
        self.at(s.out_kept, self.p0 + b)
        parts = 1 if kind == "c" else 2
        w = P // parts
        for h in range(parts):
            pt = m.prob_t[:, b % 2, h, :]
            t0, t1 = out[:, h * w:(h + 1) * w], out[:, P + h * w:P + (h + 1) * w]
            e.matmul(t0, pt[:, 0:P], v(b, h, 0), start=True, stop=True)
            e.matmul(t1, pt[:, P:2 * P], v(b, h, 0), start=True, stop=False)
            ins = e.matmul(t1, pt[:, 2 * P:3 * P], v(b, h, 1), start=False, stop=True)
        ins.then_inc(s.pair_out, 1)

    def attention(self, kind, n):
        self.scores(kind, 0)
        for b in range(n):
            if b < n - 1:
                self.scores(kind, b + 1)
            self.turn_probs(kind, b)
            self.values(kind, b)
        self.p0 += n

    def bias_tables(self, kind, l): pass
    def sub_norm(self, i): pass

    def turn_spatial(self):
        e, m, s = self.e, self.m, self.s
        e.wait_ge(s.bw_in, 16 * self.round("gmlp"))
        for g in range(8):
            ins = e.transpose(m.ps[:, 4 + g // 4, (g % 4) * P:(g % 4 + 1) * P], m.b_w[:, g, :], m.ident)
        ins.then_inc(s.bw_turned, 1)

    def gmlp(self, l):
        e, m, s = self.e, self.m, self.s
        r = self.rounds["gmlp"]
        e.wait_ge(s.bank_free, self.b0)
        e.wait_ge(s.bw_kept, 2 * r)
        e.wait_ge(s.v_normed, r)
        for t in range(TT):
            for g in range(8):
                ins = e.matmul(m.ps[:, 2 * t + g // 4, (g % 4) * P:(g % 4 + 1) * P], m.b_wt[:, g, :],
                               m.b_v[:, t, g * P:(g + 1) * P], start=True, stop=True)
            ins.then_inc(s.gated_sums, 1)

    def mixers_early(self, b, l):
        e, m, s = self.e, self.m, self.s
        ps, proj, ident = m.ps, m.proj, m.ident
        if b == 0:
            self.round("mixers")
        r = self.rounds["mixers"]
        if b == 4:
            e.wait_ge(s.bank_free, self.b0 + 4)
            for x in range(2):
                for j in range(2):
                    for t in range(TT):
                        col = C_SB + x * GROUP + j * P
                        ins = e.transpose(ps[:, 4 + x, j * 256 + t * P:j * 256 + (t + 1) * P], proj[:, t, col:col + P], ident)
            ins.then_inc(s.sb_turned, 1)
        elif b == 5:
            e.wait_ge(s.sb_kept, r)
            for h in range(4):
                part = slice(64 * (h % 2), 64 * (h % 2) + 64)
                e.matmul(ps[:, 4 + h, 0:SEQ], m.sb_t[part, 2 + h // 2, 0:P], m.sb_t[part, h // 2, :], start=True, stop=True)
                ins = e.matmul(ps[:, 4 + h, SEQ:SEQ + P], m.sb_t[part, 2 + h // 2, P:SEQ], m.sb_t[part, h // 2, P:SEQ],
                               start=True, stop=True)
            ins.then_inc(s.z_done, 1)
        elif b == 6:
            e.wait_ge(s.c_ready, r)
            e.wait_ge(s.z_taken, r)
            for t in range(TT):
                e.transpose(ps[:, 6, t * P:(t + 1) * P], m.cn[:, t, 0:P], ident)
                e.transpose(ps[0:64, 6, 256 + t * P:256 + (t + 1) * P], m.cn[:, t, P:QR], ident)
                ins = e.transpose(ps[:, 7, t * P:(t + 1) * P], m.cn[:, t, QR:QR + KVR], ident)
            ins.then_inc(s.c_turned, 1)
        elif b == 7:
            e.wait_ge(s.w_in_small, 48 * r)
            e.wait_ge(s.c_kept, r)
            for t in range(TT):
                tok = slice(t * P, (t + 1) * P)
                e.matmul(ps[:, 4 + t, 0:4 * QK], m.c_t[:, 0, tok], m.w_uq[:, 0, :], start=True, stop=False)
                e.matmul(ps[:, 4 + t, 0:4 * QK], m.c_t[0:64, 1, tok], m.w_uq[0:64, 1, :], start=False, stop=True)
                ins = e.matmul(ps[:, 6 + t, :], m.c_t[:, 2, tok], m.w_ukv[:, :], start=True, stop=True)
            ins.then_inc(s.up_done, 1)
        elif b == 9:
            e.wait_ge(s.up_used, r)
            e.wait_ge(s.z_l, r)
            for h in range(4):
                low = m.z0[:, h, :]
                e.matmul(ps[:, 4 + h, 0:SEQ], m.after, low[:, 0:SEQ], start=True, stop=False)
                e.matmul(ps[:, 4 + h, P:SEQ], m.ones, low[:, SEQ:SEQ + P], start=False, stop=True)
                ins = e.matmul(ps[:, 4 + h, SEQ:SEQ + P], m.after, low[:, SEQ:SEQ + P], start=False, stop=True,
                               skip_group_check=True)
            ins.then_inc(s.tail_done, 1)

    def mixers(self, l):
        e, m, s = self.e, self.m, self.s
        r = self.rounds["mixers"]
        ps, proj, ident = m.ps, m.proj, m.ident
        e.wait_ge(s.bank_free, self.b0)
        e.wait_ge(s.z_arg, r)
        for j in range(4):
            for t in range(TT):
                col = C_XBC + j * P
                ins = e.transpose(ps[:, 6 + j // 2, (j % 2) * 256 + t * P:(j % 2) * 256 + (t + 1) * P],
                                  proj[:, t, col:col + P], ident)
        ins.then_inc(s.xbc_turned, 1)
        e.wait_ge(s.moba_ready, r)
        for x in range(2):
            for j in range(2):
                for t in range(TT):
                    col = x * GROUP + j * P
                    ins = e.transpose(ps[:, 4 + x, j * 256 + t * P:j * 256 + (t + 1) * P], m.qk_rot[:, t, col:col + P], ident)
        ins.then_inc(s.moba_turned, 1)
        e.wait_ge(s.sb_a, r)
        for h in range(4):
            vcol = C_SB + 2 * GROUP + h * HD
            self.two_blocks(ps[:, 3, :], h, m.z1[:, h, :], lambda t: proj[:, t, vcol:vcol + HD])
        self.last.then_inc(s.sb_o, 1)
        e.wait_ge(s.moba_kept, r)
        e.wait_ge(s.xbc_kept, r)
        e.wait_ge(s.sb_o_kept, r)
        self.scores("moba", 0)
        e.wait_ge(s.xc_done, r)
        for j in range(2):
            for t in range(TT):
                ins = e.transpose(ps[:, 7, t * 256 + j * P:t * 256 + (j + 1) * P], m.xc[:, j, t * P:(t + 1) * P], ident)
        ins.then_inc(s.xh_turned, 1)
        e.wait_ge(s.a_ready, r)
        for t in range(TT):
            for h in range(4):
                e.matmul(ps[:, 5 + t, h * P:(h + 1) * P], m.a[:, t, h:h + 1].to_broadcast([P, P]), m.upto, start=True, stop=True)
        e.wait_ge(s.xh_kept, r)
        for t in range(TT):
            ins = e.matmul(ps[:, 7, t * 4:t * 4 + 4], m.upto, m.a[:, t, :], start=True, stop=True)
        ins.then_inc(s.cum_done, 1)
        self.scores("moba", 1)
        self.turn_probs("moba", 0)
        self.values("moba", 0)
        e.wait_ge(s.expo, r)
        for g in range(2):
            part = slice(64 * g, 64 * g + 64)
            e.matmul(ps[:, 7 - 2 * g, 0:SEQ], m.xc[part, 2, 0:P], m.xc[part, 3, :], start=True, stop=True)
            ins = e.matmul(ps[:, 7 - 2 * g, SEQ:SEQ + P], m.xc[part, 2, P:SEQ], m.xc[part, 3, P:SEQ], start=True, stop=True)
        ins.then_inc(s.gram_done, 1)
        self.turn_probs("moba", 1)
        self.values("moba", 1)
        self.p0 += 2
        e.wait_ge(s.mla_ready, r)
        for h in range(8):
            for t in range(TT):
                ins = e.transpose(ps[0:QK, h // 2, (h % 2) * 256 + t * P:(h % 2) * 256 + (t + 1) * P],
                                  m.qk96[:, t, h, :], ident)
        ins.then_inc(s.mla_turned, 1)
        e.wait_ge(s.mla_kept, r)
        self.scores("mla", 0)
        e.wait_ge(s.w_ready, r)
        for h in range(4):
            self.two_blocks(ps[:, 6, :], h, m.z0[:, h, :], lambda t: m.xdt[:, t, h * HD:(h + 1) * HD])
        self.last.then_inc(s.ssm_y, 1)
        self.scores("mla", 1)
        for b in range(2):
            self.turn_probs("mla", b)
            self.values("mla", b)
        self.p0 += 2

    def two_blocks(self, bank, h, w, rhs):
        e, c = self.e, slice(h * HD, (h + 1) * HD)
        e.matmul(bank[:, h * HD:(h + 1) * HD], w[:, 0:P], rhs(0), start=True, stop=True)
        e.matmul(bank[:, 256 + h * HD:256 + (h + 1) * HD], w[:, P:2 * P], rhs(0), start=True, stop=False)
        self.last = e.matmul(bank[:, 256 + h * HD:256 + (h + 1) * HD], w[:, 2 * P:3 * P], rhs(1), start=False, stop=True)


class Scalar(Program):
    def act(self, *a, **k):
        return self.nc.scalar.activation(*a, **k)

    def link(self, ins):
        self.steps_made += 1
        ins.then_inc(self.s.act_step, 1)
        self.e.wait_ge(self.s.act_step, self.steps_made)

    def split(self, b, i):
        m, s = self.m, self.s
        c = self.c0 + b + AHEAD
        if isinstance(i, int) and c >= self.total:
            return
        slot = c % RING
        self.at(s.landed[slot], 16 * (c // RING + 1), i, 16)
        self.at(s.chunk_done, c + 1 - RING, i, RING)
        self.act(m.whi[:, slot, :], m.raw[:, slot, :], ACT.Copy).then_inc(s.split_hi, 1)

    def start(self):
        e, m, s, d = self.e, self.m, self.s, self.d
        e.dma_start(m.consts[:, :], d.consts[:, 0:CONST["dist"][0]]).then_inc(s.params_in, 16)
        self.load_rows(0)
        e.dma_start(m.pos_i[:, :], d.positions.rearrange("o (t p) -> p (o t)", p=P),
                    allow_slow_non_contiguous=True).then_inc(s.pos_in, 16)
        for b in range(-AHEAD, 0):
            self.split(b, 0)
        e.wait_ge(s.rows_turned, 1)
        self.act(m.cols[:, :].rearrange("p (r c) -> p r c", c=P), m.ps[:, 0:ROW_TILES, 0:P], ACT.Copy).then_inc(s.rows_kept, 1)
        e.wait_ge(s.rows_kept, 1)

    def norm(self, gain, kind):
        e, m, s = self.e, self.m, self.s
        r = self.round("norm")

        def square(t):
            self.wait_x(t, 1)
            self.act(m.junk[:, t, :], m.x[:, t, :], ACT.Square, scale=D ** -0.5,
                     accum_out=m.ss[:, t:t + 1]).then_inc(s.squares, 1)
        if kind == "scaled":
            for t in range(TT):
                square(t)
            self.turn("xn", gain, "normed")
        else:
            self.turn("x", gain, "x", square)

    def turn(self, src, gain, ready, between=lambda t: None):
        e, m, s = self.e, self.m, self.s
        r = self.round("turn")
        if r == 1:
            e.wait_ge(s.rows_kept, 1)
        for n, (t, half) in enumerate(places(ready)):
            e.wait_ge(s.turned, 4 * (r - 1) + n + 1)
            tok, ps = slice(t * P, (t + 1) * P), view(m.ps[:, 4 + n, :], a=4)
            if gain is None:
                ins = self.act(m.h_hi[:, 4 * half:4 * half + 4, tok], ps, ACT.Copy)
            else:
                for k in range(4):
                    f = 4 * half + k
                    ins = self.act(m.h_hi[:, f, tok], ps[:, k, :], ACT.Copy, scale=m.cols[:, gain + f:gain + f + 1])
            ins.then_inc(s.hi_turned, 1)
            if half == 1:
                between(t)

    def chunk_ready(self, b, i):
        self.at(self.s.chunk_done, self.c0 + b + 1, i, RING)

    def product_tokens(self, what, l, n):
        e, m, s = self.e, self.m, self.s

        def body(b, i):
            self.split(b, i)
            if what == "out1":
                return
            self.chunk_ready(b, i)
            if what in ("a_o", "b_o", "c_o"):
                for t in range(TT):
                    ins = self.act(m.junk[:, t, b * 256:(b + 1) * 256], m.ps[:, self.bank(b), t * 256:(t + 1) * 256], ACT.Square,
                                   scale=D ** -0.5, accum_out=m.ss2[:, t, b:b + 1])
                ins.then_inc(s.o_squares, 1)
                return
            if b == 0 and isinstance(i, int):
                e.wait_ge(s.rstd, TT * self.rounds["norm"])
                self.at(s.bank_free, self.b0)
            dest = {"in1": lambda: m.proj, "a_v": lambda: m.v, "c_v": lambda: m.v, "b_in": lambda: m.b_uv}[what]()
            j = b if isinstance(i, int) else i * RING + b
            w = 256
            if what == "b_in":
                j = (b + 4) % 8
            if what == "in1":
                j = IN_ORDER[b]
                w = min(256, IN - 256 * j)
            for t in range(TT):
                ins = self.act(dest[:, t, bass.ds(j * 256, w)], m.ps[:, self.bank(b), t * 256:t * 256 + w],
                               ACT.Gelu if what == "b_in" else ACT.Copy, scale=m.rs[:, t:t + 1])
            ins.then_inc(s.bank_free, 1)
            if what == "in1":
                self.mixers_early(b, l)
            if what == "b_in" and b == 4:
                self.square_v()
        self.steps(n, body, peel=n if what in ("in1", "b_in") or n == 4 else 1)
        self.advance(n)

    def attend_chunk(self, kind, l, c):
        self.split(c, 0)
        if c == 2 and kind == "c":
            self.lambda_exps()
        for b in range(0, 8, 2):
            if scores_at(b) == c:
                self.exps(kind, b)

    def attend_pairs(self, kind, c):
        for b in range(8):
            if values_at(b) == c and kind == "c":
                self.square_out(b)
        for b in range(8):
            if turned_at(b) == c:
                self.keep_turned(kind, b)
        for b in range(1, 8, 2):
            if scores_at(b) == c:
                self.exps(kind, b)

    def square_out(self, b):
        m, s = self.m, self.s
        self.at(s.pair_out, self.p0 + b + 1)
        for t in range(TT):
            at = 8 * (b // 4) + 4 * t + b % 4
            ins = self.act(m.sub_x[:, t, :], m.ps[:, m.out_bank["c"], t * P:(t + 1) * P], ACT.Square, scale=0.125,
                           accum_out=m.st[:, at:at + 1])
        ins.then_inc(s.sub_sq, 1)

    def hidden(self, kind, l):
        e, m, s = self.e, self.m, self.s

        def hi(b, i):
            self.gated(b, i)
            j = b if isinstance(i, int) else i * RING + b
            self.act(m.hid_hi[:, bass.ds(j, 1), :], m.hid[:, b % RING:b % RING + 1, :], ACT.Copy).then_inc(s.hid_hi, 1)

        def silu(b, i):
            self.at(s.bank_free, self.b0 + b + 1, i, RING)
            self.gated(b - RING, i)
            self.act(m.silu[:, b % RING, :], m.u[:, b % RING, 0, :], ACT.Silu).then_inc(s.silu, 1)

        def body(b, i):
            self.split(b, i)
            if kind == "ffn1":
                self.chunk_ready(b, i)
                self.gated(b - RING, i)
                j = b if isinstance(i, int) else i * RING + b
                for g in range(2):
                    w = ROWS["ffn_conv_w"] + (l * 3 + 2) * 2 * FT + g * FT
                    bias = ROWS["ffn_conv_b"] + l * 2 * FT + g * FT
                    ins = self.act(m.u[:, b % RING, g, :], m.ps[:, self.bank(b), g * 256:(g + 1) * 256], ACT.Identity,
                                   bias=m.cols[:, bass.ds(j + bias, 1)], scale=m.cols[:, bass.ds(j + w, 1)])
                ins.then_inc(s.seeded, 1)
            if b > 0:
                silu(b - 1, i)
            if b > 1:
                hi(b - 2, i)
        self.steps(FT, body, peel=4)
        silu(FT - 1, 0)
        hi(FT - 2, 0)
        hi(FT - 1, 0)
        self.after_hidden(kind)

    def down(self, kind, l):
        self.round("down")
        for b in range(FT // 2):
            self.split(b, 0)
        self.advance(FT // 2, banks=False)

    def post_norm(self, source, weight):
        e, m, s = self.e, self.m, self.s
        if source == "psum" and weight is not None:
            r = self.round("post_psum")
            for t in range(TT):
                if t == 0:
                    e.wait_ge(s.first_tile, self.rounds["down"])
                else:
                    e.wait_ge(s.chunk_done, self.c0)
                for half in range(2):
                    self.act(m.junk[:, t, half * 512:(half + 1) * 512], m.ps[:, 4 + 2 * t + half, :], ACT.Square,
                             scale=D ** -0.5, accum_out=m.ss2[:, t, half:half + 1]).then_inc(s.m_squares, 1)
        self.renewed(source)

    def bias_tables(self, kind, l): pass

    def lambda_exps(self):
        m, s = self.m, self.s
        self.e.wait_ge(s.lam_dots, self.round("lam"))
        self.act(m.lam_d[:, 0:2], m.lam_d[:, 0:2], ACT.Exp).then_inc(s.lam_exps, 1)

    def exps(self, kind, b):
        m, s, par = self.m, self.s, b % 2
        self.at(s.maxed, self.p0 + b + 1)
        for h in range(2):
            for t in range(2):
                cols = slice(0, P) if t == 0 else slice(P, P + SEQ)
                ins = self.act(m.prob[:, par, h, cols], m.prob[:, par, h, cols], ACT.Exp,
                               bias=m.negmax[:, par, h, t:t + 1], accum_out=m.sums[:, par, h, t:t + 1])
        ins.then_inc(s.exps, 1)

    def keep_turned(self, kind, b):
        m, s, par, bank = self.m, self.s, b % 2, self.m.turn_bank[kind]
        parts = 1 if kind == "c" else 2
        self.at(s.probs_turned, self.p0 + b + 1)
        self.at(s.pair_out, self.p0 + b - 1)
        self.act(m.prob_t[:, par, 0:parts, :], m.ps[:, bank:bank + parts, 0:3 * P], ACT.Copy).then_inc(s.turned_copied, 1)

    def attention(self, kind, n):
        for b in range(n):
            self.exps(kind, b)
            self.keep_turned(kind, b)
        self.p0 += n

    def sub_norm(self, i): pass

    def gmlp(self, l): pass

    def square_v(self):
        e, m, s = self.e, self.m, self.s
        r = self.round("gmlp")
        e.wait_ge(s.ln_centred, r)
        for t in range(TT):
            ins = self.act(m.junk[:, t, :], m.b_v[:, t, :], ACT.Square, accum_out=m.ss3[:, t:t + 1])
        ins.then_inc(s.ln_squares, 1)

    def mixers_early(self, b, l):
        e, m, s = self.e, self.m, self.s
        ps, proj = m.ps, m.proj
        if b == 0:
            self.round("mixers")
        if b == 2 and l == 0:
            e.wait_ge(s.angles, 1)
            self.act(m.trig[:, :], m.ang[:, :], ACT.Sin).then_inc(s.sines, 1)
            e.wait_ge(s.sines, 1)
        r = self.rounds["mixers"]
        if b == 4:
            e.wait_ge(s.bank_free, self.b0 + 5)
            self.act(m.c_squares, proj[:, :, C_CQ:C_KR], ACT.Square).then_inc(s.c_sq, 1)
            e.wait_ge(s.sb_turned, r)
            self.act(m.sb_t[:, 0:2, :], view(ps[:, 4, :], a=2), ACT.Copy, scale=HD ** -0.5)
            self.act(m.sb_t[:, 2:4, :], view(ps[:, 5, :], a=2), ACT.Copy).then_inc(s.sb_kept, 1)
        elif b == 5:
            e.wait_ge(s.z_done, r)
            self.act(m.z1[:, :, :], ps[:, 4:8, 0:3 * P], ACT.Copy)
            self.act(m.z0[:, :, :], ps[:, 4:8, 0:3 * P], ACT.Abs).then_inc(s.z_taken, 1)
        elif b == 6:
            e.wait_ge(s.z_taken, r)
            self.link(self.act(m.z0[:, :, :], m.z0[:, :, :], ACT.Exp, scale=-1.0))
            self.act(m.z0[:, :, :], m.z0[:, :, :], ACT.Ln, bias=1.0).then_inc(s.z_ln, 1)
            e.wait_ge(s.c_turned, r)
            self.act(m.c_t[:, 0, :], ps[:, 6, 0:256], ACT.Copy)
            self.act(m.c_t[0:64, 1, :], ps[0:64, 6, 256:512], ACT.Copy)
            self.act(m.c_t[:, 2, :], ps[:, 7, 0:256], ACT.Copy).then_inc(s.c_kept, 1)
        elif b == 7:
            e.wait_ge(s.bank_free, self.b0 + 8)
            self.act(m.moba_x[:, :].rearrange("p (t c) -> p t c", t=2), proj[:, :, 0:512], ACT.Square).then_inc(s.moba_sq, 1)
            e.wait_ge(s.up_done, r)
            for t in range(TT):
                self.act(m.qk96[:, t, 0:4, :], ps[:, 4 + t, 0:4 * QK].rearrange("p (h c) -> p h c", h=4), ACT.Copy)
                kv = ps[:, 6 + t, :].rearrange("p (h c) -> p h c", h=4)
                self.act(m.qk96[:, t, 4:8, 0:NOPE], kv[:, :, 0:NOPE], ACT.Copy)
                for h in range(4):
                    self.act(m.qk96[:, t, 4 + h, NOPE:QK], proj[:, t, C_KR:C_KR + ROPE], ACT.Copy)
                ins = self.act(m.v_mla[:, t, :].rearrange("p (h c) -> p h c", h=4), kv[:, :, NOPE:], ACT.Copy)
            ins.then_inc(s.up_used, 1)
        elif b == 9:
            e.wait_ge(s.z_arg, r)
            self.act(m.z1[:, :, :], m.z1[:, :, :], ACT.Exp).then_inc(s.z_exp, 1)
        elif b == 10:
            e.wait_ge(s.up_used, r)
            e.wait_ge(s.moba_ready, r)
            self.act(m.rope_tmp[:, 0:2 * 8 * QK].rearrange("p (t c) -> p t c", t=2),
                     m.qk96[:, :, :, :].rearrange("p t h c -> p t (h c)"), ACT.Square).then_inc(s.mla_sq, 1)

    def mixers(self, l):
        e, m, s = self.e, self.m, self.s
        r = self.rounds["mixers"]
        ps, proj = m.ps, m.proj
        e.wait_ge(s.xbc_turned, r)
        for j in range(2):
            ins = self.act(m.xt[:, 2 * j:2 * j + 2, 3:3 + SEQ], view(ps[:, 6 + j, :], a=2), ACT.Copy)
        ins.then_inc(s.xbc_kept, 1)
        e.wait_ge(s.moba_turned, r)
        self.act(m.moba_t[:, 0:2, :], view(ps[:, 4, :], a=2), ACT.Copy, scale=HD ** -0.5)
        self.act(m.moba_t[:, 2:4, :], view(ps[:, 5, :], a=2), ACT.Copy).then_inc(s.moba_kept, 1)
        e.wait_ge(s.dt_raw, r)
        self.act(m.dt[:, 1, :], m.dt[:, 0, :], ACT.Abs).then_inc(s.dt_abs, 1)
        e.wait_ge(s.dt_abs, r)
        self.act(m.dt[:, 2, :], m.dt[:, 1, :], ACT.Exp, scale=-1.0).then_inc(s.dt_e, 1)
        self.act(m.ahead[:, :], m.wide_("a_log"), ACT.Exp).then_inc(s.a_exp, 1)
        e.wait_ge(s.dt_u, r)
        self.act(m.dt[:, 4, :], m.dt[:, 3, :], ACT.Ln).then_inc(s.dt_ln, 1)
        e.wait_ge(s.convd, r)
        self.act(m.xc[:, :, :], m.conv[:, :, :], ACT.Silu).then_inc(s.xc_done, 1)
        e.wait_ge(s.xh_turned, r)
        self.act(m.xh[:, :, :], view(ps[:, 7, :], a=2), ACT.Copy).then_inc(s.xh_kept, 1)
        self.exps("moba", 0)
        self.keep_turned("moba", 0)
        e.wait_ge(s.expo, r)
        self.act(m.z0[:, :, :], m.z0[:, :, :], ACT.Exp).then_inc(s.expo_done, 1)
        self.exps("moba", 1)
        self.keep_turned("moba", 1)
        self.p0 += 2
        e.wait_ge(s.mla_turned, r)
        for b in range(4):
            ins = self.act(m.mla_t[0:QK, 2 * b:2 * b + 2, :], view(ps[0:QK, b, :], a=2), ACT.Copy,
                           scale=QK ** -0.5 if b < 2 else 1.0)
        ins.then_inc(s.mla_kept, 1)
        self.act(m.zs[:, :, :], proj[:, :, C_Z:C_Z + GROUP], ACT.Silu).then_inc(s.z_silu, 1)
        e.wait_ge(s.sb_o_kept, r)
        e.wait_ge(s.out_kept, self.p0)
        z1 = m.z1f[:, :].rearrange("p (t c) -> p t c", t=2)
        for c in (slice(0, 256), slice(512, 768)):
            ins = self.act(z1[:, :, c], m.xn[:, :, c], ACT.Square)
        ins.then_inc(s.head_sq, 1)
        self.exps("mla", 0)
        self.keep_turned("mla", 0)
        self.exps("mla", 1)
        self.keep_turned("mla", 1)
        self.p0 += 2
        e.wait_ge(s.y_sum, r)
        for t in range(TT):
            ins = self.act(m.ps[:, 5, t * 256:(t + 1) * 256], m.y[:, t, :], ACT.Square, accum_out=m.ss3[:, t:t + 1])
        ins.then_inc(s.ssm_sq, 1)
        e.wait_ge(s.out_kept, self.p0)
        self.act(z1[:, :, 256:512], m.xn[:, :, 256:512], ACT.Square).then_inc(s.head_sq, 1)


class Vector(Program):
    def link(self, ins):
        self.steps_made += 1
        ins.then_inc(self.s.dve_step, 1)
        self.e.wait_ge(self.s.dve_step, self.steps_made)

    def split(self, b, i):
        m, s = self.m, self.s
        c = self.c0 + b + AHEAD
        if isinstance(i, int) and c >= self.total:
            return
        slot = c % RING
        self.at(s.split_hi, c + 1, i, RING)
        self.e.tensor_tensor(m.wlo[:, slot, :], m.raw[:, slot, :], m.whi[:, slot, :].bitcast(F32),
                             ALU.subtract).then_inc(s.split_lo, 1)

    def start(self):
        e, m, s = self.e, self.m, self.s
        e.memset(m.rows[:, ROW_TILES - 1, :], 0.0).then_inc(s.rows_cleared, 1)
        self.link(e.memset(m.xt[:, :, 0:3], 0.0))
        for b in range(-AHEAD, 0):
            self.split(b, 0)
        e.wait_ge(s.params_in, 16)
        e.wait_ge(s.ext_in, 16)
        e.tensor_scalar(m.ext[:, 2 * REL + 1:], m.cst("ones")[0:32, 0:127], m.ext[:, 2 * REL:2 * REL + 1], None,
                        ALU.mult).then_inc(s.ext_out, 1)

    def rotary_angles(self):
        e, m, s = self.e, self.m, self.s
        e.wait_ge(s.params_in, 16)
        e.wait_ge(s.pos_in, 16)
        self.link(e.tensor_copy(m.pos[:, :], m.pos_i[:, :]))
        half = {"64": HD // 2, "32": ROPE // 2}
        at = 0
        for name, n in half.items():
            for quarter in range(2):
                for t in range(TT):
                    ins = e.tensor_scalar(m.ang0[:, at + t * n:at + (t + 1) * n], m.cst("inv" + name), m.pos[:, t:t + 1], None, ALU.mult)
                at += TT * n
        self.link(ins)
        n_all, n_cos = at, None
        magic = 1.5 * 2.0 ** 23
        at = 0
        for name, n in half.items():
            for quarter in range(2):
                w = slice(at, at + TT * n)
                ins = e.tensor_scalar(m.turns[:, w], m.ang0[:, w], 1 / (2 * np.pi), 0.25 * quarter, ALU.mult, ALU.add)
                at += TT * n
        self.link(ins)
        self.link(e.tensor_scalar(m.turns[:, :], m.turns[:, :], magic, -magic, ALU.add, ALU.add))
        rest = 2 * np.pi
        for bits in (8, 8, 8, 24):
            scale = 2.0 ** (bits - 1 - np.floor(np.log2(rest)))
            part = float(np.float32(np.floor(rest * scale) / scale))
            rest -= part
            self.link(e.scalar_tensor_tensor(m.ang0[:, :], m.turns[:, :], -part, m.ang0[:, :], ALU.mult, ALU.add))
        at = 0
        for name, n in half.items():
            w = slice(at + TT * n, at + 2 * TT * n)
            ins = e.tensor_scalar(m.ang0[:, w], m.ang0[:, w], float(np.pi / 2), None, ALU.add)
            at += 2 * TT * n
        self.link(ins)
        lim = 3.1415925
        e.tensor_scalar(m.ang[:, :], m.ang0[:, :], lim, -lim, ALU.min, ALU.max).then_inc(s.angles, 1)

    def norm(self, gain, kind):
        e, m, s = self.e, self.m, self.s
        r = self.round("norm")
        if kind == "scaled":
            for t in range(TT):
                e.wait_ge(s.rstd, TT * (r - 1) + t + 1)
                for half in range(2):
                    c = slice(half * 512, (half + 1) * 512)
                    e.tensor_scalar(m.xn[:, t, c], m.x[:, t, c], m.rs[:, t:t + 1], None, ALU.mult).then_inc(s.normed, 1)
        self.turn("x", gain, "x")
        if kind == "features":
            for t in range(TT):
                e.wait_ge(s.rstd, TT * (r - 1) + t + 1)
                e.tensor_scalar(m.diag[:, t, :], m.ident, m.rs[:, t:t + 1], None, ALU.mult).then_inc(s.diagonals, 1)

    def take_spread(self):
        self.e.wait_ge(self.s.spread, self.round("spread"))
        self.link(self.e.tensor_copy(self.m.rb[:, :], self.m.ps[:, 3, 0:SEQ]))

    def turn(self, src, gain, ready):
        e, m, s = self.e, self.m, self.s
        r = self.round("turn")
        if r == 1:
            e.wait_ge(s.rows_kept, 1)
        for half in ((1, 0) if ready == "heads_ready" else (0, 1)):
            for t in range(TT):
                n = places(ready).index((t, half))
                e.wait_ge(s.hi_turned, 4 * (r - 1) + n + 1)
                tok, ps = slice(t * P, (t + 1) * P), view(m.ps[:, 4 + n, :], a=4)
                if gain is None:
                    f = slice(4 * half, 4 * half + 4)
                    ins = e.tensor_tensor(m.h_lo[:, f, tok], ps, m.h_hi[:, f, tok].bitcast(F32), ALU.subtract)
                else:
                    for k in range(4):
                        f = 4 * half + k
                        ins = e.scalar_tensor_tensor(m.h_lo[:, f, tok], ps[:, k, :], m.cols[:, gain + f:gain + f + 1],
                                                     m.h_hi[:, f, tok].bitcast(F32), ALU.mult, ALU.subtract)
                ins.then_inc(s.features, 1)

    def product_tokens(self, what, l, n):
        e, m, s = self.e, self.m, self.s
        post = what in ("a_o", "b_o", "c_o")
        if post:
            r = self.round("o_squares")
            g = self.rounds.get("post", 0) + 1
            e.wait_ge(s.gain_in[g % 2], 16 * ((g + 1) // 2))

        def body(b, i):
            self.split(b, i)
            c = slice(b * 256, (b + 1) * 256)
            ps = view(m.ps[:, self.bank(b), :], a=2)
            if post:
                e.wait_ge(s.o_squares, 4 * (r - 1) + b + 1)
                e.tensor_tensor(m.xn[:, :, c], ps, m.gain[:, g % 2, c].unsqueeze(1).to_broadcast([P, TT, 256]),
                                ALU.mult).then_inc(s.bank_free, 1)
            elif what == "out1":
                e.wait_ge(s.chunk_done, self.c0 + b + 1)
                e.tensor_tensor(m.x[:, :, c], ps, m.x[:, :, c], ALU.add).then_inc(s.bank_free, 1)
            elif what == "in1":
                self.mixers_early(b, l)
            elif what == "b_in":
                self.norm_v(b)
        self.steps(n, body, peel=n if what in ("in1", "b_in") or n == 4 else 1)
        self.advance(n)

    def attend_chunk(self, kind, l, c):
        e, m, s = self.e, self.m, self.s
        rb = m.rb[:, :].unsqueeze(1).to_broadcast([P, 2, SEQ])
        for b in range(8):
            if turned_at(b) == c:
                self.weigh(kind, b)
        self.split(c, 0)
        if c == 2:
            e.wait_ge(s.bias_ready, self.round("bias"))
            if kind == "c":
                self.mixing_factor()
        for b in range(0, 8, 2):
            if scores_at(b) == c:
                self.mask(kind, b)
        e.wait_ge(s.chunk_done, self.c0 + c + 1)
        if c == 0:
            self.take_spread()
        j, x = c // 3, c % 3
        if x < 2:
            e.scalar_tensor_tensor(m.qk[:, 8 * x + 2 * j:8 * x + 2 * j + 2, :], view(m.ps[:, self.bank(c), :], a=2),
                                   HD ** -0.5 if x == 0 else 1.0, rb, ALU.mult, ALU.mult).then_inc(s.bank_free, 1)
        else:
            for t in range(TT):
                ins = e.tensor_scalar(m.v[:, t, j * 256:(j + 1) * 256], m.ps[:, self.bank(c), t * 256:(t + 1) * 256],
                                      m.rs[:, t:t + 1], None, ALU.mult)
            ins.then_inc(s.bank_free, 1)

    def attend_pairs(self, kind, c):
        for b in range(8):
            if turned_at(b) == c and c >= 12:
                self.weigh(kind, b)
        for b in range(8):
            if values_at(b) == c:
                self.keep_out(kind, b)
                if b == 5 and kind == "c":
                    self.scale_out(0)
        for b in range(1, 8, 2):
            if scores_at(b) == c:
                self.mask(kind, b)

    def hidden(self, kind, l):
        e, m, s = self.e, self.m, self.s

        def lo(b, i):
            self.at(s.hid_hi, self.f0 + b + 1, i, RING)
            j = b if isinstance(i, int) else i * RING + b
            e.tensor_tensor(m.hid_lo[:, bass.ds(j, 1), :], m.hid[:, b % RING:b % RING + 1, :],
                            m.hid_hi[:, bass.ds(j, 1), :].bitcast(F32), ALU.subtract).then_inc(s.hid_ready, 1)

        def multiply(b, i):
            self.at(s.silu, self.f0 + b + 1, i, RING)
            e.tensor_tensor(m.hid[:, b % RING, :], m.silu[:, b % RING, :], m.u[:, b % RING, 1, :],
                            ALU.mult).then_inc(s.gated, 1)

        def body(b, i):
            j = b if isinstance(i, int) else i * RING + b
            bank = m.ps[:, self.bank(b), :]
            self.split(b, i)
            if kind == "ffn1":
                self.at(s.seeded, self.v0 + b + 1, i, RING)
                for tap in range(2):
                    back = 2 - tap
                    for g in range(2):
                        w = ROWS["ffn_conv_w"] + (l * 3 + tap) * 2 * FT + g * FT
                        u = m.u[:, b % RING, g, back:]
                        ins = e.scalar_tensor_tensor(u, bank[:, g * 256:(g + 1) * 256 - back],
                                                     m.cols[:, bass.ds(j + w, 1)], u, ALU.mult, ALU.add)
                    if tap == 0:
                        ins.then_inc(s.conv_half, 1)
                        self.at(s.conv_half, self.v0 + b + 1, i, RING)
                ins.then_inc(s.bank_free, 1)
            else:
                self.at(s.chunk_done, self.c0 + b + 1, i, RING)
                if b == 0:
                    self.take_spread()
                self.gated(b - RING, i)
                e.tensor_tensor(m.u[:, b % RING, :, :], view(bank, a=2), m.rb[:, :].unsqueeze(1).to_broadcast([P, 2, SEQ]),
                                ALU.mult).then_inc(s.bank_free, 1)
            if b > 0:
                self.at(s.bank_free, self.b0 + b + 1, i, RING)
                multiply(b - 1, i)
            if b > 1:
                lo(b - 2, i)
        self.steps(FT, body, peel=4)
        multiply(FT - 1, 0)
        lo(FT - 2, 0)
        lo(FT - 1, 0)
        self.after_hidden(kind)

    def down(self, kind, l):
        self.round("down")
        for b in range(FT // 2):
            self.split(b, 0)
        self.advance(FT // 2, banks=False)
    def post_norm(self, source, weight):
        e, m, s = self.e, self.m, self.s
        r = self.round("post") if weight is not None else 0
        q = self.round("post_psum") if weight is not None and source == "psum" else 0
        if q:
            e.wait_ge(s.gain_in[r % 2], 16 * ((r + 1) // 2))
        for t in range(TT if source != "chunks" else 0):
            if source == "psum" and weight is None:
                if t == 0:
                    e.wait_ge(s.first_tile, self.rounds["down"])
                else:
                    e.wait_ge(s.chunk_done, self.c0)
                for half in range(2):
                    c = slice(half * 512, (half + 1) * 512)
                    e.tensor_tensor(m.x[:, t, c], m.ps[:, 4 + 2 * t + half, :], m.x[:, t, c], ALU.add).then_inc(s.residual, 1)
                continue
            if q:
                for half in range(2):
                    c = slice(half * 512, (half + 1) * 512)
                    e.wait_ge(s.m_squares, 4 * (q - 1) + 2 * t + half + 1)
                    ins = e.scalar_tensor_tensor(m.xn[:, t, c], m.ps[:, 4 + 2 * t + half, :], weight, m.gain[:, r % 2, c],
                                                 ALU.mult, ALU.mult)
                self.link(ins)
            elif t == 0:
                e.wait_ge(s.bank_free, self.b0)
            e.wait_ge(s.m_rstd, TT * (r - 1) + t + 1)
            for half in range(2):
                c = slice(half * 512, (half + 1) * 512)
                e.scalar_tensor_tensor(m.x[:, t, c], m.xn[:, t, c], m.rs2[:, t:t + 1], m.x[:, t, c], ALU.mult,
                                       ALU.add).then_inc(s.residual, 1)
        self.renewed(source)

    def bias_tables(self, kind, l): pass

    def mixing_factor(self):
        e, m, s = self.e, self.m, self.s
        r = self.round("lam")
        e.wait_ge(s.lam_in, 32 * r)
        for j in range(2):
            ins = e.tensor_tensor_reduce(m.lam_x[:, j * 64:(j + 1) * 64], m.lam[:, 2 * j, :], m.lam[:, 2 * j + 1, :], 1.0, 0.0,
                                         ALU.mult, ALU.add, m.lam_d[:, j:j + 1])
        ins.then_inc(s.lam_dots, 1)
        e.wait_ge(s.lam_exps, r)
        self.link(e.tensor_tensor(m.lam_d[:, 2:3], m.lam_d[:, 0:1], m.lam_d[:, 1:2], ALU.subtract))
        self.link(e.tensor_scalar(m.lam_d[:, 3:4], m.lam_d[:, 2:3], -1.0, -LAMBDA_INIT, ALU.mult, ALU.add))

    def mask(self, kind, b):
        e, m, s, par = self.e, self.m, self.s, b % 2
        self.at(s.scores, self.p0 + b + 1)
        self.at(s.probs_turned, self.p0 + b - 1)
        for h in range(2):
            sc, out = m.ps[:, m.score_bank[kind] + h, 0:3 * P], m.prob[:, par, h, :]
            if kind in ("a", "c"):
                tab = m.bias[:, b * 2 + h, :] if kind == "a" else m.bias[:, b, :]
                e.tensor_tensor(out[:, 0:P], sc[:, 0:P], tab[:, 0:P][:, ::-1], ALU.add)
                ins = e.tensor_tensor(out[:, P:], sc[:, P:], tab[:, ::-1], ALU.add)
            else:
                ins = e.tensor_tensor(out, sc, m.cst("causal"), ALU.add)
        ins.then_inc(s.masked, 1)
        self.at(s.masked, self.p0 + b + 1)
        e.tensor_reduce(m.negmax[:, par, :, 0:1], m.prob[:, par, :, 0:P], AX, ALU.max, negate=True)
        e.tensor_reduce(m.negmax[:, par, :, 1:2], m.prob[:, par, :, P:], AX, ALU.max, negate=True).then_inc(s.maxed, 1)

    def weigh(self, kind, b):
        e, m, s, par = self.e, self.m, self.s, b % 2
        self.at(s.exps, self.p0 + b + 1)
        e.reciprocal(m.rsum[:, par, 0:4], m.sums[:, par, :, :].rearrange("p h t -> p (h t)")).then_inc(s.recips, 1)
        if kind != "c":
            return
        self.at(s.recips, self.p0 + b + 1)
        e.tensor_scalar(m.rsum[:, par, 4:6], m.rsum[:, par, 2:4], m.lam_d[:, 3:4], None, ALU.mult)
        for t, cols in ((0, slice(0, P)), (1, slice(P, 3 * P))):
            ins = e.tensor_scalar(m.prob[:, par, 0, cols], m.prob[:, par, 0, cols], m.rsum[:, par, t:t + 1], None, ALU.mult)
        ins.then_inc(s.weighed, 1)
        self.at(s.weighed, self.m0 + b + 1)
        for t, cols in ((0, slice(0, P)), (1, slice(P, 3 * P))):
            ins = e.scalar_tensor_tensor(m.prob[:, par, 0, cols], m.prob[:, par, 1, cols], m.rsum[:, par, 4 + t:5 + t],
                                         m.prob[:, par, 0, cols], ALU.mult, ALU.add)
        ins.then_inc(s.mixed, 1)

    def keep_out(self, kind, b):
        e, m, s, par = self.e, self.m, self.s, b % 2
        self.at(s.pair_out, self.p0 + b + 1)
        self.at(s.recips, self.p0 + b + 1)
        base = 256 if kind == "mla" else 0
        out = m.xn[:, :, b * P + base:(b + 1) * P + base]
        acc = view(m.ps[:, m.out_bank[kind], 0:SEQ], a=2)
        if kind == "c":
            self.at(s.sub_sq, self.m0 + b + 1)
            e.scalar_tensor_tensor(out, acc, 1.0 - LAMBDA_INIT, m.sub_g[:, :].unsqueeze(1).to_broadcast([P, TT, P]), ALU.mult,
                                   ALU.mult).then_inc(s.out_kept, 1)
        else:
            r = m.rsum[:, par, 0:4].rearrange("p (h t) -> p t h", t=2).unsqueeze(3).to_broadcast([P, 2, 2, HD])
            e.tensor_tensor(out.rearrange("p t (h c) -> p t h c", h=2), acc.rearrange("p t (h c) -> p t h c", h=2), r,
                            ALU.mult).then_inc(s.out_kept, 1)

    def attention(self, kind, n):
        self.mask(kind, 0)
        for b in range(n):
            if b < n - 1:
                self.mask(kind, b + 1)
            self.weigh(kind, b)
            self.keep_out(kind, b)
        self.p0 += n

    def scale_out(self, half):
        e, m, s = self.e, self.m, self.s
        e.wait_ge(s.sub_rstd, self.round("sub"))
        self.at(s.out_kept, self.p0 + 4 * half + 4)
        for t in range(TT):
            v = m.xn[:, t, half * 512:(half + 1) * 512].rearrange("p (h c) -> p h c", h=4)
            at = 8 * half + 4 * t
            e.tensor_tensor(v, v, m.st[:, at:at + 4].unsqueeze(2).to_broadcast([P, 4, P]), ALU.mult).then_inc(s.attended, 1)

    def sub_norm(self, i):
        self.p0 -= 8
        self.scale_out(1)
        self.p0 += 8

    def norm_v(self, b):
        e, m, s = self.e, self.m, self.s
        if b == 0:
            self.round("gmlp")
        r = self.rounds["gmlp"]
        if b == 4:
            e.wait_ge(s.bank_free, self.b0 + 4)
            self.link(e.tensor_reduce(m.st[:, 0:2], m.b_v, AX, ALU.add))
            self.link(e.tensor_scalar(m.st[:, 0:2], m.st[:, 0:2], 1.0 / D, None, ALU.mult))
            for t in range(TT):
                ins = e.tensor_scalar(m.b_v[:, t, :], m.b_v[:, t, :], m.st[:, t:t + 1], None, ALU.subtract)
            ins.then_inc(s.ln_centred, 1)
        elif b == 5:
            e.wait_ge(s.bw_turned, r)
            for g in range(2):
                e.tensor_tensor(m.b_wt[:, 4 * g:4 * g + 4, :], view(m.ps[:, 4 + g, :], a=4),
                                m.cst("upto").unsqueeze(1).to_broadcast([P, 4, P]), ALU.mult).then_inc(s.bw_kept, 1)
            e.wait_ge(s.ln_squares, r)
            e.tensor_scalar(m.st[:, 2:4], m.ss3[:, :], 1.0 / D, EPS, ALU.mult, ALU.add).then_inc(s.ln_ms, 1)
        elif b >= 6:
            t = b - 6
            if t == 0:
                e.wait_ge(s.ln_rstd, r)
                e.wait_ge(s.b_rows_in, 32 * r)
            self.link(e.scalar_tensor_tensor(m.b_v[:, t, :], m.b_v[:, t, :], m.st[:, 4 + t:5 + t], m.b_rows[:, 0, :], ALU.mult, ALU.mult))
            ins = e.tensor_tensor(m.b_v[:, t, :], m.b_v[:, t, :], m.b_rows[:, 1, :], ALU.add)
            if t == 1:
                ins.then_inc(s.v_normed, 1)

    def gmlp(self, l):
        e, m, s = self.e, self.m, self.s
        r = self.rounds["gmlp"]
        e.wait_ge(s.bank_free, self.b0)
        for t in range(TT):
            e.wait_ge(s.gated_sums, 2 * (r - 1) + t + 1)
            for g in range(8):
                c = slice(g * P, (g + 1) * P)
                ins = e.scalar_tensor_tensor(m.xn[:, t, c], m.ps[:, 2 * t + g // 4, (g % 4) * P:(g % 4 + 1) * P],
                                             m.cols[:, ROWS["b_b_s"] + g:ROWS["b_b_s"] + g + 1], m.b_uv[:, t, c], ALU.add, ALU.mult)
                if g % 4 == 3:
                    ins.then_inc(s.b_y, 1)

    def rope(self, src, dst, tmp, kind, n):
        e, m = self.e, self.m
        at = {"64": 0, "32": 4 * HD // 2}[kind]
        sin, cos = (m.trig[:, at + q * 2 * n:at + (q + 1) * 2 * n].rearrange("p (t c) -> p t c", t=2).unsqueeze(2)
                    .to_broadcast([P, 2, 8, n]) for q in range(2))
        x1, x2 = src[:, :, :, 0:n], src[:, :, :, n:2 * n]
        w = 2 * 8 * n
        t = [tmp[:, q * w:(q + 1) * w].rearrange("p (t h c) -> p t h c", t=2, h=8) for q in range(4)]
        e.tensor_tensor(t[0], x1, cos, ALU.mult)
        e.tensor_tensor(t[1], x2, sin, ALU.mult)
        e.tensor_tensor(t[2], x1, sin, ALU.mult)
        self.link(e.tensor_tensor(t[3], x2, cos, ALU.mult))
        e.tensor_tensor(dst[:, :, :, 0:n], t[0], t[1], ALU.subtract)
        return e.tensor_tensor(dst[:, :, :, n:2 * n], t[2], t[3], ALU.add)

    def four(self, ap, h=8):
        return ap.rearrange("p t (h c) -> p t h c", h=h)

    def gain_rows(self, ap, h, w):
        return ap.unsqueeze(1).unsqueeze(1).to_broadcast([P, 2, h, w])

    def mixers_early(self, b, l):
        e, m, s = self.e, self.m, self.s
        proj = m.proj
        if b == 0:
            self.round("mixers")
        if b == 1 and l == 0:
            self.rotary_angles()
        r = self.rounds["mixers"]
        if b == 5:
            e.wait_ge(s.c_sq, r)
            e.tensor_reduce(m.st[:, 16:18], m.c_squares[:, :, 0:QR], AX, ALU.add)
            self.link(e.tensor_reduce(m.st[:, 18:20], m.c_squares[:, :, QR:QR + KVR], AX, ALU.add))
            e.tensor_scalar(m.st[:, 16:18], m.st[:, 16:18], 1.0 / QR, EPS, ALU.mult, ALU.add)
            e.tensor_scalar(m.st[:, 18:20], m.st[:, 18:20], 1.0 / KVR, EPS, ALU.mult, ALU.add).then_inc(s.c_ms, 1)
            e.wait_ge(s.wide_in, 16 * len(WIDE) * r)
            e.wait_ge(s.c_rstd, r)
            for at, col, w, g in ((16, 0, QR, "q_norm"), (18, QR, KVR, "kv_norm")):
                for t in range(TT):
                    ins = e.scalar_tensor_tensor(m.cn[:, t, col:col + w], proj[:, t, C_CQ + col:C_CQ + col + w],
                                                 m.st[:, at + t:at + t + 1], m.wide_(g), ALU.mult, ALU.mult)
            ins.then_inc(s.c_ready, 1)
        elif b == 7:
            e.wait_ge(s.z_ln, r)
            self.link(e.scalar_tensor_tensor(m.z0[:, :, :], m.z1[:, :, :], 0.0, m.z0[:, :, :], ALU.max, ALU.add))
            self.link(e.tensor_tensor(m.z1[:, :, :], m.z1[:, :, :], m.z0[:, :, :], ALU.subtract))
        elif b == 8:
            e.scalar_tensor_tensor(m.z0[:, :, :], m.z0[:, :, :], -1.0, m.strict, ALU.mult, ALU.mult).then_inc(s.z_l, 1)
            e.wait_ge(s.moba_sq, r)
            self.link(e.tensor_reduce(m.st[:, 0:16], m.moba_x[:, :].rearrange("p (h c) -> p h c", c=HD), AX, ALU.add))
            e.tensor_scalar(m.st[:, 0:16], m.st[:, 0:16], 1.0 / HD, EPS, ALU.mult, ALU.add).then_inc(s.moba_ms, 1)
        elif b == 9:
            e.wait_ge(s.moba_rstd, r)
            q0 = m.moba_x[:, :].rearrange("p (t h c) -> p t h c", t=2, h=8)
            self.link(e.tensor_tensor(q0, self.four(proj[:, :, 0:512]),
                                      m.st[:, 0:16].rearrange("p (t h) -> p t h", t=2).unsqueeze(3).to_broadcast([P, 2, 8, HD]), ALU.mult))
            for x in range(2):
                ins = e.tensor_tensor(q0[:, :, 4 * x:4 * x + 4, :], q0[:, :, 4 * x:4 * x + 4, :],
                                      self.gain_rows(m.wide_("moba_g")[:, x * HD:(x + 1) * HD], 4, HD), ALU.mult)
            self.link(ins)
            self.rope(q0, self.four(m.qk_rot[:, :, :]), m.rope_tmp, "64", HD // 2).then_inc(s.moba_ready, 1)
            e.wait_ge(s.tail_done, r)
            e.tensor_tensor(m.z1[:, :, :], m.z1[:, :, :], m.ps[:, 4:8, 0:3 * P], ALU.add).then_inc(s.z_arg, 1)

    def mixers(self, l):
        e, m, s = self.e, self.m, self.s
        r = self.rounds["mixers"]
        ps, proj, four, gains = m.ps, m.proj, self.four, self.gain_rows
        e.wait_ge(s.bank_free, self.b0)
        e.tensor_tensor(m.dt[:, 0, :].rearrange("p (t h) -> p t h", t=2), proj[:, :, C_DT:C_DT + 4],
                        m.wide_("dt_bias").unsqueeze(1).to_broadcast([P, 2, 4]), ALU.add).then_inc(s.dt_raw, 1)
        e.wait_ge(s.z_exp, r)
        e.tensor_tensor(m.z1[:, :, :], m.z1[:, :, :], m.strict, ALU.mult).then_inc(s.sb_a, 1)
        e.wait_ge(s.mla_sq, r)
        self.link(e.tensor_reduce(m.st[:, 20:36], m.rope_tmp[:, 0:2 * 8 * QK].rearrange("p (h c) -> p h c", c=QK), AX, ALU.add))
        e.tensor_scalar(m.st[:, 20:36], m.st[:, 20:36], 1.0 / QK, EPS, ALU.mult, ALU.add).then_inc(s.mla_ms, 1)
        e.wait_ge(s.dt_e, r)
        e.tensor_scalar(m.dt[:, 3, :], m.dt[:, 2, :], 1.0, None, ALU.add).then_inc(s.dt_u, 1)
        e.wait_ge(s.xbc_kept, r)
        for tap in (3, 2, 1, 0):
            for j in range(4):
                w = ROWS["ssm_conv_w"] + (l * 4 + tap) * 4 + j
                wc = m.cols[:, w:w + 1]
                if tap == 3:
                    bias = ROWS["ssm_conv_b"] + l * 4 + j
                    ins = e.tensor_scalar(m.conv[:, j, :], m.xt[:, j, 3:3 + SEQ], wc, m.cols[:, bias:bias + 1], ALU.mult, ALU.add)
                else:
                    ins = e.scalar_tensor_tensor(m.conv[:, j, :], m.xt[:, j, tap:tap + SEQ], wc, m.conv[:, j, :], ALU.mult, ALU.add)
            if tap:
                self.link(ins)
            else:
                ins.then_inc(s.convd, 1)
        tiny = 1e-20
        e.wait_ge(s.dt_ln, r)
        e.scalar_tensor_tensor(m.dt[:, 5, :], m.dt[:, 4, :], tiny, m.dt[:, 2, :], ALU.add, ALU.mult)
        self.link(e.tensor_scalar(m.dt[:, 6, :], m.dt[:, 3, :], -1.0, tiny, ALU.add, ALU.add))
        self.link(e.reciprocal(m.dt[:, 7, :], m.dt[:, 6, :]))
        self.link(e.tensor_tensor(m.dt[:, 5, :], m.dt[:, 5, :], m.dt[:, 7, :], ALU.mult))
        self.link(e.scalar_tensor_tensor(m.dt[:, 1, :], m.dt[:, 0, :], 0.0, m.dt[:, 5, :], ALU.max, ALU.add))
        e.wait_ge(s.a_exp, r)
        e.scalar_tensor_tensor(m.a[:, :, :], m.dt[:, 1, :].rearrange("p (t h) -> p t h", t=2), -1.0,
                               m.ahead[:, :].unsqueeze(1).to_broadcast([P, 2, 4]), ALU.mult, ALU.mult).then_inc(s.a_ready, 1)
        e.wait_ge(s.sb_o, r)
        e.tensor_copy(m.xn[:, :, 512:768], view(ps[:, 3, :], a=2)).then_inc(s.sb_o_kept, 1)
        e.wait_ge(s.mla_rstd, r)
        qk = m.qk96[:, :, :, :]
        self.link(e.tensor_tensor(qk, qk, m.st[:, 20:36].rearrange("p (t h) -> p t h", t=2).unsqueeze(3).to_broadcast([P, 2, 8, QK]), ALU.mult))
        for x in range(2):
            ins = e.tensor_tensor(qk[:, :, 4 * x:4 * x + 4, :], qk[:, :, 4 * x:4 * x + 4, :],
                                  gains(m.wide_("qk_g")[:, x * QK:(x + 1) * QK], 4, QK), ALU.mult)
        self.link(ins)
        self.rope(qk[:, :, :, NOPE:], qk[:, :, :, NOPE:], m.rope_tmp, "32", ROPE // 2).then_inc(s.mla_ready, 1)
        e.wait_ge(s.mla_ready, r)
        self.mask("moba", 0)
        e.wait_ge(s.cum_done, r)
        self.link(e.tensor_scalar(m.neg[:, 0:8], ps[:, 7, 0:8], -1.0, None, ALU.mult))
        self.link(e.tensor_tensor(m.neg[:, 8:12], ps[:, 5, P - 1::P], m.neg[:, 0:4], ALU.add))
        for h in range(4):
            row = [ps[:, 5 + t, h * P:(h + 1) * P] for t in range(TT)]
            e.scalar_tensor_tensor(m.z0[:, h, 0:P], row[0], m.neg[:, h:h + 1], m.cst("upto_add"), ALU.add, ALU.add)
            e.tensor_scalar(m.z0[:, h, P:2 * P], row[1], m.neg[:, 8 + h:9 + h], None, ALU.add)
            ins = e.scalar_tensor_tensor(m.z0[:, h, 2 * P:], row[1], m.neg[:, 4 + h:5 + h], m.cst("upto_add"), ALU.add, ALU.add)
        ins.then_inc(s.expo, 1)
        self.mask("moba", 1)
        self.weigh("moba", 0)
        self.keep_out("moba", 0)
        e.wait_ge(s.expo_done, r)
        e.wait_ge(s.gram_done, r)
        for g in range(2):
            w = m.z0[:, 2 * g:2 * g + 2, :]
            e.tensor_tensor(w, w, ps[:, 7 - 2 * g, 0:3 * P].unsqueeze(1).to_broadcast([P, 2, 3 * P]), ALU.mult)
        self.weigh("moba", 1)
        self.keep_out("moba", 1)
        self.p0 += 2

        def wide4(ap):
            return ap.rearrange("p (t h) -> p t h", t=2).unsqueeze(3).to_broadcast([P, 2, 4, HD])
        e.wait_ge(s.xh_kept, r)
        e.wait_ge(s.mla_turned, r)
        e.tensor_tensor(four(m.y[:, :, :], 4), four(m.xh[:, :, :], 4), gains(m.wide_("ssm_d"), 1, 4).rearrange("p t o h -> p t (o h)")
                        .unsqueeze(3).to_broadcast([P, 2, 4, HD]), ALU.mult)
        e.tensor_tensor(four(m.xdt[:, :, :], 4), four(m.xh[:, :, :], 4), wide4(m.dt[:, 1, :]), ALU.mult).then_inc(s.w_ready, 1)
        self.mask("mla", 0)
        z1 = m.z1f[:, :].rearrange("p (t g h c) -> p t g h c", t=2, g=3, h=4)
        st = [m.st[:, 36 + 8 * x:44 + 8 * x].rearrange("p (t h) -> p t h", t=2) for x in range(3)]
        e.wait_ge(s.head_sq, 2 * r - 1)
        e.tensor_reduce(st[0], z1[:, :, 0, :, :], AX, ALU.add)
        self.link(e.tensor_reduce(st[1], z1[:, :, 2, :, :], AX, ALU.add))
        e.tensor_scalar(m.st[:, 36:52], m.st[:, 36:52], 1.0 / HD, EPS, ALU.mult, ALU.add).then_inc(s.head_ms, 1)
        self.mask("mla", 1)
        self.weigh("mla", 0)
        self.keep_out("mla", 0)
        e.wait_ge(s.ssm_y, r)
        self.link(e.tensor_tensor(m.y[:, :, :], m.y[:, :, :], view(ps[:, 6, :], a=2), ALU.add))
        e.wait_ge(s.z_silu, r)
        e.tensor_tensor(m.y[:, :, :], m.y[:, :, :], m.zs[:, :, :], ALU.mult).then_inc(s.y_sum, 1)
        self.weigh("mla", 1)

        def heads(groups):
            for x, c in groups:
                o = four(m.xn[:, :, c:c + GROUP], 4)
                ins = e.tensor_tensor(o, o, st[x].unsqueeze(3).to_broadcast([P, 2, 4, HD]), ALU.mult)
            self.link(ins)
            for x, c in groups:
                o = m.xn[:, :, c:c + GROUP]
                ins = e.tensor_tensor(o, o, m.wide_("head_g")[:, c:c + GROUP].unsqueeze(1).to_broadcast([P, 2, GROUP]), ALU.mult)
            return ins
        e.wait_ge(s.head_rstd, 2 * r - 1)
        heads(((0, 0), (1, 512)))
        self.keep_out("mla", 1)
        self.p0 += 2
        e.wait_ge(s.ssm_sq, r)
        e.tensor_scalar(m.ms2[:, 0:2], m.ss3[:, :], 1.0 / GROUP, EPS, ALU.mult, ALU.add).then_inc(s.ssm_ms, 1)
        e.wait_ge(s.head_sq, 2 * r)
        self.link(e.tensor_reduce(st[2], z1[:, :, 1, :, :], AX, ALU.add))
        e.tensor_scalar(m.st[:, 52:60], m.st[:, 52:60], 1.0 / HD, EPS, ALU.mult, ALU.add).then_inc(s.head_ms, 1)
        e.wait_ge(s.ssm_rstd, r)
        for t in range(TT):
            ins = e.scalar_tensor_tensor(m.xn[:, t, 768:D], m.y[:, t, :], m.rs2[:, t:t + 1], m.wide_("ssm_norm"), ALU.mult, ALU.mult)
        ins.then_inc(s.heads_ready, 1)
        e.wait_ge(s.head_rstd, 2 * r)
        heads(((2, 256),)).then_inc(s.heads_ready, 1)


class Pool(Program):

    def power(self, out, in_, n):
        return self.e.tensor_tensor(out, in_, self.m.cst("minus_half")[:, 0:n], ALU.pow)

    def row(self, dst, src):
        return self.e.dma_start(dst, src.unsqueeze(0).to_broadcast([P] + list(src.shape)))

    def start(self):
        e, m, s, d = self.e, self.m, self.s, self.d
        e.dma_start(m.ext[:, 0:2 * REL + 1], d.a_rel_bias.rearrange("l h c -> (l h) c")).then_inc(s.ext_in, 16)
        self.layer_rows(0)
        e.wait_ge(s.ext_out, 1)
        e.dma_start(d.ext_dram, m.ext[:, :]).then_inc(s.ext_stored, 16)
        e.wait_ge(s.ext_stored, 16)

    def layer_rows(self, l):
        m, s, d = self.m, self.s, self.d
        src = {"moba_g": d.moba_qk_g[l].rearrange("a c -> (a c)"), "q_norm": d.mla_q_norm_g[l], "kv_norm": d.mla_kv_norm_g[l],
               "qk_g": d.mla_qk_g[l].rearrange("a c -> (a c)"), "dt_bias": d.ssm_dt_bias[l], "a_log": d.ssm_a_log[l],
               "ssm_d": d.ssm_d[l], "ssm_norm": d.ssm_norm_g[l], "head_g": d.head_out_g[l].rearrange("a h c -> (a h c)")}
        for name in WIDE:
            self.row(m.wide_(name), src[name]).then_inc(s.wide_in, 16)
        self.e.dma_start(m.w_uq[:, 0, :], d.mla_w_uq[l][0:P, :]).then_inc(s.w_in_small, 16)
        self.e.dma_start(m.w_uq[0:QR - P, 1, :], d.mla_w_uq[l][P:QR, :]).then_inc(s.w_in_small, 16)
        self.e.dma_start(m.w_ukv[:, :], d.mla_w_ukv[l]).then_inc(s.w_in_small, 16)

    def load_gain(self, layer, which):
        k = len(self.gains)
        self.gains.append(None)
        if k >= 2:
            self.e.wait_ge(self.s.residual, self.gains[k - 2])
        self.row(self.m.gain[:, (k + 1) % 2, :], self.d.norm_g[layer][which]).then_inc(self.s.gain_in[(k + 1) % 2], 16)

    def norm(self, gain, kind):
        s, m = self.s, self.m
        r = self.round("norm")
        if r == 1:
            self.e.wait_ge(s.params_in, 16)
        for t in range(TT):
            self.e.wait_ge(s.squares, TT * (r - 1) + t + 1)
            self.link(self.e.tensor_scalar(m.ms[:, t:t + 1], m.ss[:, t:t + 1], EPS, None, ALU.add))
            self.power(m.rs[:, t:t + 1], m.ms[:, t:t + 1], 1).then_inc(s.rstd, 1)

    def link(self, ins):
        self.steps_made += 1
        ins.then_inc(self.s.pool_step, 1)
        self.e.wait_ge(self.s.pool_step, self.steps_made)

    def post_norm(self, source, weight):
        e, m, s = self.e, self.m, self.s
        self.renewed(source)
        if weight is None:
            return
        r = self.round("post")
        self.gains[r - 1] = self.res
        if r == 1:
            e.wait_ge(s.params_in, 16)
        if source == "product":
            e.wait_ge(s.o_squares, 4 * self.round("o_squares"))
            self.link(e.tensor_tensor(m.ss2[:, :, 0:2], m.ss2[:, :, 0:2], m.ss2[:, :, 2:4], ALU.add))
        else:
            q = self.round("post_psum")
        for t in range(TT):
            if source == "psum":
                e.wait_ge(s.m_squares, 4 * (q - 1) + 2 * t + 2)
            self.link(e.tensor_tensor(m.ms2[:, t:t + 1], m.ss2[:, t, 0:1], m.ss2[:, t, 1:2], ALU.add))
            self.link(e.tensor_scalar(m.ms2[:, t:t + 1], m.ms2[:, t:t + 1], EPS, None, ALU.add))
            self.power(m.rs2[:, t:t + 1], m.ms2[:, t:t + 1], 1).then_inc(s.m_rstd, 1)

    def product_tokens(self, what, l, n):
        if what == "in1":
            self.mixers_early(l)
        if what == "b_in":
            self.spatial(l)
        self.advance(n)

    def mixers_early(self, l):
        e, m, s = self.e, self.m, self.s
        r = self.round("mixers")
        e.wait_ge(s.c_ms, r)
        self.power(m.st[:, 16:20], m.st[:, 16:20], 4).then_inc(s.c_rstd, 1)
        e.wait_ge(s.moba_ms, r)
        self.power(m.st[:, 0:16], m.st[:, 0:16], 16).then_inc(s.moba_rstd, 1)
    def attend_chunk(self, kind, l, c): pass

    def attend_pairs(self, kind, c):
        e, m, s = self.e, self.m, self.s
        for half in range(2):
            if kind == "c" and c == values_at(4 * half + 3):
                e.wait_ge(s.sub_sq, self.m0 + 4 * half + 4)
                st = m.st[:, 8 * half:8 * half + 8]
                self.link(e.tensor_scalar(st, st, 0.5, EPS, ALU.mult, ALU.add))
                self.power(st, st, 8).then_inc(s.sub_rstd, 1)

    def hidden(self, kind, l):
        self.after_hidden(kind)

    def down(self, kind, l):
        self.advance(FT // 2, banks=False)

    def bias_tables(self, kind, l):
        e, m, s, d = self.e, self.m, self.s, self.d
        r = self.round("bias")
        e.wait_ge(s.chunk_done, self.c0)
        if kind == "a":
            w = 3 * P
            for part in range(4):
                src = bass.AP(d.ext_dram.tensor, (l * 16 + part * 4) * w + 1, [[1, P], [w, 4], [1, SEQ]])
                e.dma_start(m.bias[:, part * 4:part * 4 + 4, :], src).then_inc(s.bias_in, 16)
            self.bias_loads = self.round("bias_a") * 64
            e.wait_ge(s.bias_in, self.bias_loads)
            n = 16
        else:
            n = 8
            e.dma_start(m.dist[:, :], d.consts[:, CONST["dist"][0]:CONST["dist"][1]]).then_inc(s.dist_in, 16)
            e.wait_ge(s.dist_in, 16)
            for h in range(n):
                ins = e.tensor_scalar(m.bias[:, h, :], m.dist[:, :], 2.0 ** (-8.0 * (h + 1) / 8), 0.0, ALU.mult, ALU.add)
            self.link(ins)
            self.row(m.lam[:, :, :], d.c_lambda[l]).then_inc(s.lam_in, 16)
            self.row(m.sub_g[:, :], d.c_subln_g[l]).then_inc(s.lam_in, 16)
        e.memset(m.bias[0:CHUNK, 0:n, 0:CHUNK], BIG).then_inc(s.bias_ready, 1)

    def attention(self, kind, n): pass

    def sub_norm(self, i): pass

    def gmlp(self, l): pass

    def spatial(self, l):
        e, m, s, d = self.e, self.m, self.s, self.d
        r = self.round("gmlp")
        self.at(s.chunk_done, self.c0)
        e.dma_start(m.b_w[:, :, :], d.b_w_s[l].rearrange("g t s -> t g s")).then_inc(s.bw_in, 16)
        self.row(m.b_rows[:, 0, :], d.b_ln_g[l]).then_inc(s.b_rows_in, 16)
        self.row(m.b_rows[:, 1, :], d.b_ln_b[l]).then_inc(s.b_rows_in, 16)
        e.wait_ge(s.ln_ms, r)
        self.power(m.st[:, 4:6], m.st[:, 2:4], 2).then_inc(s.ln_rstd, 1)

    def mixers(self, l):
        e, m, s = self.e, self.m, self.s
        r = self.rounds["mixers"]
        e.wait_ge(s.mla_ms, r)
        self.power(m.st[:, 20:36], m.st[:, 20:36], 16).then_inc(s.mla_rstd, 1)
        e.wait_ge(s.head_ms, 2 * r - 1)
        self.power(m.st[:, 36:52], m.st[:, 36:52], 16).then_inc(s.head_rstd, 1)
        e.wait_ge(s.ssm_ms, r)
        self.power(m.rs2[:, :], m.ms2[:, :], 2).then_inc(s.ssm_rstd, 1)
        e.wait_ge(s.head_ms, 2 * r)
        self.power(m.st[:, 52:60], m.st[:, 52:60], 8).then_inc(s.head_rstd, 1)
        e.wait_ge(s.heads_ready, 2 * r)
        if l == 0:
            self.layer_rows(1)


LAMBDA_INIT = 0.8 - 0.6 * float(np.exp(-0.3 * 2))


def row_pieces():
    out = []
    for name, n in _rows:
        done = 0
        while done < n:
            at = ROWS[name] + done
            k = min(n - done, P - at % P)
            out.append((name, done, done + k, at // P, at % P))
            done += k
    return out


def chunks_of(stage):
    if stage[0] == "mix1":
        return -(-IN // 256) + 4
    if stage[0] == "mix2":
        return 12 if stage[1] % 3 == 1 else 16
    return FT + FT // 2


class Dram:

    def __init__(self, t):
        self.x = t["x"]
        self.positions = t["positions"]
        self.mix_norm_g = t["mix_norm_g"]
        self.w_in = t["w_in"]
        self.moba_qk_g = t["moba_qk_g"]
        self.mla_q_norm_g = t["mla_q_norm_g"]
        self.mla_kv_norm_g = t["mla_kv_norm_g"]
        self.mla_w_uq = t["mla_w_uq"]
        self.mla_w_ukv = t["mla_w_ukv"]
        self.mla_qk_g = t["mla_qk_g"]
        self.ssm_conv_w = t["ssm_conv_w"]
        self.ssm_conv_b = t["ssm_conv_b"]
        self.ssm_dt_bias = t["ssm_dt_bias"]
        self.ssm_a_log = t["ssm_a_log"]
        self.ssm_d = t["ssm_d"]
        self.ssm_norm_g = t["ssm_norm_g"]
        self.head_out_g = t["head_out_g"]
        self.w_out = t["w_out"]
        self.ffn_norm_g = t["ffn_norm_g"]
        self.ffn_w_in = t["ffn_w_in"]
        self.ffn_conv_w = t["ffn_conv_w"]
        self.ffn_conv_b = t["ffn_conv_b"]
        self.ffn_w_out = t["ffn_w_out"]
        self.norm_g = t["norm_g_2"]
        self.ff1_w_in = t["ff1_w_in_2"]
        self.ff1_w_out = t["ff1_w_out_2"]
        self.ff2_w_in = t["ff2_w_in_2"]
        self.ff2_w_out = t["ff2_w_out_2"]
        self.a_w_qkv = t["a_w_qkv_2"]
        self.a_rel_bias = t["a_rel_bias_2"]
        self.a_w_o = t["a_w_o_2"]
        self.b_w_in = t["b_w_in_2"]
        self.b_ln_g = t["b_ln_g_2"]
        self.b_ln_b = t["b_ln_b_2"]
        self.b_w_s = t["b_w_s_2"]
        self.b_b_s = t["b_b_s_2"]
        self.b_w_o = t["b_w_o_2"]
        self.c_w_qkv = t["c_w_qkv_2"]
        self.c_lambda = t["c_lambda_2"]
        self.c_subln_g = t["c_subln_g_2"]
        self.c_w_o = t["c_w_o_2"]
        self.consts = t["consts"]
        self.out = t["out"]
        self.ext_dram = t["ext_dram"]


def build(nc, d):
    with ExitStack() as ctx:
        m = Memory()

        def sb(stack, name, shape, dt=F32):
            return stack.enter_context(nc.sbuf_tensor(name, shape, dt))

        m.raw = sb(ctx, "raw", [P, RING, CW])
        m.whi = sb(ctx, "whi", [P, RING, CW], F32R)
        m.wlo = sb(ctx, "wlo", [P, RING, CW], F32R)
        m.x = sb(ctx, "x", [P, TT, D])
        m.xn = sb(ctx, "xn", [P, TT, D])
        m.consts = sb(ctx, "consts", [P, CONST["dist"][0]])
        m.cols = sb(ctx, "cols", [P, ROW_TILES * P])
        m.trig = sb(ctx, "trig", [P, 192])
        m.ss = sb(ctx, "ss", [P, 2])
        m.ms = sb(ctx, "ms", [P, 2])
        m.rs = sb(ctx, "rs", [P, 2])
        m.ss2 = sb(ctx, "ss2", [P, 2, 4])
        m.ss3 = sb(ctx, "ss3", [P, 2])
        m.rb = sb(ctx, "rb", [P, SEQ])
        m.ms2 = sb(ctx, "ms2", [P, 2])
        m.rs2 = sb(ctx, "rs2", [P, 2])
        m.st = sb(ctx, "st", [P, 60])
        m.lam_d = sb(ctx, "lam_d", [P, 4])
        m.neg = sb(ctx, "neg", [P, 12])
        m.ahead = sb(ctx, "ahead", [P, 4])
        m.pos = sb(ctx, "pos", [P, 2])
        m.pos_i = sb(ctx, "pos_i", [P, 2], I32)
        m.negmax = sb(ctx, "negmax", [P, 2, 2, 2])
        m.sums = sb(ctx, "sums", [P, 2, 2, 2])
        m.rsum = sb(ctx, "rsum", [P, 2, 6])
        m.dt = sb(ctx, "dt", [P, 8, 8])
        m.a = sb(ctx, "a", [P, TT, 4])

        def shared(name, *layouts):
            size, made = 0, []
            for layout in layouts:
                with ExitStack() as inner:
                    used = 0
                    for args in layout:
                        made.append(sb(inner, *args))
                        used += int(np.prod(args[1][1:])) * 4
                    size = max(size, used)
            sb(ctx, name, [P, size // 4])
            return made

        (m.h_hi, m.h_lo, m.moba_t) = shared(
            "mem_features",
            [("h_hi", [P, KT, SEQ], F32R), ("h_lo", [P, KT, SEQ], F32R)],
            [("moba_t", [P, 4, SEQ])])
        (m.hid_hi, m.hid_lo, m.proj, m.z0, m.z1, m.mla_t, m.xh, m.qk, m.v, m.bias, m.b_uv, m.b_w, m.b_wt, m.b_rows) = shared(
            "mem_hidden",
            [("hid_hi", [P, FT, SEQ], F32R), ("hid_lo", [P, FT, SEQ], F32R)],
            [("proj", [P, TT, IN]), ("z0", [P, 4, 3 * P]), ("z1", [P, 4, 3 * P]), ("mla_t", [P, 8, SEQ]), ("xh", [P, TT, GROUP])],
            [("qk", [P, 16, SEQ]), ("v", [P, TT, D]), ("bias", [P, 16, SEQ])],
            [("b_uv", [P, TT, 2 * D]), ("b_w", [P, 8, P]), ("b_wt", [P, 8, P]), ("b_rows", [P, 2, D])])
        (m.u, m.silu, m.hid, m.junk, m.diag, m.prob, m.prob_t, m.rope_tmp, m.moba_x, m.rows) = shared(
            "mem_small",
            [("u", [P, RING, 2, SEQ]), ("silu", [P, RING, SEQ]), ("hid", [P, RING, SEQ])],
            [("junk", [P, TT, D]), ("diag", [P, TT, P])],
            [("prob", [P, 2, 2, 3 * P]), ("prob_t", [P, 2, 2, 3 * P])],
            [("rope_tmp", [P, 4 * 2 * 8 * HD // 2]), ("moba_x", [P, TT * 512])],
            [("rows", [P, ROW_TILES, P])])
        (m.qk96, m.xdt, m.y, m.zs, m.ext, m.ang0, m.turns, m.ang, m.lam, m.lam_x, m.sub_g, m.dist, m.sub_x) = shared(
            "mem_ssm",
            [("qk96", [P, TT, 8, QK])],
            [("xdt", [P, TT, GROUP]), ("y", [P, TT, GROUP]), ("zs", [P, TT, GROUP])],
            [("ext", [32, 3 * P]), ("ang0", [P, 192]), ("turns", [P, 192]), ("ang", [P, 192])],
            [("lam", [P, 4, 64]), ("lam_x", [P, P]), ("sub_g", [P, P]), ("dist", [P, SEQ]), ("sub_x", [P, TT, P])])
        (m.gain, m.wide) = shared(
            "mem_rows",
            [("gain", [P, 2, D])],
            [("wide", [P, N_WIDE])])
        m.v_mla = sb(ctx, "v_mla", [P, TT, GROUP])
        m.c_t = sb(ctx, "c_t", [P, 3, SEQ])
        m.w_uq = sb(ctx, "w_uq", [P, 2, 4 * QK])
        m.w_ukv = sb(ctx, "w_ukv", [P, 512])
        m.xt = sb(ctx, "xt", [P, 4, 3 + SEQ])
        m.xc = sb(ctx, "xc", [P, 4, SEQ])
        m.conv = sb(ctx, "conv", [P, 4, SEQ])
        m.z0f = m.z0[:, :, :].rearrange("p h c -> p (h c)")
        early = m.mla_t[:, :, :].rearrange("p a b -> p (a b)")
        m.sb_t = m.mla_t[:, 0:4, :]
        m.qk_rot = early[:, 0:4 * SEQ].rearrange("p (t c) -> p t c", t=TT)
        m.cn = early[:, 4 * SEQ:4 * SEQ + TT * (QR + KVR)].rearrange("p (t c) -> p t c", t=TT)
        m.c_squares = m.qk96[:, :, :, :].rearrange("p t h c -> p (t h c)")[:, 0:TT * (QR + KVR)].rearrange("p (t c) -> p t c", t=TT)
        m.strict = m.consts[:, CONST["strict"][0]:CONST["strict"][1]].unsqueeze(1).to_broadcast([P, 4, 3 * P])
        m.z1f = m.z1[:, :, :].rearrange("p h c -> p (h c)")
        m.ps = ctx.enter_context(nc.psum_tensor("ps", [P, 8, 512], F32))
        m.ident = m.consts[:, CONST["ident"][0]:CONST["ident"][1]]
        m.upto = m.consts[:, CONST["upto"][0]:CONST["upto"][1]]
        m.after = m.consts[:, CONST["after"][0]:CONST["after"][1]]
        m.ones = m.consts[:, CONST["ones"][0]:CONST["ones"][1]]
        m.cst = lambda n: m.consts[:, CONST[n][0]:CONST[n][1]]
        m.wide_ = lambda n: m.wide[:, WIDE[n][0]:WIDE[n][1]]
        m.row_loads = len(row_pieces())
        m.b_v = m.b_uv[:, :, D:2 * D]
        def q_pair(tensor, tiles):
            def q(i, h, t):
                return tensor[64 * h:64 * h + 64, i, t * P:(t + 1) * P]

            def k(i, h, nk):
                return tensor[64 * h:64 * h + 64, tiles + i, 0:nk * P]
            return q, k
        m.score_bank = {"a": 4, "c": 4, "moba": 0, "mla": 0}
        m.turn_bank = {"a": 6, "c": 6, "moba": 2, "mla": 2}
        m.out_bank = {"a": 3, "c": 3, "moba": 4, "mla": 4}
        m.heads = {
            "a": (*q_pair(m.qk, 8), lambda i, h, t: m.v[:, t, i * P + h * HD:i * P + (h + 1) * HD]),
            "c": (*q_pair(m.qk, 8), lambda i, h, t: m.v[:, t, i * P:(i + 1) * P]),
            "moba": (*q_pair(m.moba_t, 2), lambda i, h, t: m.proj[:, t, 512 + i * P + h * HD:512 + i * P + (h + 1) * HD]),
            "mla": (lambda i, h, t: m.mla_t[0:QK, 2 * i + h, t * P:(t + 1) * P],
                    lambda i, h, nk: m.mla_t[0:QK, 4 + 2 * i + h, 0:nk * P],
                    lambda i, h, t: m.v_mla[:, t, i * P + h * HD:i * P + (h + 1) * HD]),
        }

        s = Semaphores(lambda name: ctx.enter_context(nc.semaphore(name)))
        total = sum(chunks_of(stage) for stage in PLAN)

        block = ctx.enter_context(nc.Block())

        def program(cls, eng):
            p = cls(nc, eng, m, s, d)
            p.total = total
            p.gains = []
            walk(p)

        @block.sync
        def _(eng):
            program(Sync, eng)

        @block.gpsimd
        def _(eng):
            program(Pool, eng)

        @block.scalar
        def _(eng):
            program(Scalar, eng)

        @block.vector
        def _(eng):
            program(Vector, eng)

        @block.tensor
        def _(eng):
            program(Tensor, eng)


INPUTS = ["x", "positions", "mix_norm_g", "w_in", "moba_qk_g", "mla_q_norm_g", "mla_kv_norm_g", "mla_w_uq", "mla_w_ukv",
          "mla_qk_g", "ssm_conv_w", "ssm_conv_b", "ssm_dt_bias", "ssm_a_log", "ssm_d", "ssm_norm_g", "head_out_g", "w_out",
          "ffn_norm_g", "ffn_w_in", "ffn_conv_w", "ffn_conv_b", "ffn_w_out", "norm_g_2", "ff1_w_in_2", "ff1_w_out_2",
          "ff2_w_in_2", "ff2_w_out_2", "a_w_qkv_2", "a_rel_bias_2", "a_w_o_2", "b_w_in_2", "b_ln_g_2", "b_ln_b_2", "b_w_s_2",
          "b_b_s_2", "b_w_o_2", "c_w_qkv_2", "c_lambda_2", "c_subln_g_2", "c_w_o_2"]


def kernel(**inputs):
    import concourse.bacc as bacc
    from concourse.bass_utils import run_bass_kernel_spmd

    nc = bacc.Bacc("TRN2", target_bir_lowering=False, num_devices=1)
    arrays, tensors = {}, {}
    for name in INPUTS + ["consts"]:
        a = np.ascontiguousarray(CONSTS if name == "consts" else inputs[name])
        arrays[f"in_{name}"] = a
        tensors[name] = nc.dram_tensor(f"in_{name}", a.shape, mybir.dt.from_np(a.dtype), kind="ExternalInput").ap()
    tensors["out"] = nc.dram_tensor("out_0", (1, SEQ, D), F32, kind="ExternalOutput").ap()
    tensors["ext_dram"] = nc.dram_tensor("ext_rel_bias", (32, 3 * P), F32, kind="Internal").ap()
    build(nc, Dram(tensors))
    return run_bass_kernel_spmd(nc, [arrays], core_ids=[0]).results[0]["out_0"]
```
